# Optimizing a Trainium2 kernel written in Bass

```python
import math
import jax, jax.numpy as jnp
from jax import lax
import numpy as np

D_MODEL = 2048
BATCH = 1
SEQ = 512
DEPTH = 1

HEAD_DIM = 128
MIX_W = D_MODEL
RET_HEADS = (MIX_W // 2) // HEAD_DIM
RET_W = RET_HEADS * HEAD_DIM
RET_CHUNK = 128
DSA_HEADS = (MIX_W // 2) // HEAD_DIM
DSA_KV_HEADS = 2
DSA_W = DSA_HEADS * HEAD_DIM
DSA_KV_W = DSA_KV_HEADS * HEAD_DIM
IDX_HEADS = 16
IDX_DIM = 64
TOPK_MAX = 256
Q_BLOCK = 128
D_FF = 4 * D_MODEL
N_MOD = 6
IN_SPLITS = (RET_W, RET_W, RET_W, RET_W,
             DSA_W, DSA_KV_W, DSA_KV_W,
             IDX_HEADS * IDX_DIM, IDX_DIM, IDX_HEADS)
IN_WIDTH = sum(IN_SPLITS)
EPS = 1e-6

kernel_name = "hybrid_retention_dsa_adaln_block"

def _rms_norm(x, g):
    xf = x.astype(jnp.float32)
    y = xf * lax.rsqrt(jnp.mean(xf * xf, axis=-1, keepdims=True) + EPS)
    return (y * g.astype(jnp.float32)).astype(x.dtype)

def _layer_norm_noaffine(x):
    xf = x.astype(jnp.float32)
    mu = jnp.mean(xf, axis=-1, keepdims=True)
    var = jnp.mean(jnp.square(xf - mu), axis=-1, keepdims=True)
    return ((xf - mu) * lax.rsqrt(var + EPS)).astype(x.dtype)

def _modulate(h, shift, scale):
    return h * (1.0 + scale[:, None, :]) + shift[:, None, :]

def _xpos_rotate(x, pos):
    d = x.shape[-1]
    angle = 1.0 / (10000.0 ** jnp.linspace(0.0, 1.0, d // 2, dtype=jnp.float32))
    theta = pos[:, None] * angle[None, :]
    sin = jnp.sin(theta)[None, :, None, :].astype(x.dtype)
    cos = jnp.cos(theta)[None, :, None, :].astype(x.dtype)
    x1, x2 = x[..., 0::2], x[..., 1::2]
    return jnp.stack([x1 * cos - x2 * sin, x1 * sin + x2 * cos], axis=-1).reshape(x.shape)

def _retention_chunkwise(q, k, v):
    B, L, H, D = q.shape
    C = RET_CHUNK
    N = L // C
    log_gamma = jnp.log(1.0 - jnp.exp2(-5.0 - jnp.arange(H, dtype=jnp.float32)))
    pos = jnp.arange(C, dtype=jnp.float32)
    diff = pos[:, None] - pos[None, :]
    dmask = jnp.where(diff[None] >= 0,
                      jnp.exp(log_gamma[:, None, None] * jnp.maximum(diff, 0.0)[None]), 0.0)
    xi = jnp.exp(log_gamma[:, None] * (pos[None, :] + 1.0))
    zeta = jnp.exp(log_gamma[:, None] * (C - 1.0 - pos[None, :]))
    chunk_decay = jnp.exp(log_gamma * C)

    def to_chunks(a):
        return a.reshape(B, N, C, H, D).transpose(1, 0, 3, 2, 4)

    def step(R, qkv):
        qc, kc, vc = qkv
        inner = jnp.einsum('bhcd,bhed->bhce', qc, kc) * dmask[None]
        o = (jnp.einsum('bhce,bhed->bhcd', inner, vc)
             + jnp.einsum('bhcd,bhde->bhce', qc, R) * xi[None, :, :, None])
        R = (R * chunk_decay[None, :, None, None]
             + jnp.einsum('bhcd,bhce->bhde', kc * zeta[None, :, :, None], vc))
        return R, o

    R0 = jnp.zeros((B, H, D, D), jnp.float32)
    _, o = lax.scan(step, R0, (to_chunks(q), to_chunks(k), to_chunks(v)))
    return o.transpose(1, 0, 3, 2, 4).reshape(B, L, H, D)

def _dsa_attention(q, k, v, q_idx, k_idx, w_idx):
    B, L, G, R, D = q.shape
    topk = min(TOPK_MAX, L // 4)
    n_blocks = L // Q_BLOCK
    key_pos = jnp.arange(L)

    def block(i):
        start = i * Q_BLOCK
        t = start + jnp.arange(Q_BLOCK)
        qb = lax.dynamic_slice_in_dim(q, start, Q_BLOCK, axis=1)
        qib = lax.dynamic_slice_in_dim(q_idx, start, Q_BLOCK, axis=1)
        wb = lax.dynamic_slice_in_dim(w_idx, start, Q_BLOCK, axis=1)
        s = jnp.einsum('bqhd,bsd->bqhs', qib, k_idx).astype(jnp.float32)
        score = jnp.einsum('bqhs,bqh->bqs', jax.nn.relu(s), wb.astype(jnp.float32))
        causal = key_pos[None, None, :] <= t[None, :, None]
        score = jnp.where(causal, score, -jnp.inf)
        _, idx = lax.top_k(score, topk)
        valid = idx <= t[None, :, None]
        k_sel = jax.vmap(lambda kb, ib: kb[ib])(k, idx)
        v_sel = jax.vmap(lambda vb, ib: vb[ib])(v, idx)
        logits = jnp.einsum('bqgrd,bqkgd->bqgrk', qb, k_sel).astype(jnp.float32)
        logits = jnp.where(valid[:, :, None, None, :], logits, -jnp.inf)
        p = jax.nn.softmax(logits, axis=-1).astype(v.dtype)
        o = jnp.einsum('bqgrk,bqkgd->bqgrd', p, v_sel)
        return o.reshape(B, Q_BLOCK, G * R * D)

    out = lax.map(block, jnp.arange(n_blocks))
    return out.transpose(1, 0, 2, 3).reshape(B, L, G * R * D)

def _layer(x, c, w_ada, b_ada, norm1_g, norm2_g, w_in, ret_beta, q_norm_g, k_norm_g,
           idx_k_norm_g, dsa_beta, w_out, w_mlp1, w_mlp2):
    B, L, _ = x.shape
    mod = jax.nn.silu(c) @ w_ada + b_ada
    shift1, scale1, gate1, shift2, scale2, gate2 = jnp.split(mod, N_MOD, axis=-1)

    h = _modulate(_rms_norm(x, norm1_g), shift1, scale1)
    proj = h @ w_in
    offs = list(np.cumsum(IN_SPLITS)[:-1])
    rq, rk, rv, rg, dq, dk, dv, iq, ik, iw = jnp.split(proj, offs, axis=-1)

    pos = jnp.arange(L, dtype=jnp.float32)
    rq = _xpos_rotate(rq.reshape(B, L, RET_HEADS, HEAD_DIM), pos)
    rk = _xpos_rotate(rk.reshape(B, L, RET_HEADS, HEAD_DIM), pos) * (HEAD_DIM ** -0.5)
    rv = rv.reshape(B, L, RET_HEADS, HEAD_DIM)
    ro = _retention_chunkwise(rq.astype(jnp.float32), rk.astype(jnp.float32), rv.astype(jnp.float32))
    ro = _layer_norm_noaffine(ro).astype(x.dtype).reshape(B, L, RET_W)
    y_ret = jax.nn.silu(rg) * (ro * ret_beta)

    dq = _rms_norm(dq.reshape(B, L, DSA_HEADS, HEAD_DIM), q_norm_g) * (HEAD_DIM ** -0.5)
    dq = dq.reshape(B, L, DSA_KV_HEADS, DSA_HEADS // DSA_KV_HEADS, HEAD_DIM)
    dk = _rms_norm(dk.reshape(B, L, DSA_KV_HEADS, HEAD_DIM), k_norm_g)
    dv = dv.reshape(B, L, DSA_KV_HEADS, HEAD_DIM)
    iq = iq.reshape(B, L, IDX_HEADS, IDX_DIM) * (IDX_DIM ** -0.5)
    ik = _rms_norm(ik, idx_k_norm_g)
    iw = iw * (IDX_HEADS ** -0.5)
    y_dsa = _dsa_attention(dq, dk, dv, iq, ik, iw) * dsa_beta

    mix = jnp.concatenate([y_ret, y_dsa], axis=-1) @ w_out
    x = x + gate1[:, None, :] * mix

    h = _modulate(_rms_norm(x, norm2_g), shift2, scale2)
    y = jnp.square(jax.nn.relu(h @ w_mlp1)) @ w_mlp2
    return x + gate2[:, None, :] * y

def setup_inputs(seed: int = 0) -> dict:
    key = jax.random.key(seed)
    ks = jax.random.split(key, 16)
    nrm = jax.random.normal
    f32 = jnp.float32
    return {
        "x": nrm(ks[0], (BATCH, SEQ, D_MODEL), f32),
        "c": nrm(ks[1], (BATCH, D_MODEL), f32),
        "w_ada": nrm(ks[2], (DEPTH, D_MODEL, N_MOD * D_MODEL), f32) * (0.5 * D_MODEL ** -0.5),
        "b_ada": nrm(ks[3], (DEPTH, N_MOD * D_MODEL), f32) * 0.01,
        "norm1_g": 1.0 + 0.02 * nrm(ks[4], (DEPTH, D_MODEL), f32),
        "norm2_g": 1.0 + 0.02 * nrm(ks[5], (DEPTH, D_MODEL), f32),
        "w_in": nrm(ks[6], (DEPTH, D_MODEL, IN_WIDTH), f32) * (D_MODEL ** -0.5),
        "ret_beta": 1.0 + 0.02 * nrm(ks[7], (DEPTH, RET_W), f32),
        "q_norm_g": 1.0 + 0.02 * nrm(ks[8], (DEPTH, HEAD_DIM), f32),
        "k_norm_g": 1.0 + 0.02 * nrm(ks[9], (DEPTH, HEAD_DIM), f32),
        "idx_k_norm_g": 1.0 + 0.02 * nrm(ks[10], (DEPTH, IDX_DIM), f32),
        "dsa_beta": 1.0 + 0.02 * nrm(ks[11], (DEPTH, DSA_W), f32),
        "w_out": nrm(ks[12], (DEPTH, MIX_W, D_MODEL), f32) * (MIX_W ** -0.5),
        "w_mlp1": nrm(ks[13], (DEPTH, D_MODEL, D_FF), f32) * (D_MODEL ** -0.5),
        "w_mlp2": nrm(ks[14], (DEPTH, D_FF, D_MODEL), f32) * (D_FF ** -0.5),
    }

def reference(x, c, w_ada, b_ada, norm1_g, norm2_g, w_in, ret_beta, q_norm_g, k_norm_g,
              idx_k_norm_g, dsa_beta, w_out, w_mlp1, w_mlp2):
    for l in range(DEPTH):
        x = _layer(x, c, w_ada[l], b_ada[l], norm1_g[l], norm2_g[l], w_in[l], ret_beta[l],
                   q_norm_g[l], k_norm_g[l], idx_k_norm_g[l], dsa_beta[l], w_out[l],
                   w_mlp1[l], w_mlp2[l])
    return x


_drawn_inputs = setup_inputs


def setup_inputs(seed=0):
    import zlib

    import numpy as np

    out = dict(_drawn_inputs(seed))
    spreads = {}
    factors = {'b_ada': 3.281,
     'norm1_g': 8.0,
     'norm2_g': 21.226,
     'ret_beta': 36.558,
     'q_norm_g': 8.0,
     'k_norm_g': 8.0,
     'idx_k_norm_g': 8.0,
     'dsa_beta': 25.912}
    for name, (base, spread) in spreads.items():
        noise = np.random.default_rng([zlib.crc32(name.encode()), seed]).standard_normal(out[name].shape)
        drawn = base * np.exp(spread * noise) if base else spread * noise
        out[name] = __import__('jax').numpy.asarray(drawn.astype(out[name].dtype))
    for name, factor in factors.items():
        out[name] = (out[name] * factor).astype(out[name].dtype)
    return out
```

```python
import math

import numpy as np

import concourse.bass as bass
from concourse import mybir

F32 = mybir.dt.float32
F32R = mybir.dt.float32r
ALU = mybir.AluOpType
ACT = mybir.ActivationFunctionType
AX = mybir.AxisListType

P = 128
L = 512
D = 2048
NB = L // P
KT = D // P
FF = 4 * D
HEADS = 8
KV = 2
PER_KV = HEADS // KV
HW = HEADS * P
IDX_HEADS, IDX_DIM = 16, 64
TOPK = L // 4
EPS = 1e-6
DROP = -3.0e38
TAKEN = -3.4e38
COL_RQ, COL_RK, COL_RV, COL_RG = 0, HW, 2 * HW, 3 * HW
COL_DQ = 4 * HW
COL_DK = COL_DQ + HW
COL_IQ = COL_DK + 2 * KV * P
COL_IK = COL_IQ + IDX_HEADS * IDX_DIM
SMALL = IDX_DIM + IDX_HEADS
HI, LO = 0, 1
PASSES = ((HI, HI), (HI, LO), (LO, HI))
V_C, V_N1, V_N2, V_RB, V_DB, V_QG, V_KG, V_IG, V_ROWS = 0, 16, 32, 48, 56, 64, 65, 66, 67
C_ID, C_CAUSAL, C_NEG, C_ONES, C_COS, C_SIN, C_QDEC, C_KDEC, C_END = (
    0, 128, 256, 384, 512, 768, 1024, 1056, 1088)

U_SMALL, U_DKV, U_IQ, U_LOOP, PER_G = 0, 1, 3, 7, 10
U_WO = U_LOOP + KV * PER_G
U_MLP = U_WO + 8
PER_C = 8
STEPS = FF // 1024
GR_DQ, GR_RG, GR_RQ, GR_RK, GR_RV = range(5)


def need(eng, sem, value):
    if isinstance(value, int) and value <= 0:
        return
    eng.wait_ge(sem, value)


class Steps:

    def __init__(self, eng, sem):
        self.eng, self.sem, self.n = eng, sem, 0

    def step(self, ins):
        ins.then_inc(self.sem, 1)
        self.n += 1

    def link(self, ins):
        self.step(ins)
        self.eng.wait_ge(self.sem, self.n)

    def wait(self):
        self.eng.wait_ge(self.sem, self.n)


def build(nc, x, vecs, b_ada, consts, w_ada, w_in, w_out, w_mlp1, w_mlp2, out):
    base = 16512

    def at(name, offset, shape, dt=F32):
        return nc.alloc_sbuf_tensor_at(name, shape, dt, offset=base + offset)

    h = at("h", 0, [P, KT, 2, L], F32R)
    raw = at("raw", 65536, [P, 2, 4096])
    w_hi = at("w_hi", 98304, [P, 4, 1024], F32R)
    w_lo = at("w_lo", 114688, [P, 4, 1024], F32R)
    XR = 131072
    resid = at("resid", XR, [P, KT, L])
    iqT = at("iqT", XR, [P, 8, L])
    y_raw = at("y_raw", XR, [P, HEADS, L])
    kT = at("kT", XR + 16384, [P, KV, L])
    v_nat = at("v_nat", XR + 20480, [P, NB, KV * P])
    qT = at("qT", XR + 24576, [P, PER_KV, L])
    RB = XR + 32768
    con = at("con", RB, [P, C_END])
    cursor = [RB + 4 * C_END]

    def small(name, *shape):
        t = at(name, cursor[0], [P, *shape])
        cursor[0] += -(-4 * math.prod(shape) // 32) * 32
        return t

    bias_cols = small("bias_cols", 6 * KT)
    vec = small("vec", V_ROWS + 1)
    mod = small("mod", 6 * KT)
    gain = small("gain", 2, KT)
    csilu = small("csilu", 2, KT)
    half = small("half", 8)
    mx = small("mx", 8)
    sums = small("sums", 8)
    ms = small("ms", 16)
    m8 = small("m8", 8)
    bn6 = small("bn6", NB, 6)
    bn2 = small("bn2", NB, 2)
    w_idx = small("w_idx", NB, IDX_HEADS)
    RC = RB + 4352 + 2048
    acc = at("acc", RC, [P, 2, L])
    ada = at("ada", RC + 4096, [P, 2, 1024])
    score = at("score", RC + 12288, [P, 1280])
    pT = at("pT", RC + 12288, [P, 1280])
    masks = at("masks", RC + 17408, [P, 1280])
    nat = at("nat", RC + 22528, [P, NB, L])
    prob = at("prob", RC + 22528, [P, 1280])
    k_nat = at("k_nat", RC + 22528, [P, NB, KV * P])
    ik_nat = at("ik_nat", RC + 26624, [P, NB, IDX_DIM])
    ik2 = at("ik2", RC + 27648, [P, NB, 2, IDX_DIM])
    ikT = at("ikT", RC + 30720, [P, L])
    v_cur = at("v_cur", RC + 32768, [P, NB, P])
    rstd1 = at("rstd1", RC + 32768, [P, L])
    rot = at("rot", RC + 34816, [P, 2, 256])
    junk = at("junk", RC + 34816, [P, L])
    stage = at("stage", RC + 36864, [P, 2, L])
    tmp1 = at("tmp1", RC + 36864, [P, 2, L])
    x_nat = at("x_nat", 65536 + 16384, [P, 2, D])
    first = [at("ada_first0", 12 * 4096, [P, 2048]), at("ada_first1", 14 * 4096, [P, 2048]),
             at("ada_first2", RC + 4096, [P, 2048]), at("ada_first3", RC + 22528, [P, 2048])]
    ret = at("ret", RC, [P, 3, 4, NB, P])
    qkT = at("qkT", RC + 24576, [P, 2, L])
    innerT = at("innerT", RC + 28672, [P, L])
    state = at("state", RC + 30720, [P, 3, P])
    z = at("z", RC + 32768, [P, NB, P])
    ysum = at("ysum", RC + 34816, [P, L])
    ss = at("ss", RC, [P, L])
    rstd2 = at("rstd2", RC + 2048, [P, L])
    mid = at("mid", RC, [P, 8, 2, L], F32R)
    relu = at("relu", RC + 32768, [P, 2, L])
    out_nat = at("out_nat", RC + 32768, [P, 2, L])
    sq = at("sq", RC + 36864, [P, 2, L])

    pj = nc.alloc_psum_tensor("pj", [P, 4, L], F32)
    pa = nc.alloc_psum_tensor("pa", [P, 4, L], F32)

    xT_dram = nc.dram_tensor("xT_dram", (P, KT, L), F32).ap()
    ret_dram = nc.dram_tensor("ret_dram", (4, L, HW), F32).ap()

    ident, causal = con[:, C_ID:C_ID + P], con[:, C_CAUSAL:C_CAUSAL + P]
    neg, ones = con[:, C_NEG:C_NEG + P], con[:, C_ONES:C_ONES + P]

    sem = nc.alloc_semaphore
    const_landed, rows_landed = sem("const_landed"), sem("rows_landed")
    x_landed = [sem("x_landed0"), sem("x_landed1")]
    first_landed = [sem(f"first_landed{i}") for i in range(4)]
    ada_landed = [sem("ada_landed0"), sem("ada_landed1")]
    raw_landed = [sem("raw_landed0"), sem("raw_landed1")]
    xT_stored, resid_landed = sem("xT_stored"), sem("resid_landed")
    ret_stored = [sem("ret_stored0"), sem("ret_stored1")]
    ret_landed = [sem(f"ret_landed{i}") for i in range(3)]
    out_stored = [sem("out_stored0"), sem("out_stored1")]
    hi_done, lo_done, chunk_used = sem("hi_done"), sem("lo_done"), sem("chunk_used")
    proj_done, proj_free = sem("proj_done"), sem("proj_free")
    rows_turned, rows_taken = sem("rows_turned"), sem("rows_taken")
    half_set, silu_exp, silu_ready = sem("half_set"), sem("silu_exp"), sem("silu_ready")
    x_turned, x_taken = sem("x_turned"), sem("x_taken")
    x_squared, x_summed = sem("x_squared"), sem("x_summed")
    ms_ready, rstd_ready = sem("ms_ready"), sem("rstd_ready")
    first_used, ada_used, acc_ready = sem("first_used"), sem("ada_used"), sem("acc_ready")
    mod_summed, mod_taken = sem("mod_summed"), sem("mod_taken")
    t_ready, h_hi, h_ready = sem("t_ready"), sem("h_hi"), sem("h_ready")
    ik_ready, ik_turned, ikT_ready = sem("ik_ready"), sem("ik_turned"), sem("ikT_ready")
    k_ready, k_turned, kT_ready = sem("k_ready"), sem("k_turned"), sem("kT_ready")
    iq_ready, idx_done, idx_taken = sem("iq_ready"), sem("idx_done"), sem("idx_taken")
    q_ready, q_turned, qT_ready = sem("q_ready"), sem("q_turned"), sem("qT_ready")
    rg_exp, stage_ready = sem("rg_exp"), sem("stage_ready")
    logits_done, logits_ready = sem("logits_done"), sem("logits_ready")
    exp_done, p_ready, p_turned, pT_ready = sem("exp_done"), sem("p_ready"), sem("p_turned"), sem("pT_ready")
    pv_done, y_ready = sem("pv_done"), sem("y_ready")
    yd_hi, yd_ready = sem("yd_hi"), sem("yd_ready")
    qk_turned, qkT_ready = sem("qk_turned"), sem("qkT_ready")
    state_done, state_ready = sem("state_done"), sem("state_ready")
    inner_done, inner_ready = sem("inner_done"), sem("inner_ready")
    o_done, z_ready, z_turned = sem("o_done"), sem("z_ready"), sem("z_turned")
    yr_hi, yr_ready = sem("yr_hi"), sem("yr_ready")
    added = sem("added")
    ss_ready, ss_summed = sem("ss_ready"), sem("ss_summed")
    t2_ready, h2_hi, h2_ready = sem("t2_ready"), sem("h2_hi"), sem("h2_ready")
    relu_done, sq_ready, mid_hi, mid_ready = sem("relu_done"), sem("sq_ready"), sem("mid_hi"), sem("mid_ready")
    out_turned, out_ready = sem("out_turned"), sem("out_ready")
    act_step, dve_step = sem("act_step"), sem("dve_step")

    w_in_v = w_in.rearrange("(k p) n -> p k n", p=P)
    w_out_v = w_out.rearrange("(k p) n -> p k n", p=P)
    w1_v = w_mlp1.rearrange("(k p) n -> p k n", p=P)
    w2_v = w_mlp2.rearrange("(k p) n -> p k n", p=P)
    ada_v = w_ada.rearrange("(k p) n -> p k n", p=P)

    def unit_source(u):
        if u == U_SMALL:
            return w_in_v[:, :, COL_IK:COL_IK + SMALL]
        if u < U_IQ:
            k, col = 8 * (u - U_DKV), COL_DK
        elif u < U_LOOP:
            k, col = 8 * ((u - U_IQ) % 2), COL_IQ + 512 * ((u - U_IQ) // 2)
        elif u < U_WO:
            g, m = divmod(u - U_LOOP, PER_G)
            first_col = {GR_DQ: COL_DQ, GR_RG: COL_RG, GR_RQ: COL_RQ, GR_RK: COL_RK, GR_RV: COL_RV}[m // 2]
            k, col = 8 * (m % 2), first_col + 512 * g
        else:
            half_, v = divmod(u - U_WO, 4)
            return w_out_v[:, 8 * (1 - half_):8 * (2 - half_), 512 * v:512 * v + 512]
        return w_in_v[:, k:k + 8, col:col + 512]

    def is_tiles(u):
        return U_IQ <= u < U_LOOP or u >= U_WO

    def raw_chunk(u, j):
        slot = raw[:, u % 2, :]
        if u == U_SMALL:
            return slot[:, 320 * j:320 * j + 320]
        if is_tiles(u):
            return slot.rearrange("p (k n) -> p k n", k=8)[:, :, P * j:P * j + P]
        return slot[:, 1024 * j:1024 * j + 1024]

    def split_chunk(w, u, j):
        if u == U_SMALL:
            return w[:, j, 0:320]
        if is_tiles(u):
            return w[:, j, :].rearrange("p (k n) -> p k n", k=8)
        return w[:, j, :]

    def span(i):
        return P * (i + 1)

    MASK_AT = [0, 128, 384, 768]
    SCORE_AT = [0, 0, 256, 640]
    LOGIT_AT = [(0, 0), (1, 0), (0, 128), (2, 0)]
    TURN_AT = [(0, 0), (1, 0), (2, 0), (1, 384)]
    PT_AT = [0, 512, 896, 1152]
    TURN_ORDER = (0, 1, 3, 2)

    ITEMS = [(i, hh) for part in range(2) for i in (1, 2, 3) for hh in range(8 * part, 8 * part + 8)]

    block = nc.Block()
    with block:

        @block.sync
        def _(sp):
            def ada_piece(t):
                n, k = divmod(t, 8)
                col = 2 * D + 512 * n
                need(sp, ada_used, t - 1)
                sp.dma_start(ada[:, t % 2, :].rearrange("p (k n) -> p k n", k=2),
                             ada_v[:, 2 * k:2 * k + 2, col:col + 512]).then_inc(ada_landed[t % 2], 16)

            def store(g, gr):
                kind = {GR_RG: 0, GR_RQ: 1, GR_RK: 2, GR_RV: 3}[gr]
                for tb in range(NB):
                    use = 16 * g + 4 * (gr - 1) + tb
                    sp.wait_ge(stage_ready, use + 1)
                    sp.dma_start(ret_dram[kind, P * tb:P * tb + P, 512 * g:512 * g + 512],
                                 stage[:, use % 2, :]).then_inc(ret_stored[use % 2], 16)

            def load_head(k):
                if k < 3:
                    sp.wait_ge(y_ready, HEADS)
                    sp.wait_ge(ada_used, 128)
                else:
                    sp.wait_ge(z_ready, k - 2)
                stores = 32 if k < 4 else 32 * KV
                if k in (0, 4):
                    for s in range(2):
                        sp.wait_ge(ret_stored[s], 16 * stores // 4)
                for kind in range(4):
                    sp.dma_start(ret[:, k % 3, kind], ret_dram[kind, :, P * k:P * k + P]
                                 .rearrange("(b p) d -> p b d", p=P)).then_inc(ret_landed[k % 3], 16)

            def actions(q):
                if q == U_LOOP - 1:
                    sp.wait_ge(first_used, 32)
                    ada_piece(0)
                    ada_piece(1)
                if U_LOOP <= q < U_WO:
                    g, m = divmod(q - U_LOOP, PER_G)
                    for gr, where in ((GR_RG, 3), (GR_RQ, 5), (GR_RK, 7), (GR_RV, 9)):
                        if m == where:
                            store(g, gr)
                if U_LOOP <= q < U_LOOP + 16:
                    for t in range(8 * (q - U_LOOP) + 2, min(8 * (q - U_LOOP) + 10, 128)):
                        ada_piece(t)
                if q == U_WO - 1:
                    for k in range(3):
                        load_head(k)
                    sp.wait_ge(yd_ready, HEADS)
                    sp.wait_ge(xT_stored, 16)
                    sp.dma_start(resid[:], xT_dram).then_inc(resid_landed, 16)
                if q == U_WO:
                    load_head(3)
                    load_head(4)
                if q == U_WO + 1:
                    load_head(5)
                    load_head(6)
                if q == U_WO + 2:
                    load_head(7)

            def load_unit(u):
                need(sp, lo_done, 4 * (u - 1))
                dst = raw[:, u % 2, 0:KT * SMALL].rearrange("p (k n) -> p k n", k=KT) if u == U_SMALL \
                    else raw[:, u % 2, :].rearrange("p (k n) -> p k n", k=8)
                sp.dma_start(dst, unit_source(u)).then_inc(raw_landed[u % 2], 16)

            def first_piece(n, s):
                cc, sec = n // 2, n % 2
                need(sp, first_used, 4 * n + s - 3)
                col = D * sec + 512 * cc
                sp.dma_start(first[s][:].rearrange("p (k n) -> p k n", k=4),
                             ada_v[:, 4 * s:4 * s + 4, col:col + 512]).then_inc(first_landed[s], 16)

            sp.dma_start(con[:], consts).then_inc(const_landed, 16)
            for s in range(2):
                sp.dma_start(x_nat[:, s, :], x[P * s:P * s + P, :]).then_inc(x_landed[s], 16)
            for s in range(4):
                first_piece(0, s)
            load_unit(U_SMALL)
            for s in range(2):
                sp.wait_ge(x_turned, 4 * s + 4)
                sp.dma_start(x_nat[:, s, :], x[P * (s + 2):P * (s + 3), :]).then_inc(x_landed[s], 16)
            for n in range(1, 8):
                for s in range(4):
                    first_piece(n, s)
                if n == 4:
                    sp.wait_ge(x_turned, 16)
                    load_unit(1)
            for u in range(2, U_MLP):
                load_unit(u)
                actions(u - 3)
            with sp.Fori(0, STEPS) as c:
                for m in range(PER_C):
                    u = U_MLP + m
                    sp.wait_ge(lo_done, 4 * (u - 1) + 4 * PER_C * c)
                    if m < 4:
                        a, hf = divmod(m, 2)
                        src = w1_v[:, 8 * hf:8 * hf + 8, bass.ds(1024 * c + 512 * a, 512)]
                    else:
                        src = w2_v[:, bass.ds(8 * c, 8), 512 * (m - 4):512 * (m - 3)]
                    sp.dma_start(raw[:, u % 2, :].rearrange("p (k n) -> p k n", k=8),
                                 src).then_inc(raw_landed[u % 2], 16)
            for t in range(KT):
                sp.wait_ge(out_ready, t + 1)
                sp.dma_start(out[:, P * t:P * t + P].rearrange("(b p) d -> p b d", p=P),
                             out_nat[:, t % 2, :].rearrange("p (b d) -> p b d", b=NB)).then_inc(out_stored[t % 2], 16)
            for s in range(2):
                sp.wait_ge(out_stored[s], 16 * KT // 2)

        @block.scalar
        def _(act):
            def split_hi(u, j, trip=0):
                need(act, chunk_used, 4 * (u - 1) + j + 1 + 4 * PER_C * trip)
                if j == 0:
                    act.wait_ge(raw_landed[u % 2], 16 * (u // 2 + 1) + 16 * (PER_C // 2) * trip)
                act.activation(split_chunk(w_hi, u, j), raw_chunk(u, j), ACT.Copy).then_inc(hi_done, 1)

            def h_high(kt):
                act.wait_ge(t_ready, kt + 1)
                act.activation(h[:, kt, HI, :], tmp1[:, kt % 2, :], ACT.Identity,
                               bias=mod[:, kt:kt + 1]).then_inc(h_hi, 1)

            def softmax_exp(hd):
                act.wait_ge(logits_ready, hd + 1)
                for i in range(NB):
                    at_ = MASK_AT[i]
                    act.activation(prob[:, at_:at_ + span(i)], prob[:, at_:at_ + span(i)], ACT.Exp,
                                   bias=mx[:, 4 + i:5 + i], accum_out=sums[:, i:i + 1]).then_inc(exp_done, 1)

            def at_position(q):
                if U_LOOP <= q < U_WO:
                    g, m = divmod(q - U_LOOP, PER_G)
                    if m == 3:
                        for tb in range(NB):
                            use = 16 * g + tb
                            act.wait_ge(proj_free, 12 + 16 * g + tb + 1)
                            need(act, ret_stored[use % 2], 16 * (use // 2))
                            act.activation(stage[:, use % 2, :], nat[:, tb, :], ACT.Exp,
                                           scale=-1.0).then_inc(rg_exp, 1)
                    if 4 <= m < 8:
                        softmax_exp(4 * g + m - 4)
                if q == U_WO - 1:
                    act.wait_ge(chunk_used, 4 * U_WO)
                    act.wait_ge(y_ready, HEADS)
                    for t in range(HEADS):
                        act.activation(h[:, 8 + t, HI, :], y_raw[:, t, :], ACT.Copy).then_inc(yd_hi, 1)

            def retention_hi(k):
                act.wait_ge(z_turned, k + 1)
                act.activation(h[:, k, HI, :], pa[:, 0, :], ACT.Copy,
                               scale=vec[:, V_RB + k:V_RB + k + 1]).then_inc(yr_hi, 1)

            act.dma_start(raw[0:96, 0, 2048:2176], b_ada).then_inc(rows_landed, 16)
            act.dma_start(raw[0:V_ROWS, 0, 2176:2304], vecs).then_inc(rows_landed, 16)
            act.wait_ge(rows_taken, 2)
            act.activation(csilu[:, 1, :], vec[:, V_C:V_C + KT], ACT.Exp, scale=-1.0).then_inc(silu_exp, 1)
            for f in range(16):
                tb, q = divmod(f, 4)
                act.wait_ge(x_turned, f + 1)
                act.activation(resid[:, 4 * q:4 * q + 4, P * tb:P * tb + P],
                               pj[:, q, :].rearrange("p (k t) -> p k t", k=4), ACT.Copy).then_inc(x_taken, 1)
            act.wait_ge(x_taken, 16)
            act.dma_start(xT_dram, resid[:]).then_inc(xT_stored, 16)
            for kt in range(KT):
                need(act, x_summed, kt - 1)
                act.activation(tmp1[:, kt % 2, :], resid[:, kt, :], ACT.Square).then_inc(x_squared, 1)
            for cc in range(4):
                for m in range(4):
                    h_high(4 * cc + m)
                split_hi(U_SMALL, cc)
            for u in range(1, U_WO + 1):
                for j in range(4):
                    split_hi(u, j)
                at_position(u - 1)
            for r in range(4, 32):
                split_hi(U_WO + r // 4, r % 4)
                if 7 <= r <= 19 and r % 2:
                    retention_hi((r - 7) // 2)
                if r == 19:
                    retention_hi(7)
            for j in range(4):
                split_hi(U_MLP, j)
            for kt in range(KT):
                act.wait_ge(t2_ready, kt + 1)
                act.activation(h[:, kt, HI, :], relu[:, kt % 2, :], ACT.Identity,
                               bias=mod[:, 48 + kt:49 + kt]).then_inc(h2_hi, 1)

            def relu_tile(n, c):
                a, j = divmod(n, 4)
                act.wait_ge(chunk_used, 4 * (U_MLP + 2 * a + 1) + j + 1 + 32 * c)
                if isinstance(c, int) and n < 2:
                    act.wait_ge(h2_ready, KT)
                else:
                    act.wait_ge(sq_ready, 8 * c + n - 1)
                act.activation(relu[:, n % 2, :], (pa if a else pj)[:, j, :], ACT.Relu).then_inc(relu_done, 1)

            def mid_high(n, c):
                act.wait_ge(sq_ready, 8 * c + n + 1)
                act.activation(mid[:, n, HI, :], sq[:, n % 2, :], ACT.Copy).then_inc(mid_hi, 1)

            def mlp_step(c, from_chunk):
                for qn in range(from_chunk, 32):
                    split_hi(U_MLP + qn // 4, qn % 4, c)
                    if 8 <= qn < 12:
                        n = qn - 8
                    elif 16 <= qn < 20:
                        n = qn - 12
                    else:
                        continue
                    relu_tile(n, c)
                    if n > 0:
                        mid_high(n - 1, c)
                    if n == 7:
                        mid_high(n, c)

            mlp_step(0, 4)
            with act.Fori(1, STEPS) as c:
                mlp_step(c, 0)
            for t in range(KT):
                act.wait_ge(out_turned, t + 1)
                need(act, out_stored[t % 2], 16 * (t // 2))
                act.activation(out_nat[:, t % 2, :], (pa if t // 4 % 2 else pj)[:, t % 4, :],
                               ACT.Copy).then_inc(out_ready, 1)

        @block.gpsimd
        def _(pool):
            def split_lo(u, j, trip=0):
                pool.wait_ge(hi_done, 4 * u + j + 1 + 4 * PER_C * trip)
                pool.tensor_tensor(split_chunk(w_lo, u, j), raw_chunk(u, j), split_chunk(w_hi, u, j).bitcast(F32),
                                   ALU.subtract).then_inc(lo_done, 1)

            powers = [0]

            def root(dst, src, width):
                powers[0] += 1
                pool.wait_ge(ms_ready, powers[0])
                pool.tensor_tensor(dst, src, half[:, 0:1].to_broadcast([P, width]), ALU.pow).then_inc(rstd_ready, 1)

            pool.wait_ge(half_set, 1)
            root(rstd1[:], rstd1[:], L)
            for u in range(U_WO):
                for j in range(4):
                    split_lo(u, j)
                if u == 1:
                    root(ms[:, 0:NB], ms[:, 0:NB], NB)
                if u == 3:
                    root(ms[:, 0:8], ms[:, 0:8], 8)
                if u >= U_LOOP and (u - U_LOOP) % PER_G == 2:
                    root(ms[:], ms[:], 16)
            for r in range(32):
                split_lo(U_WO + r // 4, r % 4)
                if 6 <= r <= 18 and r % 2 == 0:
                    root(ms[:, 0:NB], ms[:, 0:NB], NB)
                if r == 19:
                    root(ms[:, 0:NB], ms[:, 0:NB], NB)
            for j in range(4):
                split_lo(U_MLP, j)
            root(rstd2[:], rstd2[:], L)
            for j in range(4, 32):
                split_lo(U_MLP + j // 4, j % 4)
            with pool.Fori(1, STEPS) as c:
                for j in range(32):
                    split_lo(U_MLP + j // 4, j % 4, c)

        @block.vector
        def _(dve):
            own = Steps(dve, dve_step)
            dve.memset(half[:], -0.5).then_inc(half_set, 1)
            dve.wait_ge(rows_turned, 1)
            dve.tensor_copy(bias_cols[:], pa[:, 0, 0:96]).then_inc(rows_taken, 1)
            dve.wait_ge(rows_turned, 2)
            dve.tensor_copy(vec[:, 0:V_ROWS], pa[:, 1, 0:V_ROWS]).then_inc(rows_taken, 1)
            dve.wait_ge(silu_exp, 1)
            own.link(dve.tensor_scalar(csilu[:, 1, :], csilu[:, 1, :], 1.0, None, ALU.add))
            own.link(dve.reciprocal(csilu[:, 1, :], csilu[:, 1, :]))
            own.link(dve.tensor_tensor(csilu[:, 0, :], csilu[:, 1, :], vec[:, V_C:V_C + KT], ALU.mult))

            def multiply(dst, src, kts, is_first):
                for n, kt in enumerate(kts):
                    c_col = csilu[:, 0, kt:kt + 1]
                    if is_first and n == 0:
                        last = dve.tensor_scalar(dst, src(n), c_col, None, ALU.mult)
                    else:
                        own.wait()
                        last = dve.scalar_tensor_tensor(dst, src(n), c_col, dst, ALU.mult, ALU.add)
                    if n < len(kts) - 1:
                        own.step(last)
                return last

            def take_mod(n, bank, col):
                dve.wait_ge(mod_summed, n + 1)
                dve.tensor_tensor(mod[:, col:col + 4], pa[:, 3, bank:bank + 4], bias_cols[:, col:col + 4],
                                  ALU.add).then_inc(mod_taken, 1)

            def first_acc(n):
                for s in range(4):
                    dve.wait_ge(first_landed[s], 16 * (n + 1))
                    last = multiply(acc[:, n % 2, :], lambda i, s=s: first[s][:, 512 * i:512 * i + 512],
                                    range(4 * s, 4 * s + 4), s == 0)
                    last.then_inc(first_used, 1)
                    if s < 3:
                        dve.wait_ge(first_used, 4 * n + s + 1)

            def fold(kt0, which, scale_col, norm_row, count):
                own.link(dve.scalar_tensor_tensor(gain[:, which, kt0:kt0 + count],
                                                  mod[:, scale_col + kt0:scale_col + kt0 + count], 1.0,
                                                  vec[:, norm_row + kt0:norm_row + kt0 + count], ALU.add, ALU.mult))

            def modulate(kt, which, src, rstd, tmp, shift_col, ready, hi_sem, done, go):
                if go == 0:
                    need(dve, done, kt - 1)
                    dve.scalar_tensor_tensor(tmp[:, kt % 2, :], src[:, kt, :], gain[:, which, kt:kt + 1], rstd,
                                             ALU.mult, ALU.mult).then_inc(ready, 1)
                else:
                    dve.wait_ge(hi_sem, kt + 1)
                    dve.scalar_tensor_tensor(h[:, kt, LO, :], tmp[:, kt % 2, :], mod[:, shift_col + kt:shift_col + kt + 1],
                                             h[:, kt, HI, :].bitcast(F32), ALU.add, ALU.subtract).then_inc(done, 1)

            for cc in range(4):
                for sec in range(2):
                    first_acc(2 * cc + sec)
                if cc == 0:
                    dve.wait_ge(x_summed, KT)
                    dve.tensor_scalar(rstd1[:], pa[:, 2, :], 1.0 / D, EPS, ALU.mult, ALU.add).then_inc(ms_ready, 1)
                dve.wait_ge(mod_summed, 2 * cc + 2)
                for sec in range(2):
                    take_mod(2 * cc + sec, 4 * sec, KT * sec + 4 * cc)
                dve.wait_ge(mod_taken, 2 * cc + 2)
                fold(4 * cc, 0, KT, V_N1, 4)
                dve.wait_ge(rstd_ready, 1)
                for m in range(5):
                    kt = 4 * cc + m
                    if m < 4:
                        modulate(kt, 0, resid, rstd1[:], tmp1, 0, t_ready, h_hi, h_ready, 0)
                    if m > 0:
                        modulate(kt - 1, 0, resid, rstd1[:], tmp1, 0, t_ready, h_hi, h_ready, 1)

            def bank_ready(u_last, ni, b):
                if ni is not None and b < 3:
                    dve.wait_ge(proj_done, 3 * ni + b + 1)
                else:
                    dve.wait_ge(chunk_used, 4 * u_last + (b if ni is None else 3) + 1)

            def mean_square(src, n, width):
                places = L // width
                for i in range(n):
                    if i % places == 0:
                        own.wait()
                    at_ = width * (i % places)
                    own.step(dve.tensor_tensor_reduce(junk[:, at_:at_ + width], src(i), src(i), 1.0, 0.0, ALU.mult, ALU.add,
                                                      ms[:, i:i + 1]))
                own.wait()
                dve.tensor_scalar(ms[:, 0:n], ms[:, 0:n], 1.0 / width, EPS, ALU.mult, ALU.add).then_inc(ms_ready, 1)

            for tb in range(NB):
                dve.wait_ge(chunk_used, 4)
                own.step(dve.tensor_copy(ik_nat[:, tb, :], pj[:, tb, 0:IDX_DIM]))
                dve.tensor_scalar(w_idx[:, tb, :], pj[:, tb, IDX_DIM:SMALL], (IDX_HEADS * IDX_DIM) ** -0.5, None,
                                  ALU.mult).then_inc(proj_free, 1)
            own.wait()
            mean_square(lambda tb: ik_nat[:, tb, :], NB, IDX_DIM)
            dve.wait_ge(rstd_ready, 2)
            for tb in range(NB):
                for twice in range(2):
                    dve.tensor_scalar(ik2[:, tb, twice, :], ik_nat[:, tb, :], ms[:, tb:tb + 1], None,
                                      ALU.mult).then_inc(ik_ready, 1)
            dve.wait_ge(xT_stored, 16)
            for tb in range(NB):
                bank_ready(2, 0, tb)
                own.step(dve.tensor_copy(k_nat[:, tb, :], pj[:, tb, 0:KV * P]))
                dve.tensor_copy(v_nat[:, tb, :], pj[:, tb, KV * P:]).then_inc(proj_free, 1)
            own.wait()
            dve.wait_ge(ik_ready, 8)
            mean_square(lambda i: k_nat[:, i // 2, P * (i % 2):P * (i % 2) + P], 8, P)
            dve.wait_ge(ik_turned, 1)
            dve.tensor_scalar(ikT[:], pa[:, 0, :], vec[:, V_IG:V_IG + 1], None, ALU.mult).then_inc(ikT_ready, 1)
            dve.wait_ge(rstd_ready, 3)
            for i in range(8):
                k_i = k_nat[:, i // 2, P * (i % 2):P * (i % 2) + P]
                dve.tensor_scalar(k_i, k_i, ms[:, i:i + 1], None, ALU.mult).then_inc(k_ready, 1)
            for g in range(KV):
                dve.wait_ge(k_turned, g + 1)
                dve.tensor_scalar(kT[:, g, :], pa[:, 1 + g, :], vec[:, V_KG:V_KG + 1], None, ALU.mult).then_inc(kT_ready, 1)

            def take_iq(part):
                for b in range(4):
                    bank_ready(U_IQ + 2 * part + 1, None, b)
                    dve.tensor_copy(iqT[:, 4 * part + b, :], pj[:, b, :]).then_inc(iq_ready, 1)

            def index_item(n):
                i, hh = ITEMS[n]
                dst = score[:, SCORE_AT[i]:SCORE_AT[i] + span(i)]
                dve.wait_ge(idx_done, n + 1)
                w_col = w_idx[:, i, hh:hh + 1]
                if hh == 0:
                    dve.tensor_scalar(dst, pa[:, n % 4, 0:span(i)], 0.0, w_col, ALU.max, ALU.mult).then_inc(idx_taken, 1)
                    dve.wait_ge(idx_taken, n + 1)
                else:
                    dve.tensor_scalar(junk[:, 0:span(i)], pa[:, n % 4, 0:span(i)], 0.0, w_col, ALU.max,
                                      ALU.mult).then_inc(idx_taken, 1)
                    dve.wait_ge(idx_taken, n + 1)
                    own.link(dve.tensor_tensor(dst, dst, junk[:, 0:span(i)], ALU.add))

            take_iq(0)
            for n in range(24):
                index_item(n)
            take_iq(1)
            for n in range(24, 48):
                index_item(n)

            dve.tensor_copy(masks[:, 0:P], neg)
            for i in (1, 2, 3):
                s_i = score[:, SCORE_AT[i]:SCORE_AT[i] + span(i)]
                own.link(dve.tensor_tensor(s_i[:, span(i) - P:], s_i[:, span(i) - P:], neg, ALU.add))
                for _ in range(TOPK // 8):
                    own.link(dve.max(m8[:], s_i))
                    own.link(dve.match_replace(s_i, m8[:], s_i, TAKEN))
                own.step(dve.tensor_scalar(masks[:, MASK_AT[i]:MASK_AT[i] + span(i)], s_i, 0.5 * (TAKEN + DROP), DROP,
                                           ALU.is_gt, ALU.mult))
            own.wait()

            def take_qhead_norm(g):
                for tb in range(NB):
                    bank_ready(U_LOOP + PER_G * g + 1, 1 + 5 * g, tb)
                    dve.tensor_copy(nat[:, tb, :], pj[:, tb, :]).then_inc(proj_free, 1)
                dve.wait_ge(proj_free, 8 + 16 * g + 4)
                mean_square(lambda i: nat[:, i // 4, P * (i % 4):P * (i % 4) + P], 16, P)

            def scale_q(g):
                dve.wait_ge(rstd_ready, 4 + g)
                for tb in range(NB):
                    n3 = nat[:, tb, :].rearrange("p (h d) -> p h d", h=4)
                    dve.tensor_tensor(n3, n3, ms[:, 4 * tb:4 * tb + 4].unsqueeze(2).to_broadcast([P, 4, P]),
                                      ALU.mult).then_inc(q_ready, 1)

            def take_qT(g):
                for j in range(PER_KV):
                    dve.wait_ge(q_turned, 4 * g + j + 1)
                    dve.tensor_scalar(qT[:, j, :], pa[:, j, :], vec[:, V_QG:V_QG + 1], float(P) ** -0.5, ALU.mult,
                                      ALU.mult).then_inc(qT_ready, 1)

            def take_gate(g):
                for tb in range(NB):
                    bank_ready(U_LOOP + PER_G * g + 3, 2 + 5 * g, tb)
                    dve.tensor_copy(nat[:, tb, :], pj[:, tb, :]).then_inc(proj_free, 1)

            def silu_gate(g):
                for tb in range(NB):
                    use = 16 * g + tb
                    s_ = stage[:, use % 2, :]
                    dve.wait_ge(rg_exp, 4 * g + tb + 1)
                    own.link(dve.tensor_scalar(s_, s_, 1.0, None, ALU.add))
                    own.link(dve.reciprocal(s_, s_))
                    dve.tensor_tensor(s_, s_, nat[:, tb, :], ALU.mult).then_inc(stage_ready, 1)

            def take_rotated(g, gr):
                dec = C_QDEC if gr == GR_RQ else C_KDEC
                for tb in range(NB):
                    use = 16 * g + 4 * (gr - 1) + tb
                    x3 = pj[:, tb, :].rearrange("p (h d two) -> p h d two", h=4, two=2)
                    s3 = stage[:, use % 2, :].rearrange("p (h d two) -> p h d two", h=4, two=2)
                    cos = con[:, C_COS + 64 * tb:C_COS + 64 * tb + 64].unsqueeze(1).to_broadcast([P, 4, 64])
                    sin = con[:, C_SIN + 64 * tb:C_SIN + 64 * tb + 64].unsqueeze(1).to_broadcast([P, 4, 64])
                    r0 = rot[:, 0, :].rearrange("p (h d) -> p h d", h=4)
                    r1 = rot[:, 1, :].rearrange("p (h d) -> p h d", h=4)
                    bank_ready(U_LOOP + PER_G * g + 2 * gr + 1, 1 + gr + 5 * g, tb)
                    need(dve, ret_stored[use % 2], 16 * (use // 2))
                    own.step(dve.tensor_tensor(r0, x3[:, :, :, 0], cos, ALU.mult))
                    own.link(dve.tensor_tensor(r1, x3[:, :, :, 1], sin, ALU.mult))
                    own.step(dve.tensor_tensor(s3[:, :, :, 0], r0, r1, ALU.subtract))
                    own.wait()
                    own.step(dve.tensor_tensor(r0, x3[:, :, :, 0], sin, ALU.mult))
                    dve.tensor_tensor(r1, x3[:, :, :, 1], cos, ALU.mult).then_inc(proj_free, 1)
                    own.wait()
                    dve.wait_ge(proj_free, 8 + 16 * g + 4 * gr + tb + 1)
                    own.link(dve.tensor_tensor(s3[:, :, :, 1], r0, r1, ALU.add))
                    sh = stage[:, use % 2, :].rearrange("p (h d) -> p h d", h=4)
                    d_ = con[:, dec + 8 * tb + 4 * g:dec + 8 * tb + 4 * g + 4].unsqueeze(2).to_broadcast([P, 4, P])
                    dve.tensor_tensor(sh, sh, d_, ALU.mult).then_inc(stage_ready, 1)

            def take_v(g):
                for tb in range(NB):
                    use = 16 * g + 12 + tb
                    bank_ready(U_LOOP + PER_G * g + 9, 5 + 5 * g, tb)
                    need(dve, ret_stored[use % 2], 16 * (use // 2))
                    dve.tensor_copy(stage[:, use % 2, :], pj[:, tb, :]).then_inc(stage_ready, 1)

            def masked_logits(hd):
                for i in (0, 2, 1, 3):
                    bank, col = LOGIT_AT[i]
                    dve.wait_ge(logits_done, 3 * hd + bank + 1)
                    own.step(dve.tensor_tensor_reduce(
                        prob[:, MASK_AT[i]:MASK_AT[i] + span(i)], pa[:, bank, col:col + span(i)],
                        masks[:, MASK_AT[i]:MASK_AT[i] + span(i)], 1.0, -3.0e38, ALU.add, ALU.max, mx[:, i:i + 1]))
                own.wait()
                dve.tensor_scalar(mx[:, 4:8], mx[:, 0:4], -1.0, None, ALU.mult).then_inc(logits_ready, 1)

            def normalise(hd):
                dve.wait_ge(exp_done, 4 * hd + 4)
                own.link(dve.reciprocal(sums[:, 4:8], sums[:, 0:4]))
                for i in range(NB):
                    p_i = prob[:, MASK_AT[i]:MASK_AT[i] + span(i)]
                    dve.tensor_scalar(p_i, p_i, sums[:, 4 + i:5 + i], None, ALU.mult).then_inc(p_ready, 1)

            def take_pT(hd):
                for n, kb in enumerate(TURN_ORDER):
                    (bank, col), width = TURN_AT[kb], L - P * kb
                    dve.wait_ge(p_turned, 3 * hd + bank + 1)
                    dve.tensor_copy(pT[:, PT_AT[kb]:PT_AT[kb] + width], pa[:, bank, col:col + width]).then_inc(pT_ready, 1)

            def take_y(hd):
                dve.wait_ge(pv_done, hd + 1)
                dve.tensor_scalar(y_raw[:, hd, :], pa[:, 3, :], vec[:, V_DB + hd:V_DB + hd + 1], None,
                                  ALU.mult).then_inc(y_ready, 1)

            def later_acc(n):
                for k in range(8):
                    t = 8 * n + k
                    dve.wait_ge(ada_landed[t % 2], 16 * (t // 2 + 1))
                    if k > 0:
                        dve.wait_ge(ada_used, t)
                    multiply(acc[:, n % 2, :], lambda i, t=t: ada[:, t % 2, 512 * i:512 * i + 512],
                             (2 * k, 2 * k + 1), k == 0).then_inc(ada_used, 1)

            def take_later_mod(n):
                take_mod(8 + n, 0, 2 * KT + 4 * n)

            for q in range(U_LOOP, U_WO):
                g, m = divmod(q - U_LOOP, PER_G)
                if m == 0:
                    dve.tensor_copy(v_cur[:], v_nat[:, :, P * g:P * g + P]).then_inc(dve_step, 1)
                    own.n += 1
                if 1 <= q - U_LOOP <= 16:
                    take_later_mod(q - U_LOOP - 1)
                if m == 1:
                    take_qhead_norm(g)
                    scale_q(g)
                if m == 3:
                    take_qT(g)
                    take_gate(g)
                    silu_gate(g)
                if 5 <= m <= 8:
                    take_pT(4 * g + m - 5)
                if 4 <= m <= 7:
                    masked_logits(4 * g + m - 4)
                if 5 <= m <= 8:
                    take_y(4 * g + m - 5)
                if m in (5, 7):
                    take_rotated(g, GR_RQ if m == 5 else GR_RK)
                if m == 9:
                    take_v(g)
                if 4 <= m <= 7:
                    normalise(4 * g + m - 4)
                if q < U_LOOP + 16:
                    later_acc(q - U_LOOP)
            dve.wait_ge(mod_taken, 24)
            fold(0, 1, 4 * KT, V_N2, KT)

            for t in range(HEADS):
                dve.wait_ge(yd_hi, t + 1)
                dve.tensor_tensor(h[:, 8 + t, LO, :], y_raw[:, t, :], h[:, 8 + t, HI, :].bitcast(F32),
                                  ALU.subtract).then_inc(yd_ready, 1)

            def add_out(v, last):
                t = v % KT
                dve.wait_ge(chunk_used, 4 * U_WO + v + 1)
                if v == 0:
                    dve.wait_ge(resid_landed, 16)
                if last:
                    dve.wait_ge(added, v - KT + 1)
                dve.scalar_tensor_tensor(resid[:, t, :], pj[:, t % 4, :], mod[:, 2 * KT + t:2 * KT + t + 1],
                                         resid[:, t, :], ALU.mult, ALU.add).then_inc(added, 1)
                if last:
                    dve.wait_ge(added, v + 1)
                    if t == 0:
                        own.link(dve.tensor_tensor(ss[:], resid[:, t, :], resid[:, t, :], ALU.mult))
                    else:
                        own.link(dve.tensor_tensor(sq[:, 0, :], resid[:, t, :], resid[:, t, :], ALU.mult))
                        if t < KT - 1:
                            own.link(dve.tensor_tensor(ss[:], ss[:], sq[:, 0, :], ALU.add))
                        else:
                            dve.tensor_tensor(ss[:], ss[:], sq[:, 0, :], ALU.add).then_inc(ss_ready, 1)

            def ret_turned(k):
                for b in range(2):
                    dve.wait_ge(qk_turned, 2 * k + b + 1)
                    dve.tensor_copy(qkT[:, b, :], pa[:, b, :]).then_inc(qkT_ready, 1)
                dve.wait_ge(state_done, k + 1)
                dve.tensor_copy(state[:].rearrange("p a b -> p (a b)"), pa[:, 2, 0:3 * P]).then_inc(state_ready, 1)

            def ret_inner(k):
                dve.wait_ge(inner_done, k + 1)
                dve.tensor_tensor(innerT[:].rearrange("p (n c) -> p n c", n=NB),
                                  pa[:, 3, :].rearrange("p (n c) -> p n c", n=NB),
                                  causal.unsqueeze(1).to_broadcast([P, NB, P]), ALU.mult).then_inc(inner_ready, 1)

            def ret_norm(k):
                dve.wait_ge(o_done, k + 1)
                for n in range(NB):
                    own.step(dve.bn_stats(bn6[:, n, :], pa[:, 3, P * n:P * n + P]))
                own.wait()
                for n in range(NB):
                    own.step(dve.bn_aggr(bn2[:, n, :], bn6[:, n, :]))
                own.wait()
                dve.tensor_scalar(ms[:, 0:NB], bn2[:, :, 1], EPS, None, ALU.add).then_inc(ms_ready, 1)
                dve.wait_ge(rstd_ready, 6 + k)
                for n in range(NB):
                    own.step(dve.tensor_scalar(z[:, n, :], pa[:, 3, P * n:P * n + P], bn2[:, n, 0:1], ms[:, n:n + 1],
                                               ALU.subtract, ALU.mult))
                own.wait()
                dve.tensor_tensor(z[:], z[:], ret[:, k % 3, 0], ALU.mult).then_inc(z_ready, 1)

            def ret_low(k):
                dve.wait_ge(yr_hi, k + 1)
                dve.scalar_tensor_tensor(h[:, k, LO, :], pa[:, 0, :], vec[:, V_RB + k:V_RB + k + 1],
                                         h[:, k, HI, :].bitcast(F32), ALU.mult, ALU.subtract).then_inc(yr_ready, 1)

            for r in range(16):
                add_out(r, False)
                k, odd = divmod(r, 2)
                if not odd:
                    if k > 0:
                        ret_norm(k - 1)
                    ret_turned(k)
                else:
                    ret_inner(k)
                    if k > 0:
                        ret_low(k - 1)
            ret_norm(7)
            ret_low(7)
            for r in range(16, 32):
                add_out(r, True)

            dve.wait_ge(ss_summed, 1)
            dve.tensor_scalar(rstd2[:], pa[:, 2, :], 1.0 / D, EPS, ALU.mult, ALU.add).then_inc(ms_ready, 1)
            dve.wait_ge(rstd_ready, 14)
            for kt in range(KT + 1):
                if kt < KT:
                    modulate(kt, 1, resid, rstd2[:], relu, 3 * KT, t2_ready, h2_hi, h2_ready, 0)
                if kt > 0:
                    modulate(kt - 1, 1, resid, rstd2[:], relu, 3 * KT, t2_ready, h2_hi, h2_ready, 1)

            def mlp_step(c, last):
                for n in range(9):
                    if n < 8:
                        dve.wait_ge(relu_done, 8 * c + n + 1)
                        if n > 1:
                            dve.wait_ge(mid_ready, 8 * c + n - 1)
                        dve.tensor_tensor(sq[:, n % 2, :], relu[:, n % 2, :], relu[:, n % 2, :],
                                          ALU.mult).then_inc(sq_ready, 1)
                    if n > 0:
                        dve.wait_ge(mid_hi, 8 * c + n)
                        dve.tensor_tensor(mid[:, n - 1, LO, :], sq[:, (n - 1) % 2, :],
                                          mid[:, n - 1, HI, :].bitcast(F32), ALU.subtract).then_inc(mid_ready, 1)
                dve.wait_ge(mid_ready, 8 * c + 8)
                dve.wait_ge(added, 32 + 16 * c)
                for t in range(KT):
                    v, j = divmod(t, 4)
                    dve.wait_ge(chunk_used, 4 * (U_MLP + 4 + v) + j + 1 + 32 * c)
                    dve.scalar_tensor_tensor(resid[:, t, :], (pa if v % 2 else pj)[:, j, :],
                                             mod[:, 5 * KT + t:5 * KT + t + 1], resid[:, t, :], ALU.mult,
                                             ALU.add).then_inc(added, 1)

            with dve.Fori(0, STEPS) as c:
                mlp_step(c, False)

        @block.tensor
        def _(pe):
            def product(dst, lhs, rhs, start, stop):
                for n, (a, b) in enumerate(PASSES):
                    last = pe.matmul(dst, lhs[a], rhs[b], start=start and n == 0, stop=stop and n == 2)
                return last

            def turn(dst, src):
                return pe.transpose(dst, src, ident)

            group_use = [0]

            def tokens_chunk(u, j, k0, is_first, is_last, freed, count):
                pe.wait_ge(lo_done, 4 * u + j + 1)
                for tb in range(NB):
                    if is_first and j == 0:
                        pe.wait_ge(freed, count + tb + 1)
                    for kk in range(2):
                        kt = k0 + 2 * j + kk
                        cols = slice(512 * kk, 512 * kk + 512)
                        last = product(pj[:, tb, :], [h[:, kt, s, P * tb:P * tb + P] for s in (HI, LO)],
                                       [w_hi[:, j, cols], w_lo[:, j, cols]],
                                       is_first and j == 0 and kk == 0, is_last and j == 3 and kk == 1)
                    if is_last and j == 3 and tb < 3:
                        last.then_inc(proj_done, 1)
                last.then_inc(chunk_used, 1)

            def features_chunk(q, src, k0, bank, start, stop, ready=None, count=0, trip=0):
                j = q % 4
                pe.wait_ge(lo_done, q + 1 + 32 * trip)
                for kk in range(8):
                    if ready is not None:
                        pe.wait_ge(ready, count + kk + 1)
                    last = product(bank, [w[:, j, P * kk:P * kk + P] for w in (w_hi, w_lo)],
                                   [src[:, k0 + kk, s, :] for s in (HI, LO)], start and kk == 0, stop and kk == 7)
                last.then_inc(chunk_used, 1)

            pe.wait_ge(const_landed, 16)
            pe.wait_ge(rows_landed, 32)
            pe.transpose(pa[:, 0, 0:96], raw[0:96, 0, 2048:2176], con[0:96, C_ID:C_ID + 96]).then_inc(rows_turned, 1)
            pe.transpose(pa[:, 1, 0:V_ROWS], raw[0:V_ROWS, 0, 2176:2304],
                         con[0:V_ROWS, C_ID:C_ID + V_ROWS]).then_inc(rows_turned, 1)
            for tb in range(NB):
                pe.wait_ge(x_landed[tb % 2], 16 * (tb // 2 + 1))
                for q in range(4):
                    need(pe, x_taken, 4 * tb + q - 3)
                    for m in range(4):
                        last = turn(pj[:, q, P * m:P * m + P], x_nat[:, tb % 2, P * (4 * q + m):P * (4 * q + m + 1)])
                    last.then_inc(x_turned, 1)
            for kt in range(KT):
                pe.wait_ge(x_squared, kt + 1)
                pe.matmul(pa[:, 2, :], ones, tmp1[:, kt % 2, :], start=kt == 0, stop=kt == KT - 1).then_inc(x_summed, 1)

            def sum_mod(n, col, counted, value):
                pe.wait_ge(counted, value)
                for m in range(4):
                    last = pe.matmul(pa[:, 3, col + m:col + m + 1], acc[:, n % 2, P * m:P * m + P], ones[:, 0:1],
                                     start=True, stop=True)
                last.then_inc(mod_summed, 1)

            for cc in range(4):
                for sec in range(2):
                    n = 2 * cc + sec
                    need(pe, mod_taken, 2 * cc)
                    sum_mod(n, 4 * sec, first_used, 4 * (n + 1))
                pe.wait_ge(h_ready, 4 * cc + 4)
                pe.wait_ge(lo_done, cc + 1)
                for tb in range(NB):
                    for kk in range(4):
                        cols = slice(SMALL * kk, SMALL * kk + SMALL)
                        last = product(pj[:, tb, 0:SMALL],
                                       [h[:, 4 * cc + kk, s, P * tb:P * tb + P] for s in (HI, LO)],
                                       [w_hi[:, cc, cols], w_lo[:, cc, cols]],
                                       cc == 0 and kk == 0, cc == 3 and kk == 3)
                last.then_inc(chunk_used, 1)

            def index_item(n):
                i, hh = ITEMS[n]
                rows = slice(IDX_DIM * (hh % 2), IDX_DIM * (hh % 2) + IDX_DIM)
                if n < 4:
                    pe.wait_ge(ikT_ready, 1)
                    pe.wait_ge(kT_ready, KV)
                    pe.wait_ge(mod_taken, 8)
                need(pe, idx_taken, n - 3)
                need(pe, iq_ready, 4 if n < 24 else 8)
                pe.matmul(pa[:, n % 4, 0:span(i)], iqT[rows, hh // 2, P * i:P * i + P], ikT[rows, 0:span(i)],
                          start=True, stop=True).then_inc(idx_done, 1)

            for u in (1, 2):
                for j in range(4):
                    tokens_chunk(u, j, 8 * (u - 1), u == 1, u == 2, proj_free, 0)
                if u == 1:
                    pe.wait_ge(ik_ready, 8)
                    for tb in range(NB):
                        last = turn(pa[:, 0, P * tb:P * tb + P], ik2[:, tb].rearrange("p a b -> p (a b)"))
                    last.then_inc(ik_turned, 1)
            for u in range(U_IQ, U_LOOP):
                part, hf = divmod(u - U_IQ, 2)
                for j in range(4):
                    if hf == 0:
                        if part == 0:
                            pe.wait_ge(proj_free, 4 + j + 1)
                        else:
                            pe.wait_ge(iq_ready, j + 1)
                    features_chunk(4 * u + j, h, 8 * hf, pj[:, j, :], hf == 0, hf == 1)
                    if part == 1:
                        for n in range(3 * (4 * hf + j), 3 * (4 * hf + j) + 3):
                            index_item(n)
                if u == U_IQ:
                    pe.wait_ge(k_ready, 8)
                    for g in range(KV):
                        for tb in range(NB):
                            last = turn(pa[:, 1 + g, P * tb:P * tb + P], k_nat[:, tb, P * g:P * g + P])
                        last.then_inc(k_turned, 1)
            for n in range(24, 48):
                index_item(n)

            def q_transposes(g):
                pe.wait_ge(q_ready, 4 * g + 4)
                need(pe, mod_taken, 8 + PER_G * g + 3)
                pe.wait_ge(idx_taken, 48)
                need(pe, y_ready, 4 * g)
                for j in range(PER_KV):
                    for tb in range(NB):
                        last = turn(pa[:, j, P * tb:P * tb + P], nat[:, tb, P * j:P * j + P])
                    last.then_inc(q_turned, 1)

            def head_logits(hd):
                g, j = divmod(hd, PER_KV)
                pe.wait_ge(qT_ready, 4 * g + 4)
                need(pe, pT_ready, 4 * hd)
                for i in (0, 2, 1, 3):
                    bank, col = LOGIT_AT[i]
                    last = pe.matmul(pa[:, bank, col:col + span(i)], qT[:, j, P * i:P * i + P], kT[:, g, 0:span(i)],
                                     start=True, stop=True)
                    if i != 0:
                        last.then_inc(logits_done, 1)

            def p_transposes(hd):
                pe.wait_ge(p_ready, 4 * hd + 4)
                need(pe, pT_ready, 4 * hd)
                for kb in TURN_ORDER:
                    bank, col = TURN_AT[kb]
                    for i in range(kb, NB):
                        at_ = MASK_AT[i] + P * kb
                        last = turn(pa[:, bank, col + P * (i - kb):col + P * (i - kb + 1)], prob[:, at_:at_ + P])
                    if kb != 1:
                        last.then_inc(p_turned, 1)

            def head_out(hd):
                for kb in range(NB):
                    pe.wait_ge(pT_ready, 4 * hd + (1, 2, 4, 4)[kb])
                    width = L - P * kb
                    last = pe.matmul(pa[:, 3, P * kb:], v_cur[:, kb, :], pT[:, PT_AT[kb]:PT_AT[kb] + width],
                                     start=kb == 0, stop=kb == NB - 1, skip_group_check=True)
                last.then_inc(pv_done, 1)

            for q in range(U_LOOP, U_WO):
                g, m = divmod(q - U_LOOP, PER_G)
                if m < 2:
                    freed, count = (stage_ready, 16 * g - 4) if g else (iq_ready, 4)
                else:
                    freed, count = proj_free, 8 + 16 * g + 4 * (m // 2 - 1)
                for j in range(4):
                    tokens_chunk(q, j, 8 * (m % 2), m % 2 == 0, m % 2 == 1, freed, count)
                if 1 <= q - U_LOOP <= 16:
                    n = q - U_LOOP - 1
                    if n == 0:
                        pe.wait_ge(idx_taken, 48)
                    need(pe, y_ready, max(0, min(4, m - 5)) + 4 * g)
                    need(pe, qT_ready, 4 * (g + (m > 3)))
                    pe.wait_ge(mod_taken, 8 + n)
                    sum_mod(n, 0, ada_used, 8 * (n + 1))
                if m == 3:
                    q_transposes(g)
                if 5 <= m <= 8:
                    p_transposes(4 * g + m - 5)
                    pe.wait_ge(pT_ready, 4 * (4 * g + m - 4))
                if 4 <= m <= 7:
                    head_logits(4 * g + m - 4)
                if 5 <= m <= 8:
                    need(pe, mod_taken, 8 + min(16, q - U_LOOP))
                    head_out(4 * g + m - 5)

            def ret_turn(k):
                pe.wait_ge(ret_landed[k % 3], 64 * (k // 3 + 1))
                pe.wait_ge(y_ready, HEADS)
                need(pe, yr_ready, k - 1 if k else 0)
                need(pe, state_ready, k)
                for b, kind in enumerate((1, 2)):
                    for n in range(NB):
                        last = turn(pa[:, b, P * n:P * n + P], ret[:, k % 3, kind, n, :])
                    last.then_inc(qk_turned, 1)
                for n in range(1, NB):
                    for e in range(n):
                        last = pe.matmul(pa[:, 2, P * (n - 1):P * n], ret[:, k % 3, 2, e, :], ret[:, k % 3, 3, e, :],
                                         start=e == 0, stop=e == n - 1)
                last.then_inc(state_done, 1)

            def ret_inner(k):
                pe.wait_ge(qkT_ready, 2 * k + 2)
                need(pe, z_ready, k)
                for n in range(NB):
                    last = pe.matmul(pa[:, 3, P * n:P * n + P], qkT[:, 1, P * n:P * n + P], qkT[:, 0, P * n:P * n + P],
                                     start=True, stop=True)
                last.then_inc(inner_done, 1)

            def ret_out(k):
                pe.wait_ge(inner_ready, k + 1)
                pe.wait_ge(state_ready, k + 1)
                for n in range(NB):
                    last = pe.matmul(pa[:, 3, P * n:P * n + P], innerT[:, P * n:P * n + P], ret[:, k % 3, 3, n, :],
                                     start=True, stop=n == 0)
                    if n > 0:
                        last = pe.matmul(pa[:, 3, P * n:P * n + P], qkT[:, 0, P * n:P * n + P], state[:, n - 1, :],
                                         start=False, stop=True)
                last.then_inc(o_done, 1)

            def ret_back(k):
                pe.wait_ge(z_ready, k + 1)
                pe.wait_ge(qkT_ready, 2 * min(k + 2, HEADS))
                for n in range(NB):
                    last = turn(pa[:, 0, P * n:P * n + P], z[:, n, :])
                last.then_inc(z_turned, 1)

            for r in range(32):
                half_, t = divmod(r, KT)
                if r >= 4:
                    pe.wait_ge(added, r - 3)
                if r < 4:
                    pe.wait_ge(stage_ready, 28 + r + 1)
                features_chunk(4 * U_WO + r, h, 8 * (1 - half_), pj[:, t % 4, :], True, True,
                               (yd_ready if half_ == 0 else yr_ready) if t == 0 else None)
                if r < 16:
                    k, odd = divmod(r, 2)
                    if not odd:
                        if k > 0:
                            ret_out(k - 1)
                        need(pe, yr_ready, k - 1)
                        ret_turn(k)
                    else:
                        ret_inner(k)
                        if k > 0:
                            ret_back(k - 1)
                if r == 15:
                    ret_out(7)
                    ret_back(7)

            pe.wait_ge(ss_ready, 1)
            pe.matmul(pa[:, 2, :], ones, ss[:], start=True, stop=True).then_inc(ss_summed, 1)

            def mlp_step(c):
                for m in range(4):
                    a, hf = divmod(m, 2)
                    banks = pa if a else pj
                    for j in range(4):
                        if hf == 0:
                            pe.wait_ge(added, (24 if a == 0 else 28) + j + 1 + 16 * c)
                        features_chunk(4 * (U_MLP + m) + j, h, 8 * hf, banks[:, j, :], hf == 0, hf == 1,
                                       h2_ready if a == 0 and j == 0 else None, 8 * hf, c)
                for v in range(4):
                    banks = pa if v % 2 else pj
                    for j in range(4):
                        if v < 2:
                            pe.wait_ge(relu_done, 4 * v + j + 1 + 8 * c)
                        else:
                            pe.wait_ge(added, 32 + 4 * (v - 2) + j + 1 + 16 * c)
                        q = 4 * (U_MLP + 4 + v) + j
                        pe.wait_ge(lo_done, q + 1 + 32 * c)
                        for kk in range(8):
                            if v == 0 and j == 0:
                                pe.wait_ge(mid_ready, kk + 1 + 8 * c)
                            last = product(banks[:, j, :], [w[:, j, P * kk:P * kk + P] for w in (w_hi, w_lo)],
                                           [mid[:, kk, s, :] for s in (HI, LO)], kk == 0, kk == 7)
                        last.then_inc(chunk_used, 1)

            with pe.Fori(0, STEPS) as c:
                mlp_step(c)
            for t in range(KT):
                pe.wait_ge(added, 32 + 16 * (STEPS - 1) + t + 1)
                banks = pa if t // 4 % 2 else pj
                if t < 8:
                    pe.wait_ge(added, 32 + 16 * (STEPS - 1) + t + 9)
                else:
                    pe.wait_ge(out_ready, t - 7)
                for tb in range(NB):
                    last = turn(banks[:, t % 4, P * tb:P * tb + P], resid[:, t, P * tb:P * tb + P])
                last.then_inc(out_turned, 1)


def _constants():
    c = np.zeros((P, C_END), np.float32)
    i = np.arange(P)
    c[:, C_ID:C_ID + P] = np.eye(P)
    c[:, C_CAUSAL:C_CAUSAL + P] = i[None, :] >= i[:, None]
    c[:, C_NEG:C_NEG + P] = np.where(i[None, :] <= i[:, None], 0.0, DROP)
    c[:, C_ONES:C_ONES + P] = 1.0
    angle = (1.0 / (np.float32(10000.0) ** np.linspace(0.0, 1.0, P // 2, dtype=np.float32))).astype(np.float32)
    for b in range(NB):
        theta = ((P * b + i).astype(np.float32)[:, None] * angle[None, :]).astype(np.float64)
        c[:, C_COS + 64 * b:C_COS + 64 * b + 64] = np.cos(theta)
        c[:, C_SIN + 64 * b:C_SIN + 64 * b + 64] = np.sin(theta)
        for hd in range(HEADS):
            log_gamma = math.log(1.0 - 2.0 ** (-5.0 - hd))
            c[:, C_QDEC + 8 * b + hd] = np.exp(log_gamma * (P * b + i))
            c[:, C_KDEC + 8 * b + hd] = np.exp(-log_gamma * (P * b + i)) * P ** -0.5
    return c


def kernel(x, c, w_ada, b_ada, norm1_g, norm2_g, w_in, ret_beta, q_norm_g, k_norm_g, idx_k_norm_g, dsa_beta,
           w_out, w_mlp1, w_mlp2):
    import concourse.bacc as _bacc
    from concourse.bass_utils import run_bass_kernel_spmd as _run

    flat = lambda a: np.ascontiguousarray(a).reshape(-1)
    arrays = {
        "x_in": np.ascontiguousarray(x).reshape(L, D),
        "vecs": np.concatenate([flat(a) for a in (c, norm1_g, norm2_g, ret_beta, dsa_beta, q_norm_g, k_norm_g,
                                                  idx_k_norm_g, idx_k_norm_g)]).reshape(V_ROWS, P),
        "b_ada_in": np.ascontiguousarray(b_ada).reshape(6 * KT, P),
        "consts": _constants(),
        "w_ada_in": np.ascontiguousarray(w_ada).reshape(D, 6 * D),
        "w_in_in": np.ascontiguousarray(w_in).reshape(D, -1),
        "w_out_in": np.ascontiguousarray(w_out).reshape(D, D),
        "w_mlp1_in": np.ascontiguousarray(w_mlp1).reshape(D, FF),
        "w_mlp2_in": np.ascontiguousarray(w_mlp2).reshape(FF, D),
    }
    nc = _bacc.Bacc("TRN2", target_bir_lowering=False, num_devices=1)
    args = [nc.dram_tensor(n, a.shape, mybir.dt.from_np(a.dtype), kind="ExternalInput").ap()
            for n, a in arrays.items()]
    out = nc.dram_tensor("out", (L, D), F32, kind="ExternalOutput").ap()
    build(nc, *args, out)
    r = _run(nc, [arrays], core_ids=[0])
    return r.results[0]["out"].reshape(1, L, D)
```

```python
import math

import numpy as np

import concourse.bass as bass
from concourse import mybir

F32 = mybir.dt.float32
F32R = mybir.dt.float32r
ALU = mybir.AluOpType
ACT = mybir.ActivationFunctionType
AX = mybir.AxisListType

P = 128
L = 512
D = 2048
NB = L // P
KT = D // P
FF = 4 * D
HEADS = 8
KV = 2
PER_KV = HEADS // KV
HW = HEADS * P
IDX_HEADS, IDX_DIM = 16, 64
TOPK = L // 4
EPS = 1e-6
DROP = -3.0e38
TAKEN = -3.4e38
COL_RQ, COL_RK, COL_RV, COL_RG = 0, HW, 2 * HW, 3 * HW
COL_DQ = 4 * HW
COL_DK = COL_DQ + HW
COL_IQ = COL_DK + 2 * KV * P
COL_IK = COL_IQ + IDX_HEADS * IDX_DIM
SMALL = IDX_DIM + IDX_HEADS
HI, LO = 0, 1
PASSES = ((HI, HI), (HI, LO), (LO, HI))
V_C, V_N1, V_N2, V_RB, V_DB, V_QG, V_KG, V_IG, V_ROWS = 0, 16, 32, 48, 56, 64, 65, 66, 67
C_ID, C_CAUSAL, C_NEG, C_ONES, C_COS, C_SIN, C_QDEC, C_KDEC, C_END = (
    0, 128, 256, 384, 512, 768, 1024, 1056, 1088)

U_DKV, U_SMALL, U_IQ, U_LOOP, PER_G = 0, 2, 3, 7, 10
U_WO = U_LOOP + KV * PER_G
U_MLP = U_WO + 8
PER_C = 8
STEPS = FF // 1024
GR_DQ, GR_RG, GR_RQ, GR_RK, GR_RV = range(5)
Q_LOOP, Q_WO, Q_MLP = 4 * U_LOOP, 4 * U_WO, 4 * U_MLP
PER_GQ = 4 * PER_G
LOGITS_AT = (19, 22, 27, 30)
TURNS_AT = (21, 26, 29, 34)
OUTS_AT = (22, 27, 30, 35)
Q_TURN_AT = 11
Q_TOPK = 31
ROUNDS = (4, 4, 4, 4, 3, 3, 3, 3, 4, 3, 3, 3, 3, 2, 2)
Q_ADA = 44
ADA_ACCS = 16


def need(eng, sem, value):
    if isinstance(value, int) and value <= 0:
        return
    eng.wait_ge(sem, value)


class Steps:

    def __init__(self, eng, sem):
        self.eng, self.sem, self.n = eng, sem, 0

    def step(self, ins):
        ins.then_inc(self.sem, 1)
        self.n += 1

    def link(self, ins):
        self.step(ins)
        self.eng.wait_ge(self.sem, self.n)

    def wait(self):
        self.eng.wait_ge(self.sem, self.n)


def build(nc, x, vecs, b_ada, consts, w_ada, w_in, w_out, w_mlp1, w_mlp2, out):
    base = 16512

    def at(name, offset, shape, dt=F32):
        return nc.alloc_sbuf_tensor_at(name, shape, dt, offset=base + offset)

    h = at("h", 0, [P, KT, 2, L], F32R)
    raw = at("raw", 65536, [P, 2, 4096])
    w_hi = at("w_hi", 98304, [P, 4, 1024], F32R)
    w_lo = at("w_lo", 114688, [P, 4, 1024], F32R)
    XR = 131072
    resid = at("resid", XR, [P, KT, L])
    iqT = at("iqT", XR, [P, 8, L])
    y_raw = at("y_raw", XR, [P, HEADS, L])
    kT = at("kT", XR + 16384, [P, KV, L])
    v_nat = at("v_nat", XR + 20480, [P, NB, KV * P])
    qT = at("qT", XR + 24576, [P, PER_KV, L])
    RB = XR + 32768
    con = at("con", RB, [P, C_END])
    cursor = [RB + 4 * C_END]

    def small(name, *shape):
        t = at(name, cursor[0], [P, *shape])
        cursor[0] += -(-4 * math.prod(shape) // 32) * 32
        return t

    bias_cols = small("bias_cols", 6 * KT)
    vec = small("vec", V_ROWS + 1)
    mod = small("mod", 6 * KT)
    gain = small("gain", 2, KT)
    csilu = small("csilu", 2, KT)
    half = small("half", 8)
    mx = small("mx", 8)
    sums = small("sums", 8)
    ms = small("ms", 16)
    m8 = small("m8", 8)
    bn6 = small("bn6", NB, 6)
    bn2 = small("bn2", NB, 2)
    w_idx = small("w_idx", NB, IDX_HEADS)
    RC = RB + 4352 + 2048
    acc = at("acc", RC, [P, 2, L])
    ada = at("ada", RC + 4096, [P, 2, 1024])
    score = at("score", RC + 12288, [P, 1280])
    pT = at("pT", RC + 12288, [P, 1280])
    masks = at("masks", RC + 17408, [P, 1280])
    nat = at("nat", RC + 22528, [P, NB, L])
    prob = at("prob", RC + 22528, [P, 1280])
    k_nat = at("k_nat", RC + 22528, [P, NB, KV * P])
    ik_nat = at("ik_nat", RC + 26624, [P, NB, IDX_DIM])
    ik2 = at("ik2", RC + 27648, [P, NB, 2, IDX_DIM])
    ikT = at("ikT", RC + 30720, [P, L])
    v_cur = at("v_cur", RC + 32768, [P, NB, P])
    rstd1 = at("rstd1", RC + 32768, [P, L])
    x_junk = at("x_junk", RC + 12288, [P, D])
    rows = at("rows", RC + 20480, [P, 2, P])
    rot = at("rot", RC + 34816, [P, 2, 256])
    junk = at("junk", RC + 34816, [P, L])
    stage = at("stage", RC + 36864, [P, 2, L])
    tmp1 = at("tmp1", RC + 36864, [P, 2, L])
    diag1 = at("diag1", RC + 36864, [P, NB, P])
    x_nat = at("x_nat", 65536 + 16384, [P, 2, D])
    first = [at("ada_first0", 12 * 4096, [P, 2048]), at("ada_first1", 14 * 4096, [P, 2048]),
             at("ada_first2", RC + 4096, [P, 2048]), at("ada_first3", RC + 22528, [P, 2048])]
    ret = at("ret", RC, [P, 3, 4, NB, P])
    qkT = at("qkT", RC + 24576, [P, 2, L])
    innerT = at("innerT", RC + 28672, [P, L])
    state = at("state", RC + 30720, [P, 3, P])
    z = at("z", RC + 32768, [P, NB, P])
    ysum = at("ysum", RC + 34816, [P, L])
    ss = at("ss", RC, [P, L])
    diag2 = at("diag2", RC + 2048, [P, NB, P])
    mid = at("mid", RC, [P, 8, 2, L], F32R)
    relu = at("relu", RC + 32768, [P, 2, L])
    out_nat = at("out_nat", RC + 32768, [P, 2, L])
    sq = at("sq", RC + 36864, [P, 2, L])

    pj = nc.alloc_psum_tensor("pj", [P, 4, L], F32)
    pa = nc.alloc_psum_tensor("pa", [P, 4, L], F32)

    xT_dram = nc.dram_tensor("xT_dram", (P, KT, L), F32).ap()
    ret_dram = nc.dram_tensor("ret_dram", (4, L, HW), F32).ap()

    ident, causal = con[:, C_ID:C_ID + P], con[:, C_CAUSAL:C_CAUSAL + P]
    neg, ones = con[:, C_NEG:C_NEG + P], con[:, C_ONES:C_ONES + P]

    sem = nc.alloc_semaphore
    const_landed, rows_landed = sem("const_landed"), sem("rows_landed")
    x_landed = [sem("x_landed0"), sem("x_landed1")]
    first_landed = [sem(f"first_landed{i}") for i in range(4)]
    ada_landed = [sem("ada_landed0"), sem("ada_landed1")]
    raw_landed = [sem("raw_landed0"), sem("raw_landed1")]
    xT_stored, resid_landed = sem("xT_stored"), sem("resid_landed")
    ret_stored = [sem("ret_stored0"), sem("ret_stored1")]
    v_taken, v_stored = sem("v_taken"), sem("v_stored")
    ret_landed = [sem(f"ret_landed{i}") for i in range(3)]
    out_stored = [sem("out_stored0"), sem("out_stored1")]
    hi_done, lo_done, chunk_used = sem("hi_done"), sem("lo_done"), sem("chunk_used")
    proj_done, proj_free = sem("proj_done"), sem("proj_free")
    rows_turned, rows_taken = sem("rows_turned"), sem("rows_taken")
    half_set, silu_exp, silu_ready = sem("half_set"), sem("silu_exp"), sem("silu_ready")
    x_turned, x_taken = sem("x_turned"), sem("x_taken")
    x_squared = sem("x_squared")
    diag_ready, rstd_spread = sem("diag_ready"), sem("rstd_spread")
    ms_ready, rstd_ready = sem("ms_ready"), sem("rstd_ready")
    first_used, ada_used, acc_ready = sem("first_used"), sem("ada_used"), sem("acc_ready")
    mod_summed, mod_taken = sem("mod_summed"), sem("mod_taken")
    t_ready, h_hi, h_ready = sem("t_ready"), sem("h_hi"), sem("h_ready")
    ik_ready, ik_turned, ikT_ready = sem("ik_ready"), sem("ik_turned"), sem("ikT_ready")
    k_ready, k_turned, kT_ready = sem("k_ready"), sem("k_turned"), sem("kT_ready")
    iq_ready, idx_done, idx_taken = sem("iq_ready"), sem("idx_done"), sem("idx_taken")
    idx_added = sem("idx_added")
    q_ready, q_turned, qT_ready = sem("q_ready"), sem("q_turned"), sem("qT_ready")
    rg_exp, stage_ready = sem("rg_exp"), sem("stage_ready")
    logits_done, logits_ready = sem("logits_done"), sem("logits_ready")
    exp_done, p_ready, p_turned, pT_ready = sem("exp_done"), sem("p_ready"), sem("p_turned"), sem("pT_ready")
    pv_done, y_ready = sem("pv_done"), sem("y_ready")
    yd_hi, yd_ready = sem("yd_hi"), sem("yd_ready")
    qk_turned, qkT_ready = sem("qk_turned"), sem("qkT_ready")
    state_done, state_ready = sem("state_done"), sem("state_ready")
    inner_done, inner_ready = sem("inner_done"), sem("inner_ready")
    o_done, z_ready, z_turned = sem("o_done"), sem("z_ready"), sem("z_turned")
    yr_hi, yr_ready = sem("yr_hi"), sem("yr_ready")
    added = sem("added")
    ss_ready, ss_summed = sem("ss_ready"), sem("ss_summed")
    t2_ready, h2_hi, h2_ready = sem("t2_ready"), sem("h2_hi"), sem("h2_ready")
    relu_done, sq_ready, mid_hi, mid_ready = sem("relu_done"), sem("sq_ready"), sem("mid_hi"), sem("mid_ready")
    out_turned, out_ready = sem("out_turned"), sem("out_ready")
    dve_step = sem("dve_step")

    w_in_v = w_in.rearrange("(k p) n -> p k n", p=P)
    w_out_v = w_out.rearrange("(k p) n -> p k n", p=P)
    w1_v = w_mlp1.rearrange("(k p) n -> p k n", p=P)
    w2_v = w_mlp2.rearrange("(k p) n -> p k n", p=P)
    ada_v = w_ada.rearrange("(k p) n -> p k n", p=P)

    def unit_source(u):
        if u == U_SMALL:
            return w_in_v[:, :, COL_IK:COL_IK + SMALL]
        if u < U_SMALL:
            k, col = 8 * (u - U_DKV), COL_DK
        elif u < U_LOOP:
            k, col = 8 * ((u - U_IQ) % 2), COL_IQ + 512 * ((u - U_IQ) // 2)
        elif u < U_WO:
            g, m = divmod(u - U_LOOP, PER_G)
            first_col = {GR_DQ: COL_DQ, GR_RG: COL_RG, GR_RQ: COL_RQ, GR_RK: COL_RK, GR_RV: COL_RV}[m // 2]
            k, col = 8 * (m % 2), first_col + 512 * g
        else:
            half_, v = divmod(u - U_WO, 4)
            return w_out_v[:, 8 * (1 - half_):8 * (2 - half_), 512 * v:512 * v + 512]
        return w_in_v[:, k:k + 8, col:col + 512]

    def is_tiles(u):
        return U_IQ <= u < U_LOOP or u >= U_WO

    def raw_chunk(u, j):
        slot = raw[:, u % 2, :]
        if u == U_SMALL:
            return slot[:, 320 * j:320 * j + 320]
        if is_tiles(u):
            return slot.rearrange("p (k n) -> p k n", k=8)[:, :, P * j:P * j + P]
        return slot[:, 1024 * j:1024 * j + 1024]

    def split_chunk(w, u, j):
        if u == U_SMALL:
            return w[:, j, 0:320]
        if is_tiles(u):
            return w[:, j, :].rearrange("p (k n) -> p k n", k=8)
        return w[:, j, :]

    def span(i):
        return P * (i + 1)

    MASK_AT = [0, 128, 384, 768]
    SCORE_AT = [0, 0, 256, 640]
    LOGIT_AT = [(0, 0), (1, 0), (0, 128), (2, 0)]
    TURN_AT = [(0, 0), (1, 0), (2, 0), (1, 384)]
    PT_AT = [0, 512, 896, 1152]
    TURN_ORDER = (0, 1, 3, 2)

    ITEMS = [(i, hh) for part in range(2) for i in (1, 2, 3) for hh in range(8 * part, 8 * part + 8)]

    block = nc.Block()
    with block:

        @block.sync
        def _(sp):
            def ada_piece(t):
                n, k = divmod(t, 8)
                col = 2 * D + 512 * n
                if t == 0:
                    sp.wait_ge(first_used, 32)
                need(sp, ada_used, t - 1)
                sp.dma_start(ada[:, t % 2, :].rearrange("p (k n) -> p k n", k=2),
                             ada_v[:, 2 * k:2 * k + 2, col:col + 512]).then_inc(ada_landed[t % 2], 16)

            def store(g, gr, tb):
                use = 12 * g + 4 * (gr - 1) + tb
                sp.wait_ge(stage_ready, use + 1)
                sp.dma_start(ret_dram[gr - 1, P * tb:P * tb + P, 512 * g:512 * g + 512],
                             stage[:, use % 2, :]).then_inc(ret_stored[use % 2], 16)

            def store_v(g):
                sp.wait_ge(v_taken, 4 * g + 4)
                sp.dma_start(ret_dram[3, :, 512 * g:512 * g + 512].rearrange("(b p) n -> p b n", p=P),
                             nat[:]).then_inc(v_stored, 16)

            def load_head(k):
                g = k // 4
                if k < 3:
                    sp.wait_ge(y_ready, HEADS)
                    sp.wait_ge(mod_taken, 8 + ADA_ACCS)
                else:
                    sp.wait_ge(z_ready, k - 2)
                for s in range(2):
                    sp.wait_ge(ret_stored[s], 96 * (g + 1))
                sp.wait_ge(v_stored, 16 * (g + 1))
                for kind in range(4):
                    sp.dma_start(ret[:, k % 3, kind], ret_dram[kind, :, P * k:P * k + P]
                                 .rearrange("(b p) d -> p b d", p=P)).then_inc(ret_landed[k % 3], 16)

            def slot(q):
                if Q_LOOP <= q < Q_WO:
                    g, r = divmod(q - Q_LOOP, PER_GQ)
                    if r in (16, 17):
                        for tb in (0, 1):
                            store(g, GR_RG, 2 * (r - 16) + tb)
                    if r in (23, 31):
                        for tb in range(NB):
                            store(g, GR_RQ if r == 23 else GR_RK, tb)
                    if r == 39:
                        store_v(g)
                if Q_ADA - 1 <= q < Q_WO - 1:
                    for t in range(2 * (q + 1 - Q_ADA), 2 * (q + 1 - Q_ADA) + 2):
                        ada_piece(t)

            def after_unit(u):
                if u == U_WO - 1:
                    for k in range(3):
                        load_head(k)
                    sp.wait_ge(yd_ready, HEADS)
                    sp.wait_ge(xT_stored, 16)
                    sp.dma_start(resid[:], xT_dram).then_inc(resid_landed, 16)
                for k in {U_WO: (3,), U_WO + 1: (4, 5), U_WO + 2: (6, 7)}.get(u, ()):
                    load_head(k)

            def load_unit(u):
                need(sp, lo_done, 4 * (u - 1))
                dst = raw[:, u % 2, 0:KT * SMALL].rearrange("p (k n) -> p k n", k=KT) if u == U_SMALL \
                    else raw[:, u % 2, :].rearrange("p (k n) -> p k n", k=8)
                sp.dma_start(dst, unit_source(u)).then_inc(raw_landed[u % 2], 16)

            def first_piece(cc, t):
                s, sec = divmod(t, 2)
                need(sp, first_used, 8 * cc + t - 3)
                col = D * sec + 512 * cc
                sp.dma_start(first[t % 4][:].rearrange("p (k n) -> p k n", k=4),
                             ada_v[:, 4 * s:4 * s + 4, col:col + 512]).then_inc(first_landed[t % 4], 16)

            sp.dma_start(con[:], consts).then_inc(const_landed, 16)
            for s in range(2):
                sp.dma_start(x_nat[:, s, :], x[P * s:P * s + P, :]).then_inc(x_landed[s], 16)
            for t in range(4):
                first_piece(0, t)
            for s in range(2):
                sp.wait_ge(x_turned, 4 * s + 4)
                sp.wait_ge(x_squared, s + 1)
                sp.dma_start(x_nat[:, s, :], x[P * (s + 2):P * (s + 3), :]).then_inc(x_landed[s], 16)
            for t in range(4, 8):
                first_piece(0, t)
            load_unit(0)
            for cc in range(1, 4):
                for t in range(8):
                    first_piece(cc, t)
                    if cc == 1 and t == 0:
                        sp.wait_ge(x_turned, 16)
                        sp.wait_ge(x_squared, 4)
                        load_unit(1)
                    if cc == 2 and t == 4:
                        load_unit(2)
            for u in range(3, U_MLP):
                load_unit(u)
                for q in range(4 * (u - 2), 4 * (u - 1)):
                    slot(q)
                after_unit(u - 2)
            with sp.Fori(0, STEPS) as c:
                for m in range(PER_C):
                    u = U_MLP + m
                    sp.wait_ge(lo_done, 4 * (u - 1) + 4 * PER_C * c)
                    if m < 4:
                        a, hf = divmod(m, 2)
                        src = w1_v[:, 8 * hf:8 * hf + 8, bass.ds(1024 * c + 512 * a, 512)]
                    else:
                        src = w2_v[:, bass.ds(8 * c, 8), 512 * (m - 4):512 * (m - 3)]
                    sp.dma_start(raw[:, u % 2, :].rearrange("p (k n) -> p k n", k=8),
                                 src).then_inc(raw_landed[u % 2], 16)

        @block.scalar
        def _(act):
            def split_hi(u, j, trip=0):
                need(act, chunk_used, 4 * (u - 1) + j + 1 + 4 * PER_C * trip)
                if j == 0:
                    act.wait_ge(raw_landed[u % 2], 16 * (u // 2 + 1) + 16 * (PER_C // 2) * trip)
                act.activation(split_chunk(w_hi, u, j), raw_chunk(u, j), ACT.Copy).then_inc(hi_done, 1)

            def h_high(kt):
                act.wait_ge(t_ready, kt + 1)
                act.activation(h[:, kt, HI, :], tmp1[:, kt % 2, :], ACT.Identity,
                               bias=mod[:, kt:kt + 1]).then_inc(h_hi, 1)

            def softmax_exp(hd):
                act.wait_ge(logits_ready, hd + 1)
                for i in range(NB):
                    at_ = MASK_AT[i]
                    act.activation(prob[:, at_:at_ + span(i)], prob[:, at_:at_ + span(i)], ACT.Exp,
                                   bias=mx[:, 4 + i:5 + i], accum_out=sums[:, i:i + 1]).then_inc(exp_done, 1)

            def take_pT(hd):
                for kb in TURN_ORDER:
                    (bank, col), width = TURN_AT[kb], L - P * kb
                    act.wait_ge(p_turned, 3 * hd + bank + 1)
                    act.activation(pT[:, PT_AT[kb]:PT_AT[kb] + width], pa[:, bank, col:col + width],
                                   ACT.Copy).then_inc(pT_ready, 1)

            def gate_exp(g, tb):
                use = 12 * g + tb
                act.wait_ge(proj_free, 12 + 16 * g + tb + 1)
                need(act, ret_stored[use % 2], 16 * (use // 2))
                act.activation(stage[:, use % 2, :], nat[:, tb, :], ACT.Exp, scale=-1.0).then_inc(rg_exp, 1)

            def index_relu(n):
                i, hh = ITEMS[n]
                act.wait_ge(idx_done, n + 1)
                need(act, idx_added, n - 1)
                act.activation(stage[:, n % 2, 0:span(i)], pa[:, n % 4, 0:span(i)], ACT.Relu).then_inc(idx_taken, 1)

            def slot(q):
                if 20 <= q < 36:
                    for n in range(3 * (q - 20), 3 * (q - 20) + 3):
                        index_relu(n)
                if Q_LOOP <= q < Q_WO:
                    g, r = divmod(q - Q_LOOP, PER_GQ)
                    if r in (15, 16):
                        for tb in (0, 1):
                            gate_exp(g, 2 * (r - 15) + tb)
                    if r in LOGITS_AT:
                        softmax_exp(4 * g + LOGITS_AT.index(r))
                    if r in TURNS_AT:
                        take_pT(4 * g + TURNS_AT.index(r))
                if q == Q_WO - 1:
                    act.wait_ge(chunk_used, Q_WO)
                    act.wait_ge(y_ready, HEADS)
                    for t in range(HEADS):
                        act.activation(h[:, 8 + t, HI, :], y_raw[:, t, :], ACT.Copy).then_inc(yd_hi, 1)
                if Q_WO <= q < Q_WO + 16 and q % 2 == 0:
                    for b in range(2):
                        act.wait_ge(qk_turned, q - Q_WO + b + 1)
                        act.activation(qkT[:, b, :], pa[:, b, :], ACT.Copy).then_inc(qkT_ready, 1)
                if Q_WO + 3 <= q < Q_WO + 16 and q % 2:
                    retention_hi((q - Q_WO - 3) // 2)
                if q == Q_WO + 15:
                    retention_hi(7)

            def retention_hi(k):
                act.wait_ge(z_turned, k + 1)
                act.activation(h[:, k, HI, :], pa[:, 0, :], ACT.Copy,
                               scale=vec[:, V_RB + k:V_RB + k + 1]).then_inc(yr_hi, 1)

            act.dma_start(rows[0:96, 0, :], b_ada).then_inc(rows_landed, 16)
            act.dma_start(rows[0:V_ROWS, 1, :], vecs).then_inc(rows_landed, 16)
            act.wait_ge(rows_taken, 2)
            act.activation(csilu[:, 1, :], vec[:, V_C:V_C + KT], ACT.Exp, scale=-1.0).then_inc(silu_exp, 1)
            for tb in range(NB):
                act.wait_ge(x_landed[tb % 2], 16 * (tb // 2 + 1))
                need(act, x_squared, tb)
                act.activation(x_junk[:], x_nat[:, tb % 2, :], ACT.Square,
                               accum_out=ms[:, tb:tb + 1]).then_inc(x_squared, 1)
                for q in range(4):
                    act.wait_ge(x_turned, 4 * tb + q + 1)
                    act.activation(resid[:, 4 * q:4 * q + 4, P * tb:P * tb + P],
                                   pj[:, q, :].rearrange("p (k t) -> p k t", k=4), ACT.Copy).then_inc(x_taken, 1)
            act.wait_ge(x_taken, 16)
            act.dma_start(xT_dram, resid[:]).then_inc(xT_stored, 16)
            for q in range(4):
                split_hi(0, q)
            for cc in range(4):
                for m in range(4):
                    h_high(4 * cc + m)
                for q in (4 + 2 * cc, 5 + 2 * cc):
                    split_hi(q // 4, q % 4)
                    slot(q - 4)
            for q in range(12, Q_MLP):
                split_hi(q // 4, q % 4)
                slot(q - 4)
            for j in range(4):
                split_hi(U_MLP, j)
            for kt in range(KT):
                act.wait_ge(t2_ready, kt + 1)
                act.activation(h[:, kt, HI, :], relu[:, kt % 2, :], ACT.Identity,
                               bias=mod[:, 48 + kt:49 + kt]).then_inc(h2_hi, 1)

            def relu_tile(n, c):
                a, j = divmod(n, 4)
                act.wait_ge(chunk_used, 4 * (U_MLP + 2 * a + 1) + j + 1 + 32 * c)
                if isinstance(c, int) and c == 0 and n < 2:
                    act.wait_ge(h2_ready, KT)
                else:
                    act.wait_ge(sq_ready, 8 * c + n - 1)
                act.activation(relu[:, n % 2, :], (pa if a else pj)[:, j, :], ACT.Relu).then_inc(relu_done, 1)

            def mid_high(n, c):
                act.wait_ge(sq_ready, 8 * c + n + 1)
                act.activation(mid[:, n, HI, :], sq[:, n % 2, :], ACT.Copy).then_inc(mid_hi, 1)

            def output(t):
                act.wait_ge(out_turned, t + 1)
                need(act, out_stored[t % 2], 16 * (t // 2))
                act.activation(out_nat[:, t % 2, :], (pa if t // 4 % 2 else pj)[:, t % 4, :],
                               ACT.Copy).then_inc(out_ready, 1)
                act.wait_ge(out_ready, t + 1)
                act.dma_start(out[:, P * t:P * t + P].rearrange("(b p) d -> p b d", p=P),
                              out_nat[:, t % 2, :].rearrange("p (b d) -> p b d", b=NB)).then_inc(out_stored[t % 2], 16)

            def mlp_step(c, from_chunk, last=False):
                for qn in range(from_chunk, 32):
                    split_hi(U_MLP + qn // 4, qn % 4, c)
                    if 8 <= qn < 12 or 16 <= qn < 20:
                        n = qn - 8 if qn < 12 else qn - 12
                        relu_tile(n, c)
                        if n > 0:
                            mid_high(n - 1, c)
                        if n == 7:
                            mid_high(n, c)
                    if last and qn > 20:
                        output(qn - 21)
                if last:
                    for t in range(11, KT):
                        output(t)

            mlp_step(0, 4)
            with act.Fori(1, STEPS - 1) as c:
                mlp_step(c, 0)
            mlp_step(STEPS - 1, 0, last=True)
            for s in range(2):
                act.wait_ge(out_stored[s], 16 * KT // 2)

        @block.gpsimd
        def _(pool):
            def split_lo(u, j, trip=0):
                pool.wait_ge(hi_done, 4 * u + j + 1 + 4 * PER_C * trip)
                pool.tensor_tensor(split_chunk(w_lo, u, j), raw_chunk(u, j), split_chunk(w_hi, u, j).bitcast(F32),
                                   ALU.subtract).then_inc(lo_done, 1)

            powers = [0]

            def root(dst, src, width):
                powers[0] += 1
                pool.wait_ge(ms_ready, powers[0])
                pool.tensor_tensor(dst, src, half[:, 0:1].to_broadcast([P, width]), ALU.pow).then_inc(rstd_ready, 1)

            def slot(q):
                if q == 8:
                    root(ms[:, 0:8], ms[:, 0:8], 8)
                if q == 12:
                    root(ms[:, 0:NB], ms[:, 0:NB], NB)
                if Q_LOOP <= q < Q_WO and (q - Q_LOOP) % PER_GQ == 8:
                    root(ms[:], ms[:], 16)
                if Q_WO + 2 <= q < Q_WO + 16 and q % 2 == 0:
                    root(ms[:, 0:NB], ms[:, 0:NB], NB)
                if q == Q_WO + 15:
                    root(ms[:, 0:NB], ms[:, 0:NB], NB)

            pool.wait_ge(half_set, 1)
            root(ms[:, 0:NB], ms[:, 0:NB], NB)
            for q in range(Q_MLP):
                split_lo(q // 4, q % 4)
                slot(q - 4)
            for j in range(4):
                split_lo(U_MLP, j)
            root(ms[:, 0:NB], ms[:, 0:NB], NB)
            for j in range(4, 32):
                split_lo(U_MLP + j // 4, j % 4)
            with pool.Fori(1, STEPS) as c:
                for j in range(32):
                    split_lo(U_MLP + j // 4, j % 4, c)

        @block.vector
        def _(dve):
            own = Steps(dve, dve_step)
            dve.memset(half[:], -0.5).then_inc(half_set, 1)
            dve.wait_ge(rows_turned, 1)
            dve.tensor_copy(bias_cols[:], pa[:, 0, 0:96]).then_inc(rows_taken, 1)
            dve.wait_ge(rows_turned, 2)
            dve.tensor_copy(vec[:, 0:V_ROWS], pa[:, 1, 0:V_ROWS]).then_inc(rows_taken, 1)
            dve.wait_ge(silu_exp, 1)
            own.link(dve.tensor_scalar(csilu[:, 1, :], csilu[:, 1, :], 1.0, None, ALU.add))
            own.link(dve.reciprocal(csilu[:, 1, :], csilu[:, 1, :]))
            own.link(dve.tensor_tensor(csilu[:, 0, :], csilu[:, 1, :], vec[:, V_C:V_C + KT], ALU.mult))

            def multiply(dst, src, kts, is_first):
                for n, kt in enumerate(kts):
                    c_col = csilu[:, 0, kt:kt + 1]
                    if is_first and n == 0:
                        last = dve.tensor_scalar(dst, src(n), c_col, None, ALU.mult)
                    else:
                        own.wait()
                        last = dve.scalar_tensor_tensor(dst, src(n), c_col, dst, ALU.mult, ALU.add)
                    if n < len(kts) - 1:
                        own.step(last)
                return last

            def take_mod(n, bank, col):
                dve.wait_ge(mod_summed, n + 1)
                dve.tensor_tensor(mod[:, col:col + 4], pa[:, 3, bank:bank + 4], bias_cols[:, col:col + 4],
                                  ALU.add).then_inc(mod_taken, 1)

            def first_accs(cc):
                for s in range(4):
                    for sec in range(2):
                        dve.wait_ge(first_landed[(2 * s + sec) % 4], 16 * (2 * cc + s // 2 + 1))
                    for i in range(4):
                        for sec in range(2):
                            src = first[(2 * s + sec) % 4][:, 512 * i:512 * i + 512]
                            c_col, dst = csilu[:, 0, 4 * s + i:4 * s + i + 1], acc[:, sec, :]
                            if s == 0 and i == 0:
                                last = dve.tensor_scalar(dst, src, c_col, None, ALU.mult)
                            else:
                                if i > 0:
                                    dve.wait_ge(dve_step, own.n if (i == 3 and sec == 1) else own.n - 1)
                                else:
                                    dve.wait_ge(first_used, 8 * cc + 2 * s - 1 + sec)
                                last = dve.scalar_tensor_tensor(dst, src, c_col, dst, ALU.mult, ALU.add)
                            if i < 3:
                                own.step(last)
                            else:
                                last.then_inc(first_used, 1)

            def spread(stat, diag, ready_count):
                dve.wait_ge(rstd_ready, ready_count)
                for tb in range(NB):
                    dve.tensor_scalar(diag[:, tb, :], ident, stat[:, tb:tb + 1], None, ALU.mult).then_inc(diag_ready, 1)

            def fold(kt0, which, scale_col, norm_row, count):
                own.link(dve.scalar_tensor_tensor(gain[:, which, kt0:kt0 + count],
                                                  mod[:, scale_col + kt0:scale_col + kt0 + count], 1.0,
                                                  vec[:, norm_row + kt0:norm_row + kt0 + count], ALU.add, ALU.mult))

            def modulate(kt, which, src, rstd, tmp, shift_col, ready, hi_sem, done, go):
                if go == 0:
                    need(dve, done, kt - 1)
                    dve.scalar_tensor_tensor(tmp[:, kt % 2, :], src[:, kt, :], gain[:, which, kt:kt + 1], rstd,
                                             ALU.mult, ALU.mult).then_inc(ready, 1)
                else:
                    dve.wait_ge(hi_sem, kt + 1)
                    dve.scalar_tensor_tensor(h[:, kt, LO, :], tmp[:, kt % 2, :], mod[:, shift_col + kt:shift_col + kt + 1],
                                             h[:, kt, HI, :].bitcast(F32), ALU.add, ALU.subtract).then_inc(done, 1)

            for cc in range(4):
                first_accs(cc)
                if cc == 0:
                    dve.wait_ge(x_squared, NB)
                    dve.tensor_scalar(ms[:, 0:NB], ms[:, 0:NB], 1.0 / D, EPS, ALU.mult, ALU.add).then_inc(ms_ready, 1)
                dve.wait_ge(mod_summed, 2 * cc + 2)
                for sec in range(2):
                    take_mod(2 * cc + sec, 4 * sec, KT * sec + 4 * cc)
                dve.wait_ge(mod_taken, 2 * cc + 2)
                fold(4 * cc, 0, KT, V_N1, 4)
                if cc == 0:
                    spread(ms, diag1, 1)
                    dve.wait_ge(rstd_spread, 1)
                    own.link(dve.tensor_copy(rstd1[:], pa[:, 2, :]))
                    dve.wait_ge(x_taken, 16)
                for m in range(5):
                    kt = 4 * cc + m
                    if m < 4:
                        modulate(kt, 0, resid, rstd1[:], tmp1, 0, t_ready, h_hi, h_ready, 0)
                    if m > 0:
                        modulate(kt - 1, 0, resid, rstd1[:], tmp1, 0, t_ready, h_hi, h_ready, 1)

            def bank_ready(u_last, ni, b):
                if ni is not None and b < 3:
                    dve.wait_ge(proj_done, 3 * ni + b + 1)
                else:
                    dve.wait_ge(chunk_used, 4 * u_last + (b if ni is None else 3) + 1)

            def mean_square(src, n, width):
                places = L // width
                for i in range(n):
                    if i % places == 0:
                        own.wait()
                    at_ = width * (i % places)
                    own.step(dve.tensor_tensor_reduce(junk[:, at_:at_ + width], src(i), src(i), 1.0, 0.0, ALU.mult, ALU.add,
                                                      ms[:, i:i + 1]))
                own.wait()
                dve.tensor_scalar(ms[:, 0:n], ms[:, 0:n], 1.0 / width, EPS, ALU.mult, ALU.add).then_inc(ms_ready, 1)

            def take_small():
                for tb in range(NB):
                    dve.wait_ge(chunk_used, 4 * U_SMALL + 4)
                    own.step(dve.tensor_copy(ik_nat[:, tb, :], pj[:, tb, 0:IDX_DIM]))
                    dve.tensor_scalar(w_idx[:, tb, :], pj[:, tb, IDX_DIM:SMALL], (IDX_HEADS * IDX_DIM) ** -0.5, None,
                                      ALU.mult).then_inc(proj_free, 1)
                own.wait()
                dve.wait_ge(k_ready, 8)
                mean_square(lambda tb: ik_nat[:, tb, :], NB, IDX_DIM)

            def scale_small():
                dve.wait_ge(rstd_ready, 3)
                for tb in range(NB):
                    for twice in range(2):
                        dve.tensor_scalar(ik2[:, tb, twice, :], ik_nat[:, tb, :], ms[:, tb:tb + 1], None,
                                          ALU.mult).then_inc(ik_ready, 1)

            def take_kv():
                dve.wait_ge(xT_stored, 16)
                for tb in range(NB):
                    bank_ready(U_DKV + 1, 0, tb)
                    own.step(dve.tensor_copy(k_nat[:, tb, :], pj[:, tb, 0:KV * P]))
                    dve.tensor_copy(v_nat[:, tb, :], pj[:, tb, KV * P:]).then_inc(proj_free, 1)
                own.wait()
                mean_square(lambda i: k_nat[:, i // 2, P * (i % 2):P * (i % 2) + P], 8, P)

            def scale_k():
                dve.wait_ge(rstd_ready, 2)
                for i in range(8):
                    k_i = k_nat[:, i // 2, P * (i % 2):P * (i % 2) + P]
                    dve.tensor_scalar(k_i, k_i, ms[:, i:i + 1], None, ALU.mult).then_inc(k_ready, 1)

            def take_kT():
                for g in range(KV):
                    dve.wait_ge(k_turned, g + 1)
                    dve.tensor_scalar(kT[:, g, :], pa[:, 1 + g, :], vec[:, V_KG:V_KG + 1], None,
                                      ALU.mult).then_inc(kT_ready, 1)

            def take_ikT():
                dve.wait_ge(ik_turned, 1)
                dve.tensor_scalar(ikT[:], pa[:, 0, :], vec[:, V_IG:V_IG + 1], None, ALU.mult).then_inc(ikT_ready, 1)

            def take_iq(part):
                for b in range(4):
                    bank_ready(U_IQ + 2 * part + 1, None, b)
                    dve.tensor_copy(iqT[:, 4 * part + b, :], pj[:, b, :]).then_inc(iq_ready, 1)

            def index_item(n):
                i, hh = ITEMS[n]
                dst = score[:, SCORE_AT[i]:SCORE_AT[i] + span(i)]
                src, w_col = stage[:, n % 2, 0:span(i)], w_idx[:, i, hh:hh + 1]
                dve.wait_ge(idx_taken, n + 1)
                if hh == 0:
                    dve.tensor_scalar(dst, src, w_col, None, ALU.mult).then_inc(idx_added, 1)
                else:
                    dve.wait_ge(idx_added, n)
                    dve.scalar_tensor_tensor(dst, src, w_col, dst, ALU.mult, ALU.add).then_inc(idx_added, 1)

            def topk_round(n):
                i, k = 1 + n // (TOPK // 8), n % (TOPK // 8)
                s_i = score[:, SCORE_AT[i]:SCORE_AT[i] + span(i)]
                if k == 0:
                    dve.wait_ge(idx_added, 24 + 8 * i)
                    own.link(dve.tensor_tensor(s_i[:, span(i) - P:], s_i[:, span(i) - P:], neg, ALU.add))
                own.link(dve.max(m8[:], s_i))
                own.link(dve.match_replace(s_i, m8[:], s_i, TAKEN))
                if k == TOPK // 8 - 1:
                    own.link(dve.tensor_scalar(masks[:, MASK_AT[i]:MASK_AT[i] + span(i)], s_i, 0.5 * (TAKEN + DROP),
                                               DROP, ALU.is_gt, ALU.mult))

            def take_q(g):
                need(dve, v_stored, 16 * g)
                for tb in range(NB):
                    bank_ready(U_LOOP + PER_G * g + 1, 1 + 5 * g, tb)
                    dve.tensor_copy(nat[:, tb, :], pj[:, tb, :]).then_inc(proj_free, 1)
                dve.wait_ge(proj_free, 8 + 16 * g + 4)
                mean_square(lambda i: nat[:, i // 4, P * (i % 4):P * (i % 4) + P], 16, P)

            def scale_q(g, blocks):
                dve.wait_ge(rstd_ready, 4 + g)
                for tb in blocks:
                    n3 = nat[:, tb, :].rearrange("p (h d) -> p h d", h=4)
                    dve.tensor_tensor(n3, n3, ms[:, 4 * tb:4 * tb + 4].unsqueeze(2).to_broadcast([P, 4, P]),
                                      ALU.mult).then_inc(q_ready, 1)

            def take_qT(g):
                for j in range(PER_KV):
                    dve.wait_ge(q_turned, 4 * g + j + 1)
                    dve.tensor_scalar(qT[:, j, :], pa[:, j, :], vec[:, V_QG:V_QG + 1], float(P) ** -0.5, ALU.mult,
                                      ALU.mult).then_inc(qT_ready, 1)

            def take_gate(g):
                for tb in range(NB):
                    bank_ready(U_LOOP + PER_G * g + 3, 2 + 5 * g, tb)
                    dve.tensor_copy(nat[:, tb, :], pj[:, tb, :]).then_inc(proj_free, 1)

            def silu_gate(g, tb):
                use = 12 * g + tb
                s_ = stage[:, use % 2, :]
                dve.wait_ge(rg_exp, 4 * g + tb + 1)
                own.link(dve.tensor_scalar(s_, s_, 1.0, None, ALU.add))
                own.link(dve.reciprocal(s_, s_))
                dve.tensor_tensor(s_, s_, nat[:, tb, :], ALU.mult).then_inc(stage_ready, 1)

            def take_rotated(g, gr):
                dec = C_QDEC if gr == GR_RQ else C_KDEC
                for tb in range(NB):
                    use = 12 * g + 4 * (gr - 1) + tb
                    x3 = pj[:, tb, :].rearrange("p (h d two) -> p h d two", h=4, two=2)
                    s3 = stage[:, use % 2, :].rearrange("p (h d two) -> p h d two", h=4, two=2)
                    cos = con[:, C_COS + 64 * tb:C_COS + 64 * tb + 64].unsqueeze(1).to_broadcast([P, 4, 64])
                    sin = con[:, C_SIN + 64 * tb:C_SIN + 64 * tb + 64].unsqueeze(1).to_broadcast([P, 4, 64])
                    r0 = rot[:, 0, :].rearrange("p (h d) -> p h d", h=4)
                    r1 = rot[:, 1, :].rearrange("p (h d) -> p h d", h=4)
                    bank_ready(U_LOOP + PER_G * g + 2 * gr + 1, 1 + gr + 5 * g, tb)
                    own.step(dve.tensor_tensor(r0, x3[:, :, :, 0], cos, ALU.mult))
                    own.link(dve.tensor_tensor(r1, x3[:, :, :, 1], sin, ALU.mult))
                    need(dve, ret_stored[use % 2], 16 * (use // 2))
                    own.step(dve.tensor_tensor(s3[:, :, :, 0], r0, r1, ALU.subtract))
                    own.wait()
                    own.step(dve.tensor_tensor(r0, x3[:, :, :, 0], sin, ALU.mult))
                    dve.tensor_tensor(r1, x3[:, :, :, 1], cos, ALU.mult).then_inc(proj_free, 1)
                    own.wait()
                    dve.wait_ge(proj_free, 8 + 16 * g + 4 * gr + tb + 1)
                    own.link(dve.tensor_tensor(s3[:, :, :, 1], r0, r1, ALU.add))
                    sh = stage[:, use % 2, :].rearrange("p (h d) -> p h d", h=4)
                    d_ = con[:, dec + 8 * tb + 4 * g:dec + 8 * tb + 4 * g + 4].unsqueeze(2).to_broadcast([P, 4, P])
                    dve.tensor_tensor(sh, sh, d_, ALU.mult).then_inc(stage_ready, 1)

            def take_v(g):
                for tb in range(NB):
                    bank_ready(U_LOOP + PER_G * g + 9, 5 + 5 * g, tb)
                    dve.tensor_copy(nat[:, tb, :], pj[:, tb, :]).then_inc(v_taken, 1)

            def masked_logits(hd):
                for i in (0, 2, 1, 3):
                    bank, col = LOGIT_AT[i]
                    dve.wait_ge(logits_done, 3 * hd + bank + 1)
                    own.step(dve.tensor_tensor_reduce(
                        prob[:, MASK_AT[i]:MASK_AT[i] + span(i)], pa[:, bank, col:col + span(i)],
                        masks[:, MASK_AT[i]:MASK_AT[i] + span(i)], 1.0, -3.0e38, ALU.add, ALU.max, mx[:, i:i + 1]))
                own.wait()
                dve.tensor_scalar(mx[:, 4:8], mx[:, 0:4], -1.0, None, ALU.mult).then_inc(logits_ready, 1)

            def normalise(hd):
                dve.wait_ge(exp_done, 4 * hd + 4)
                own.link(dve.reciprocal(sums[:, 4:8], sums[:, 0:4]))
                for i in range(NB):
                    p_i = prob[:, MASK_AT[i]:MASK_AT[i] + span(i)]
                    dve.tensor_scalar(p_i, p_i, sums[:, 4 + i:5 + i], None, ALU.mult).then_inc(p_ready, 1)

            def take_y(hd):
                dve.wait_ge(pv_done, hd + 1)
                dve.tensor_scalar(y_raw[:, hd, :], pa[:, 3, :], vec[:, V_DB + hd:V_DB + hd + 1], None,
                                  ALU.mult).then_inc(y_ready, 1)

            def later_piece(t):
                n, k = divmod(t, 8)
                dve.wait_ge(ada_landed[t % 2], 16 * (t // 2 + 1))
                if k > 0:
                    dve.wait_ge(ada_used, t)
                multiply(acc[:, n % 2, :], lambda i, t=t: ada[:, t % 2, 512 * i:512 * i + 512],
                         (2 * k, 2 * k + 1), k == 0).then_inc(ada_used, 1)

            rounds_done = 0
            for q in range(Q_WO):
                if q == 7:
                    take_kv()
                if q == 12:
                    scale_k()
                    take_small()
                if q == 13:
                    take_kT()
                if q == 14:
                    scale_small()
                if q == 16:
                    take_ikT()
                if q == 19:
                    take_iq(0)
                if q == 27:
                    take_iq(1)
                if 20 <= q < 36:
                    for n in range(3 * (q - 20), 3 * (q - 20) + 3):
                        index_item(n)
                if q >= Q_LOOP:
                    g, r = divmod(q - Q_LOOP, PER_GQ)
                    if r == 7:
                        take_q(g)
                    if r in (9, 10):
                        scale_q(g, (0, 1) if r == 9 else (2, 3))
                    if r == Q_TURN_AT:
                        take_qT(g)
                    if r == 15:
                        take_gate(g)
                    if r in (16, 17):
                        for tb in (0, 1):
                            silu_gate(g, 2 * (r - 16) + tb)
                    if r == 18:
                        own.step(dve.tensor_copy(v_cur[:], v_nat[:, :, P * g:P * g + P]))
                        if g == 0:
                            own.step(dve.tensor_copy(masks[:, 0:P], neg))
                        own.wait()
                    if r in (23, 31):
                        take_rotated(g, GR_RQ if r == 23 else GR_RK)
                    if r == 39:
                        take_v(g)
                    if r in OUTS_AT:
                        take_y(4 * g + OUTS_AT.index(r))
                    if r in LOGITS_AT:
                        masked_logits(4 * g + LOGITS_AT.index(r))
                    if r - 1 in LOGITS_AT:
                        normalise(4 * g + LOGITS_AT.index(r - 1))
                if Q_TOPK <= q < Q_TOPK + len(ROUNDS):
                    for _ in range(ROUNDS[q - Q_TOPK]):
                        topk_round(rounds_done)
                        rounds_done += 1
                if q >= Q_ADA + 4 and (q - Q_ADA) % 4 == 0:
                    n = (q - Q_ADA) // 4 - 1
                    take_mod(8 + n, 0, 2 * KT + 4 * n)
                if q >= Q_ADA:
                    for t in (2 * (q - Q_ADA), 2 * (q - Q_ADA) + 1):
                        later_piece(t)
            take_mod(8 + ADA_ACCS - 1, 0, 2 * KT + 4 * (ADA_ACCS - 1))
            dve.wait_ge(mod_taken, 8 + ADA_ACCS)
            fold(0, 1, 4 * KT, V_N2, KT)

            for t in range(HEADS):
                dve.wait_ge(yd_hi, t + 1)
                dve.tensor_tensor(h[:, 8 + t, LO, :], y_raw[:, t, :], h[:, 8 + t, HI, :].bitcast(F32),
                                  ALU.subtract).then_inc(yd_ready, 1)

            def add_out(v, last):
                t = v % KT
                dve.wait_ge(chunk_used, 4 * U_WO + v + 1)
                if v == 0:
                    dve.wait_ge(resid_landed, 16)
                if last:
                    dve.wait_ge(added, v - KT + 1)
                dve.scalar_tensor_tensor(resid[:, t, :], pj[:, t % 4, :], mod[:, 2 * KT + t:2 * KT + t + 1],
                                         resid[:, t, :], ALU.mult, ALU.add).then_inc(added, 1)
                if last:
                    dve.wait_ge(added, v + 1)
                    if t == 0:
                        own.link(dve.tensor_tensor(ss[:], resid[:, t, :], resid[:, t, :], ALU.mult))
                    else:
                        own.link(dve.tensor_tensor(sq[:, 0, :], resid[:, t, :], resid[:, t, :], ALU.mult))
                        if t < KT - 1:
                            own.link(dve.tensor_tensor(ss[:], ss[:], sq[:, 0, :], ALU.add))
                        else:
                            dve.tensor_tensor(ss[:], ss[:], sq[:, 0, :], ALU.add).then_inc(ss_ready, 1)

            def ret_state(k):
                dve.wait_ge(state_done, k + 1)
                dve.tensor_copy(state[:].rearrange("p a b -> p (a b)"), pa[:, 2, 0:3 * P]).then_inc(state_ready, 1)

            def ret_inner(k):
                dve.wait_ge(inner_done, k + 1)
                dve.tensor_tensor(innerT[:].rearrange("p (n c) -> p n c", n=NB),
                                  pa[:, 3, :].rearrange("p (n c) -> p n c", n=NB),
                                  causal.unsqueeze(1).to_broadcast([P, NB, P]), ALU.mult).then_inc(inner_ready, 1)

            def ret_norm(k):
                dve.wait_ge(o_done, k + 1)
                for n in range(NB):
                    own.step(dve.bn_stats(bn6[:, n, :], pa[:, 3, P * n:P * n + P]))
                own.wait()
                for n in range(NB):
                    own.step(dve.bn_aggr(bn2[:, n, :], bn6[:, n, :]))
                own.wait()
                dve.tensor_scalar(ms[:, 0:NB], bn2[:, :, 1], EPS, None, ALU.add).then_inc(ms_ready, 1)
                dve.wait_ge(rstd_ready, 6 + k)
                for n in range(NB):
                    own.step(dve.tensor_scalar(z[:, n, :], pa[:, 3, P * n:P * n + P], bn2[:, n, 0:1], ms[:, n:n + 1],
                                               ALU.subtract, ALU.mult))
                own.wait()
                dve.tensor_tensor(z[:], z[:], ret[:, k % 3, 0], ALU.mult).then_inc(z_ready, 1)

            def ret_low(k):
                dve.wait_ge(yr_hi, k + 1)
                dve.scalar_tensor_tensor(h[:, k, LO, :], pa[:, 0, :], vec[:, V_RB + k:V_RB + k + 1],
                                         h[:, k, HI, :].bitcast(F32), ALU.mult, ALU.subtract).then_inc(yr_ready, 1)

            for r in range(16):
                add_out(r, False)
                k, odd = divmod(r, 2)
                if not odd:
                    if k > 0:
                        ret_norm(k - 1)
                    ret_state(k)
                else:
                    ret_inner(k)
                    if k > 0:
                        ret_low(k - 1)
            ret_norm(7)
            ret_low(7)
            for r in range(16, 32):
                add_out(r, True)

            dve.wait_ge(ss_summed, 1)
            dve.tensor_scalar(ms[:, 0:NB], pa[:, 2, 0:NB], 1.0 / D, EPS, ALU.mult, ALU.add).then_inc(ms_ready, 1)
            spread(ms, diag2, 14)
            dve.wait_ge(rstd_spread, 2)
            for kt in range(KT + 1):
                if kt < KT:
                    modulate(kt, 1, resid, pa[:, 2, :], relu, 3 * KT, t2_ready, h2_hi, h2_ready, 0)
                if kt > 0:
                    modulate(kt - 1, 1, resid, pa[:, 2, :], relu, 3 * KT, t2_ready, h2_hi, h2_ready, 1)

            def mlp_step(c, last):
                for n in range(9):
                    if n < 8:
                        dve.wait_ge(relu_done, 8 * c + n + 1)
                        if n > 1:
                            dve.wait_ge(mid_ready, 8 * c + n - 1)
                        dve.tensor_tensor(sq[:, n % 2, :], relu[:, n % 2, :], relu[:, n % 2, :],
                                          ALU.mult).then_inc(sq_ready, 1)
                    if n > 0:
                        dve.wait_ge(mid_hi, 8 * c + n)
                        dve.tensor_tensor(mid[:, n - 1, LO, :], sq[:, (n - 1) % 2, :],
                                          mid[:, n - 1, HI, :].bitcast(F32), ALU.subtract).then_inc(mid_ready, 1)
                dve.wait_ge(mid_ready, 8 * c + 8)
                dve.wait_ge(added, 32 + 16 * c)
                for t in range(KT):
                    v, j = divmod(t, 4)
                    dve.wait_ge(chunk_used, 4 * (U_MLP + 4 + v) + j + 1 + 32 * c)
                    dve.scalar_tensor_tensor(resid[:, t, :], (pa if v % 2 else pj)[:, j, :],
                                             mod[:, 5 * KT + t:5 * KT + t + 1], resid[:, t, :], ALU.mult,
                                             ALU.add).then_inc(added, 1)

            with dve.Fori(0, STEPS) as c:
                mlp_step(c, False)

        @block.tensor
        def _(pe):
            def product(dst, lhs, rhs, start, stop):
                for n, (a, b) in enumerate(PASSES):
                    last = pe.matmul(dst, lhs[a], rhs[b], start=start and n == 0, stop=stop and n == 2)
                return last

            def turn(dst, src):
                return pe.transpose(dst, src, ident)

            def tokens_chunk(u, j, k0, is_first, is_last, freed, count):
                pe.wait_ge(lo_done, 4 * u + j + 1)
                for tb in range(NB):
                    if is_first and j == 0 and freed is not None:
                        pe.wait_ge(freed, count + tb + 1)
                    for kk in range(2):
                        kt = k0 + 2 * j + kk
                        cols = slice(512 * kk, 512 * kk + 512)
                        last = product(pj[:, tb, :], [h[:, kt, s, P * tb:P * tb + P] for s in (HI, LO)],
                                       [w_hi[:, j, cols], w_lo[:, j, cols]],
                                       is_first and j == 0 and kk == 0, is_last and j == 3 and kk == 1)
                    if is_last and j == 3 and tb < 3:
                        last.then_inc(proj_done, 1)
                last.then_inc(chunk_used, 1)

            def features_chunk(q, src, k0, bank, start, stop, ready=None, count=0, trip=0):
                j = q % 4
                pe.wait_ge(lo_done, q + 1 + 32 * trip)
                for kk in range(8):
                    if ready is not None:
                        pe.wait_ge(ready, count + kk + 1)
                    last = product(bank, [w[:, j, P * kk:P * kk + P] for w in (w_hi, w_lo)],
                                   [src[:, k0 + kk, s, :] for s in (HI, LO)], start and kk == 0, stop and kk == 7)
                last.then_inc(chunk_used, 1)

            pe.wait_ge(const_landed, 16)
            pe.wait_ge(rows_landed, 32)
            pe.transpose(pa[:, 0, 0:96], rows[0:96, 0, :], con[0:96, C_ID:C_ID + 96]).then_inc(rows_turned, 1)
            pe.transpose(pa[:, 1, 0:V_ROWS], rows[0:V_ROWS, 1, :],
                         con[0:V_ROWS, C_ID:C_ID + V_ROWS]).then_inc(rows_turned, 1)
            for tb in range(NB):
                pe.wait_ge(x_landed[tb % 2], 16 * (tb // 2 + 1))
                for q in range(4):
                    need(pe, x_taken, 4 * tb + q - 3)
                    for m in range(4):
                        last = turn(pj[:, q, P * m:P * m + P], x_nat[:, tb % 2, P * (4 * q + m):P * (4 * q + m + 1)])
                    last.then_inc(x_turned, 1)
            def spread(diag, count):
                pe.wait_ge(diag_ready, count)
                for tb in range(NB):
                    last = pe.matmul(pa[:, 2, P * tb:P * tb + P], ones, diag[:, tb, :], start=True, stop=True)
                last.then_inc(rstd_spread, 1)

            def sum_mod(n, col, counted, value):
                pe.wait_ge(counted, value)
                for m in range(4):
                    last = pe.matmul(pa[:, 3, col + m:col + m + 1], acc[:, n % 2, P * m:P * m + P], ones[:, 0:1],
                                     start=True, stop=True)
                last.then_inc(mod_summed, 1)

            for cc in range(4):
                for sec in range(2):
                    need(pe, mod_taken, 2 * cc)
                    sum_mod(sec, 4 * sec, first_used, 8 * (cc + 1))
                if cc == 0:
                    spread(diag1, NB)
                    pe.wait_ge(x_taken, 16)
                for q in (2 * cc, 2 * cc + 1):
                    pe.wait_ge(h_ready, 2 * q + 2)
                    tokens_chunk(q // 4, q % 4, 8 * (q // 4), q < 4, q >= 4, None, 0)
            for j in range(4):
                pe.wait_ge(lo_done, 4 * U_SMALL + j + 1)
                for tb in range(NB):
                    if j == 0:
                        pe.wait_ge(proj_free, tb + 1)
                    for kk in range(4):
                        cols = slice(SMALL * kk, SMALL * kk + SMALL)
                        last = product(pj[:, tb, 0:SMALL],
                                       [h[:, 4 * j + kk, s, P * tb:P * tb + P] for s in (HI, LO)],
                                       [w_hi[:, j, cols], w_lo[:, j, cols]],
                                       j == 0 and kk == 0, j == 3 and kk == 3)
                last.then_inc(chunk_used, 1)

            def index_item(n):
                i, hh = ITEMS[n]
                rows = slice(IDX_DIM * (hh % 2), IDX_DIM * (hh % 2) + IDX_DIM)
                if n < 4:
                    pe.wait_ge(ikT_ready, 1)
                    pe.wait_ge(kT_ready, KV)
                    pe.wait_ge(mod_taken, 8)
                need(pe, idx_taken, n - 3)
                need(pe, iq_ready, 4 if n < 24 else 8)
                pe.matmul(pa[:, n % 4, 0:span(i)], iqT[rows, hh // 2, P * i:P * i + P], ikT[rows, 0:span(i)],
                          start=True, stop=True).then_inc(idx_done, 1)

            for q in range(4 * U_IQ, Q_LOOP):
                part, r = divmod(q - 4 * U_IQ, 8)
                hf, j = divmod(r, 4)
                if hf == 0:
                    if part == 0:
                        pe.wait_ge(proj_free, 4 + j + 1)
                    else:
                        pe.wait_ge(iq_ready, j + 1)
                features_chunk(q, h, 8 * hf, pj[:, j, :], hf == 0, hf == 1)
                if q == 13:
                    pe.wait_ge(k_ready, 8)
                    for g in range(KV):
                        for tb in range(NB):
                            last = turn(pa[:, 1 + g, P * tb:P * tb + P], k_nat[:, tb, P * g:P * g + P])
                        last.then_inc(k_turned, 1)
                if q == 16:
                    pe.wait_ge(ik_ready, 8)
                    for tb in range(NB):
                        last = turn(pa[:, 0, P * tb:P * tb + P], ik2[:, tb].rearrange("p a b -> p (a b)"))
                    last.then_inc(ik_turned, 1)
                if q >= 20:
                    for n in range(3 * (q - 20), 3 * (q - 20) + 3):
                        index_item(n)

            done = {"mods": 8, "heads": 0, "turns": 0}

            def bank3_free():
                pe.wait_ge(idx_taken, 48)
                pe.wait_ge(mod_taken, done["mods"])
                need(pe, y_ready, done["heads"])
                need(pe, qT_ready, done["turns"])

            def q_transposes(g):
                pe.wait_ge(q_ready, 4 * g + 4)
                bank3_free()
                for j in range(PER_KV):
                    for tb in range(NB):
                        last = turn(pa[:, j, P * tb:P * tb + P], nat[:, tb, P * j:P * j + P])
                    last.then_inc(q_turned, 1)
                done["turns"] += 4

            def head_logits(hd):
                g, j = divmod(hd, PER_KV)
                pe.wait_ge(qT_ready, 4 * g + 4)
                need(pe, pT_ready, 4 * hd)
                for i in (0, 2, 1, 3):
                    bank, col = LOGIT_AT[i]
                    last = pe.matmul(pa[:, bank, col:col + span(i)], qT[:, j, P * i:P * i + P], kT[:, g, 0:span(i)],
                                     start=True, stop=True)
                    if i != 0:
                        last.then_inc(logits_done, 1)

            def p_transposes(hd):
                pe.wait_ge(p_ready, 4 * hd + 4)
                need(pe, logits_ready, hd + 1)
                for kb in TURN_ORDER:
                    bank, col = TURN_AT[kb]
                    for i in range(kb, NB):
                        at_ = MASK_AT[i] + P * kb
                        last = turn(pa[:, bank, col + P * (i - kb):col + P * (i - kb + 1)], prob[:, at_:at_ + P])
                    if kb != 1:
                        last.then_inc(p_turned, 1)

            def head_out(hd):
                bank3_free()
                for kb in range(NB):
                    pe.wait_ge(pT_ready, 4 * hd + (1, 2, 4, 4)[kb])
                    width = L - P * kb
                    last = pe.matmul(pa[:, 3, P * kb:], v_cur[:, kb, :], pT[:, PT_AT[kb]:PT_AT[kb] + width],
                                     start=kb == 0, stop=kb == NB - 1, skip_group_check=True)
                last.then_inc(pv_done, 1)
                done["heads"] += 1

            def later_mod(n):
                bank3_free()
                sum_mod(n % 2, 0, ada_used, 8 * (n + 1))
                done["mods"] += 1

            for q in range(Q_LOOP, Q_WO):
                g, r = divmod(q - Q_LOOP, PER_GQ)
                group, hf = r // 8, r % 8 // 4
                if group == 0:
                    freed, count = (v_taken, 4 * g - 4) if g else (iq_ready, 4)
                else:
                    freed, count = proj_free, 8 + 16 * g + 4 * (group - 1)
                tokens_chunk(q // 4, q % 4, 8 * hf, hf == 0, hf == 1, freed, count)
                if q < 36:
                    for n in range(3 * (q - 20), 3 * (q - 20) + 3):
                        index_item(n)
                if r == Q_TURN_AT:
                    q_transposes(g)
                if q >= Q_ADA + 4 and (q - Q_ADA) % 4 == 0:
                    later_mod((q - Q_ADA) // 4 - 1)
                if r in TURNS_AT:
                    p_transposes(4 * g + TURNS_AT.index(r))
                if r in OUTS_AT:
                    head_out(4 * g + OUTS_AT.index(r))
                if r in LOGITS_AT:
                    head_logits(4 * g + LOGITS_AT.index(r))
            later_mod(ADA_ACCS - 1)

            def ret_turn(k):
                pe.wait_ge(ret_landed[k % 3], 64 * (k // 3 + 1))
                bank3_free()
                need(pe, yr_ready, k - 1)
                need(pe, state_ready, k)
                for b, kind in enumerate((1, 2)):
                    for n in range(NB):
                        last = turn(pa[:, b, P * n:P * n + P], ret[:, k % 3, kind, n, :])
                    last.then_inc(qk_turned, 1)
                for n in range(1, NB):
                    for e in range(n):
                        last = pe.matmul(pa[:, 2, P * (n - 1):P * n], ret[:, k % 3, 2, e, :], ret[:, k % 3, 3, e, :],
                                         start=e == 0, stop=e == n - 1)
                last.then_inc(state_done, 1)

            def ret_inner(k):
                pe.wait_ge(qkT_ready, 2 * k + 2)
                need(pe, z_ready, k)
                for n in range(NB):
                    last = pe.matmul(pa[:, 3, P * n:P * n + P], qkT[:, 1, P * n:P * n + P], qkT[:, 0, P * n:P * n + P],
                                     start=True, stop=True)
                last.then_inc(inner_done, 1)

            def ret_out(k):
                pe.wait_ge(inner_ready, k + 1)
                pe.wait_ge(state_ready, k + 1)
                for n in range(NB):
                    last = pe.matmul(pa[:, 3, P * n:P * n + P], innerT[:, P * n:P * n + P], ret[:, k % 3, 3, n, :],
                                     start=True, stop=n == 0)
                    if n > 0:
                        last = pe.matmul(pa[:, 3, P * n:P * n + P], qkT[:, 0, P * n:P * n + P], state[:, n - 1, :],
                                         start=False, stop=True)
                last.then_inc(o_done, 1)

            def ret_back(k):
                pe.wait_ge(z_ready, k + 1)
                pe.wait_ge(qkT_ready, 2 * min(k + 2, HEADS))
                for n in range(NB):
                    last = turn(pa[:, 0, P * n:P * n + P], z[:, n, :])
                last.then_inc(z_turned, 1)

            for r in range(32):
                half_, t = divmod(r, KT)
                if r >= 4:
                    pe.wait_ge(added, r - 3)
                if r < 4:
                    pe.wait_ge(v_taken, 4 + r + 1)
                features_chunk(4 * U_WO + r, h, 8 * (1 - half_), pj[:, t % 4, :], True, True,
                               (yd_ready if half_ == 0 else yr_ready) if t == 0 else None)
                if r < 16:
                    k, odd = divmod(r, 2)
                    if not odd:
                        if k > 0:
                            ret_out(k - 1)
                        need(pe, yr_ready, k - 1)
                        ret_turn(k)
                    else:
                        ret_inner(k)
                        if k > 0:
                            ret_back(k - 1)
                if r == 15:
                    ret_out(7)
                    ret_back(7)

            pe.wait_ge(ss_ready, 1)
            for tb in range(NB):
                last = pe.matmul(pa[:, 2, tb:tb + 1], ss[:, P * tb:P * tb + P], ones[:, 0:1], start=True, stop=True)
            last.then_inc(ss_summed, 1)
            spread(diag2, 2 * NB)

            def output(t):
                pe.wait_ge(added, 32 + KT * (STEPS - 1) + t + 1)
                for tb in range(NB):
                    last = turn((pa if t // 4 % 2 else pj)[:, t % 4, P * tb:P * tb + P], resid[:, t, P * tb:P * tb + P])
                last.then_inc(out_turned, 1)

            def mlp_step(c, final=False):
                for m in range(4):
                    a, hf = divmod(m, 2)
                    banks = pa if a else pj
                    for j in range(4):
                        if hf == 0:
                            pe.wait_ge(added, (24 if a == 0 else 28) + j + 1 + 16 * c)
                        features_chunk(4 * (U_MLP + m) + j, h, 8 * hf, banks[:, j, :], hf == 0, hf == 1,
                                       h2_ready if a == 0 and j == 0 else None, 8 * hf, c)
                for v in range(4):
                    banks = pa if v % 2 else pj
                    for j in range(4):
                        if v < 2:
                            pe.wait_ge(relu_done, 4 * v + j + 1 + 8 * c)
                        elif final:
                            pe.wait_ge(out_ready, 4 * (v - 2) + j + 1)
                        else:
                            pe.wait_ge(added, 32 + 4 * (v - 2) + j + 1 + 16 * c)
                        q = 4 * (U_MLP + 4 + v) + j
                        pe.wait_ge(lo_done, q + 1 + 32 * c)
                        for kk in range(8):
                            if v == 0 and j == 0:
                                pe.wait_ge(mid_ready, kk + 1 + 8 * c)
                            last = product(banks[:, j, :], [w[:, j, P * kk:P * kk + P] for w in (w_hi, w_lo)],
                                           [mid[:, kk, s, :] for s in (HI, LO)], kk == 0, kk == 7)
                        last.then_inc(chunk_used, 1)
                        if final and 4 * v + j > 0:
                            output(4 * v + j - 1)
                if final:
                    output(KT - 1)

            with pe.Fori(0, STEPS - 1) as c:
                mlp_step(c)
            mlp_step(STEPS - 1, final=True)


def _constants():
    c = np.zeros((P, C_END), np.float32)
    i = np.arange(P)
    c[:, C_ID:C_ID + P] = np.eye(P)
    c[:, C_CAUSAL:C_CAUSAL + P] = i[None, :] >= i[:, None]
    c[:, C_NEG:C_NEG + P] = np.where(i[None, :] <= i[:, None], 0.0, DROP)
    c[:, C_ONES:C_ONES + P] = 1.0
    angle = (1.0 / (np.float32(10000.0) ** np.linspace(0.0, 1.0, P // 2, dtype=np.float32))).astype(np.float32)
    for b in range(NB):
        theta = ((P * b + i).astype(np.float32)[:, None] * angle[None, :]).astype(np.float64)
        c[:, C_COS + 64 * b:C_COS + 64 * b + 64] = np.cos(theta)
        c[:, C_SIN + 64 * b:C_SIN + 64 * b + 64] = np.sin(theta)
        for hd in range(HEADS):
            log_gamma = math.log(1.0 - 2.0 ** (-5.0 - hd))
            c[:, C_QDEC + 8 * b + hd] = np.exp(log_gamma * (P * b + i))
            c[:, C_KDEC + 8 * b + hd] = np.exp(-log_gamma * (P * b + i)) * P ** -0.5
    return c


def kernel(x, c, w_ada, b_ada, norm1_g, norm2_g, w_in, ret_beta, q_norm_g, k_norm_g, idx_k_norm_g, dsa_beta,
           w_out, w_mlp1, w_mlp2):
    import concourse.bacc as _bacc
    from concourse.bass_utils import run_bass_kernel_spmd as _run

    flat = lambda a: np.ascontiguousarray(a).reshape(-1)
    arrays = {
        "x_in": np.ascontiguousarray(x).reshape(L, D),
        "vecs": np.concatenate([flat(a) for a in (c, norm1_g, norm2_g, ret_beta, dsa_beta, q_norm_g, k_norm_g,
                                                  idx_k_norm_g, idx_k_norm_g)]).reshape(V_ROWS, P),
        "b_ada_in": np.ascontiguousarray(b_ada).reshape(6 * KT, P),
        "consts": _constants(),
        "w_ada_in": np.ascontiguousarray(w_ada).reshape(D, 6 * D),
        "w_in_in": np.ascontiguousarray(w_in).reshape(D, -1),
        "w_out_in": np.ascontiguousarray(w_out).reshape(D, D),
        "w_mlp1_in": np.ascontiguousarray(w_mlp1).reshape(D, FF),
        "w_mlp2_in": np.ascontiguousarray(w_mlp2).reshape(FF, D),
    }
    nc = _bacc.Bacc("TRN2", target_bir_lowering=False, num_devices=1)
    args = [nc.dram_tensor(n, a.shape, mybir.dt.from_np(a.dtype), kind="ExternalInput").ap()
            for n, a in arrays.items()]
    out = nc.dram_tensor("out", (L, D), F32, kind="ExternalOutput").ap()
    build(nc, *args, out)
    r = _run(nc, [arrays], core_ids=[0])
    return r.results[0]["out"].reshape(1, L, D)
```

```python
import math

import numpy as np

import concourse.bass as bass
from concourse import mybir

F32 = mybir.dt.float32
F32R = mybir.dt.float32r
ALU = mybir.AluOpType
ACT = mybir.ActivationFunctionType

P = 128
L = 512
D = 2048
NB = L // P
KT = D // P
FF = 4 * D
HEADS = 8
KV = 2
PER_KV = HEADS // KV
HW = HEADS * P
IDX_HEADS, IDX_DIM = 16, 64
TOPK = L // 4
EPS = 1e-6
DROP = -3.0e38
TAKEN = -3.4e38
COL_RQ, COL_RK, COL_RV, COL_RG = 0, HW, 2 * HW, 3 * HW
COL_DQ = 4 * HW
COL_DK = COL_DQ + HW
COL_IQ = COL_DK + 2 * KV * P
COL_IK = COL_IQ + IDX_HEADS * IDX_DIM
SMALL = IDX_DIM + IDX_HEADS
HI, LO = 0, 1
PASSES = ((HI, HI), (HI, LO), (LO, HI))
V_C, V_N1, V_N2, V_RB, V_DB, V_QG, V_KG, V_IG, V_ROWS = 0, 16, 32, 48, 56, 64, 65, 66, 67
C_ID, C_CAUSAL, C_NEG, C_ONES, C_COS, C_SIN, C_QDEC, C_KDEC, C_END = (
    0, 128, 256, 384, 512, 768, 1024, 1056, 1088)

U_SMALL, U_IQ, U_LOOP, PER_G = 4, 5, 7, 10
IQ_EARLY = 3
EARLY = 4 * P + IQ_EARLY * P
LATE = P + SMALL
IQ_ORDER = (0, 1, 2, 7, 3, 4, 5, 6)
Q_SMALL, Q_IQ = 4 * U_SMALL, 4 * U_IQ
U_WO = U_LOOP + KV * PER_G
U_MLP = U_WO + 8
PER_C = 8
STEPS = FF // 1024
GR_DQ, GR_RG, GR_RQ, GR_RK, GR_RV = range(5)
Q_LOOP, Q_WO, Q_MLP = 4 * U_LOOP, 4 * U_WO, 4 * U_MLP
PER_GQ = 4 * PER_G
LOGITS_AT = (20, 24, 28, 32)
TURNS_AT = (23, 27, 30, 35)
OUTS_AT = (24, 28, 31, 36)
Q_TURN_AT = 11
Q_TOPK = 30
ROUNDS = (2, 2, 2, 2, 3, 4, 3, 3, 2, 3, 3, 3, 3, 3, 3, 3, 4)
Q_INDEX = 24
INDEX_ITEMS = (6, 6, 6, 6, 4, 4, 4, 4, 4, 4)
Q_ADA = 17
ADA_FREE = [q for q in range(Q_ADA, Q_WO) if q < Q_LOOP or (q - Q_LOOP) % PER_GQ not in (23, 24, 31, 32)]
ADA_ACCS = 16
ADA_SLOTS = [ADA_FREE[5 * n:5 * n + 5] for n in range(ADA_ACCS)]


def need(eng, sem, value):
    if isinstance(value, int) and value <= 0:
        return
    eng.wait_ge(sem, value)


class Steps:

    def __init__(self, eng, sem):
        self.eng, self.sem, self.n = eng, sem, 0

    def step(self, ins):
        ins.then_inc(self.sem, 1)
        self.n += 1

    def link(self, ins):
        self.step(ins)
        self.eng.wait_ge(self.sem, self.n)

    def wait(self):
        self.eng.wait_ge(self.sem, self.n)


def build(nc, x, vecs, b_ada, consts, w_ada, w_in, w_out, w_mlp1, w_mlp2, out):
    base = 16512

    def at(name, offset, shape, dt=F32):
        return nc.alloc_sbuf_tensor_at(name, shape, dt, offset=base + offset)

    h = at("h", 0, [P, KT, 2, L], F32R)
    raw = at("raw", 65536, [P, 2, 4096])
    w_hi = at("w_hi", 98304, [P, 4, 1024], F32R)
    w_lo = at("w_lo", 114688, [P, 4, 1024], F32R)
    XR = 131072
    resid = at("resid", XR, [P, KT, L])
    iqT = at("iqT", XR, [P, 8, L])
    y_raw = at("y_raw", XR, [P, HEADS, L])
    kT = at("kT", XR + 16384, [P, KV, L])
    v_nat = at("v_nat", XR + 20480, [P, NB, KV * P])
    qT = at("qT", XR + 24576, [P, PER_KV, L])
    RB = XR + 32768
    con = at("con", RB, [P, C_END])
    cursor = [RB + 4 * C_END]

    def small(name, *shape):
        t = at(name, cursor[0], [P, *shape])
        cursor[0] += -(-4 * math.prod(shape) // 32) * 32
        return t

    bias_cols = small("bias_cols", 6 * KT)
    vec = small("vec", V_ROWS + 1)
    mod = small("mod", 6 * KT)
    gain = small("gain", 2, KT)
    csilu = small("csilu", 2, KT)
    half = small("half", 8)
    mx = small("mx", 8)
    sums = small("sums", 8)
    ms = small("ms", 16)
    m8 = small("m8", 8)
    bn6 = small("bn6", NB, 6)
    bn2 = small("bn2", NB, 2)
    w_idx = small("w_idx", NB, IDX_HEADS)
    RC = RB + 4352 + 2048
    acc = at("acc", RC, [P, 2, L])
    ada = at("ada", RC + 4096, [P, 2, 1024])
    score = at("score", RC + 12288, [P, 1280])
    pT = at("pT", RC + 12288, [P, 1280])
    masks = at("masks", RC + 17408, [P, 1280])
    nat = at("nat", RC + 22528, [P, NB, L])
    prob = at("prob", RC + 22528, [P, 1280])
    k_nat = at("k_nat", RC + 22528, [P, NB, KV * P])
    ik_nat = at("ik_nat", RC + 26624, [P, NB, IDX_DIM])
    ik2 = at("ik2", RC + 27648, [P, NB, 2, IDX_DIM])
    ikT = at("ikT", RC + 30720, [P, L])
    v_cur = at("v_cur", RC + 32768, [P, NB, P])
    rstd1 = at("rstd1", RC + 32768, [P, L])
    x_junk = at("x_junk", RC + 12288, [P, D])
    rows = at("rows", RC + 20480, [P, 2, P])
    rot = at("rot", RC + 34816, [P, 2, 256])
    junk = at("junk", RC + 34816, [P, L])
    shift_acc = at("shift_acc", RC + 34816, [P, L])
    stage = at("stage", RC + 36864, [P, 2, L])
    tmp1 = at("tmp1", RC + 36864, [P, 2, L])
    diag1 = at("diag1", RC + 36864, [P, NB, P])
    x_nat = at("x_nat", 65536 + 16384, [P, 2, D])
    first = [at("ada_first0", 12 * 4096, [P, 2048]), at("ada_first1", 14 * 4096, [P, 2048]),
             at("ada_first2", RC + 4096, [P, 2048]), at("ada_first3", RC + 22528, [P, 2048])]
    ret = at("ret", RC, [P, 3, 4, NB, P])
    qkT = at("qkT", RC + 24576, [P, 2, L])
    innerT = at("innerT", RC + 28672, [P, L])
    state = at("state", RC + 30720, [P, 3, P])
    z = at("z", RC + 32768, [P, NB, P])
    gate_e = [at("gate_e0", RC + 34816, [P, L]), at("gate_e1", RC + 38912, [P, L])]
    ss = at("ss", RC, [P, L])
    diag2 = at("diag2", RC + 2048, [P, NB, P])
    mid = at("mid", RC, [P, 8, 2, L], F32R)
    relu = at("relu", RC + 32768, [P, 2, L])
    out_nat = at("out_nat", RC + 32768, [P, 2, L])
    sq = at("sq", RC + 36864, [P, 2, L])

    pj = nc.alloc_psum_tensor("pj", [P, 4, L], F32)
    pa = nc.alloc_psum_tensor("pa", [P, 4, L], F32)

    xT_dram = nc.dram_tensor("xT_dram", (P, KT, L), F32).ap()
    ret_dram = nc.dram_tensor("ret_dram", (4, L, HW), F32).ap()

    ident, causal = con[:, C_ID:C_ID + P], con[:, C_CAUSAL:C_CAUSAL + P]
    neg, ones = con[:, C_NEG:C_NEG + P], con[:, C_ONES:C_ONES + P]

    sem = nc.alloc_semaphore
    const_landed, rows_landed = sem("const_landed"), sem("rows_landed")
    x_landed = [sem("x_landed0"), sem("x_landed1")]
    first_landed = [sem(f"first_landed{i}") for i in range(4)]
    ada_landed = [sem("ada_landed0"), sem("ada_landed1")]
    raw_landed = [sem("raw_landed0"), sem("raw_landed1")]
    xT_stored, resid_landed = sem("xT_stored"), sem("resid_landed")
    ret_stored = [sem("ret_stored0"), sem("ret_stored1")]
    v_taken, nat_stored = sem("v_taken"), sem("nat_stored")
    ret_landed = [sem(f"ret_landed{i}") for i in range(3)]
    out_stored = [sem("out_stored0"), sem("out_stored1")]
    hi_done, lo_done, chunk_used = sem("hi_done"), sem("lo_done"), sem("chunk_used")
    proj_done, proj_free = sem("proj_done"), sem("proj_free")
    rows_turned, rows_taken = sem("rows_turned"), sem("rows_taken")
    half_set, silu_exp, silu_ready = sem("half_set"), sem("silu_exp"), sem("silu_ready")
    x_turned, x_taken = sem("x_turned"), sem("x_taken")
    x_squared = sem("x_squared")
    diag_ready, rstd_spread = sem("diag_ready"), sem("rstd_spread")
    ms_ready, rstd_ready = sem("ms_ready"), sem("rstd_ready")
    first_scaled = sem("first_scaled")
    scale_used = sem("scale_used")
    shift_used = [sem("shift_used_vector"), sem("shift_used_gpsimd")]
    ada_scaled = sem("ada_scaled")
    ada_used = [sem("ada_used_vector"), sem("ada_used_gpsimd")]
    mod_summed, mod_taken = sem("mod_summed"), sem("mod_taken")
    t_ready, h_hi, h_ready = sem("t_ready"), sem("h_hi"), sem("h_ready")
    ik_ready, ik_turned, ikT_ready = sem("ik_ready"), sem("ik_turned"), sem("ikT_ready")
    k_ready, k_turned, kT_ready = sem("k_ready"), sem("k_turned"), sem("kT_ready")
    iq_ready, idx_done, idx_taken = sem("iq_ready"), sem("idx_done"), sem("idx_taken")
    idx_added = sem("idx_added")
    q_ready, q_turned, qT_ready = sem("q_ready"), sem("q_turned"), sem("qT_ready")
    rg_exp, stage_ready = sem("rg_exp"), sem("stage_ready")
    logits_done, logits_ready = sem("logits_done"), sem("logits_ready")
    exp_done, p_ready, p_turned, pT_ready = sem("exp_done"), sem("p_ready"), sem("p_turned"), sem("pT_ready")
    pv_done, y_ready = sem("pv_done"), sem("y_ready")
    yd_hi, yd_ready = sem("yd_hi"), sem("yd_ready")
    qk_turned, qkT_ready = sem("qk_turned"), sem("qkT_ready")
    state_done, state_ready = sem("state_done"), sem("state_ready")
    inner_done, inner_ready = sem("inner_done"), sem("inner_ready")
    o_done, z_ready, z_turned = sem("o_done"), sem("z_ready"), sem("z_turned")
    yr_hi, yr_ready = sem("yr_hi"), sem("yr_ready")
    added = sem("added")
    ss_ready, ss_summed = sem("ss_ready"), sem("ss_summed")
    t2_ready, h2_hi, h2_ready = sem("t2_ready"), sem("h2_hi"), sem("h2_ready")
    relu_done, sq_ready, mid_hi, mid_ready = sem("relu_done"), sem("sq_ready"), sem("mid_hi"), sem("mid_ready")
    out_turned, out_ready = sem("out_turned"), sem("out_ready")
    dve_step, pool_step = sem("dve_step"), sem("pool_step")

    w_in_v = w_in.rearrange("(k p) n -> p k n", p=P)
    w_out_v = w_out.rearrange("(k p) n -> p k n", p=P)
    w1_v = w_mlp1.rearrange("(k p) n -> p k n", p=P)
    w2_v = w_mlp2.rearrange("(k p) n -> p k n", p=P)
    ada_v = w_ada.rearrange("(k p) n -> p k n", p=P)

    def unit_source(u):
        if u < U_SMALL:
            return w_in_v[:, 4 * u:4 * u + 4, COL_DK:COL_DK + EARLY]
        if u == U_SMALL:
            return w_in_v[:, :, COL_IK - P:COL_IK + SMALL]
        if u < U_LOOP:
            k, col = 8 * (u - U_IQ), COL_IQ + IQ_EARLY * P
        elif u < U_WO:
            g, m = divmod(u - U_LOOP, PER_G)
            first_col = {GR_DQ: COL_DQ, GR_RG: COL_RG, GR_RQ: COL_RQ, GR_RK: COL_RK, GR_RV: COL_RV}[m // 2]
            k, col = 8 * (m % 2), first_col + 512 * g
        else:
            half_, v = divmod(u - U_WO, 4)
            return w_out_v[:, 8 * (1 - half_):8 * (2 - half_), 512 * v:512 * v + 512]
        return w_in_v[:, k:k + 8, col:col + 512]

    def is_tiles(u):
        return U_IQ <= u < U_LOOP or u >= U_WO

    def raw_chunk(u, j):
        slot = raw[:, u % 2, :]
        if u <= U_SMALL:
            width = 4 * LATE if u == U_SMALL else EARLY
            return slot[:, width * j:width * j + width]
        if is_tiles(u):
            return slot.rearrange("p (k n) -> p k n", k=8)[:, :, P * j:P * j + P]
        return slot[:, 1024 * j:1024 * j + 1024]

    def split_chunk(w, u, j):
        if u <= U_SMALL:
            return w[:, j, 0:4 * LATE if u == U_SMALL else EARLY]
        if is_tiles(u):
            return w[:, j, :].rearrange("p (k n) -> p k n", k=8)
        return w[:, j, :]

    def span(i):
        return P * (i + 1)

    MASK_AT = [0, 128, 384, 768]
    SCORE_AT = [0, 0, 256, 640]
    LOGIT_AT = [(0, 0), (1, 0), (0, 128), (2, 0)]
    TURN_AT = [(0, 0), (1, 0), (2, 0), (1, 384)]
    PT_AT = [0, 512, 896, 1152]
    TURN_ORDER = (0, 1, 3, 2)

    ITEMS = [(i, 2 * t + m) for part in range(2) for i in (1, 2, 3)
             for t in IQ_ORDER[4 * part:4 * part + 4] for m in range(2)]

    def items_at(q):
        m = q - Q_INDEX
        return range(sum(INDEX_ITEMS[:m]), sum(INDEX_ITEMS[:m + 1])) if 0 <= m < len(INDEX_ITEMS) else ()

    def ada_pieces_at(q):
        return [(n, 2 * slots.index(q) + e) for n, slots in enumerate(ADA_SLOTS) if q in slots[:4] for e in range(2)]

    def ada_sum_at(q):
        return [n for n, slots in enumerate(ADA_SLOTS) if q == slots[4]]

    block = nc.Block()
    with block:

        @block.sync
        def _(sp):
            def ada_piece(n, k):
                piece, col = 8 * n + k, 2 * D + 512 * n
                if piece == 0:
                    sp.wait_ge(scale_used, 16)
                for used in ada_used:
                    need(sp, used, piece - 1)
                sp.dma_start(ada[:, piece % 2, :].rearrange("p (k n) -> p k n", k=2),
                             ada_v[:, 2 * k:2 * k + 2, col:col + 512]).then_inc(ada_landed[piece % 2], 16)

            def store(g, gr, tb):
                use = 8 * g + 4 * (gr - GR_RQ) + tb
                sp.wait_ge(stage_ready, use + 1)
                sp.dma_start(ret_dram[gr - 1, P * tb:P * tb + P, 512 * g:512 * g + 512],
                             stage[:, use % 2, :]).then_inc(ret_stored[use % 2], 16)

            def store_nat(kind, g, taken, count):
                sp.wait_ge(taken, count)
                sp.dma_start(ret_dram[kind, :, 512 * g:512 * g + 512].rearrange("(b p) n -> p b n", p=P),
                             nat[:]).then_inc(nat_stored, 16)

            def load_head(k):
                g = k // 4
                if k < 3:
                    sp.wait_ge(y_ready, HEADS)
                    sp.wait_ge(mod_taken, 8 + ADA_ACCS)
                else:
                    sp.wait_ge(z_ready, k - 2)
                for s in range(2):
                    sp.wait_ge(ret_stored[s], 64 * (g + 1))
                sp.wait_ge(nat_stored, 32 * (g + 1))
                for kind in range(4):
                    sp.dma_start(ret[:, k % 3, kind], ret_dram[kind, :, P * k:P * k + P]
                                 .rearrange("(b p) d -> p b d", p=P)).then_inc(ret_landed[k % 3], 16)

            def slot(q):
                if Q_LOOP <= q < Q_WO:
                    g, r = divmod(q - Q_LOOP, PER_GQ)
                    if r == 15:
                        store_nat(0, g, proj_free, 8 + 16 * g + 8)
                    if r in (23, 31):
                        for tb in range(NB):
                            store(g, GR_RQ if r == 23 else GR_RK, tb)
                    if r == 39:
                        store_nat(3, g, v_taken, 4 * g + 4)
                for n, k in ada_pieces_at(q + 1):
                    ada_piece(n, k)

            def after_unit(u):
                if u == U_WO - 1:
                    for k in range(3):
                        load_head(k)
                    sp.wait_ge(yd_ready, HEADS)
                    sp.wait_ge(xT_stored, 16)
                    sp.dma_start(resid[:], xT_dram).then_inc(resid_landed, 16)
                for k in {U_WO: (3,), U_WO + 1: (4, 5), U_WO + 2: (6, 7)}.get(u, ()):
                    load_head(k)

            def load_unit(u):
                need(sp, lo_done, 4 * (u - 1))
                rows, width = (4, EARLY) if u < U_SMALL else (KT, LATE) if u == U_SMALL else (8, 512)
                dst = raw[:, u % 2, 0:rows * width].rearrange("p (k n) -> p k n", k=rows)
                sp.dma_start(dst, unit_source(u)).then_inc(raw_landed[u % 2], 16)

            def first_piece(cc, t):
                s, sec = divmod(t, 2)
                for used in shift_used if sec else (scale_used,):
                    need(sp, used, 4 * cc + s - 1)
                col = D * (1 - sec) + 512 * cc
                sp.dma_start(first[t % 4][:].rearrange("p (k n) -> p k n", k=4),
                             ada_v[:, 4 * s:4 * s + 4, col:col + 512]).then_inc(first_landed[t % 4], 16)

            sp.dma_start(con[:], consts).then_inc(const_landed, 16)
            for s in range(2):
                sp.dma_start(x_nat[:, s, :], x[P * s:P * s + P, :]).then_inc(x_landed[s], 16)
            for t in range(4):
                first_piece(0, t)
            for s in range(2):
                sp.wait_ge(x_turned, 4 * s + 4)
                sp.wait_ge(x_squared, s + 1)
                sp.dma_start(x_nat[:, s, :], x[P * (s + 2):P * (s + 3), :]).then_inc(x_landed[s], 16)
            for t in range(4, 8):
                first_piece(0, t)
            load_unit(0)
            for cc in range(1, 4):
                for t in range(8):
                    if t == 4:
                        if cc == 1:
                            sp.wait_ge(x_turned, 16)
                            sp.wait_ge(x_squared, 4)
                        load_unit(cc)
                    first_piece(cc, t)
            load_unit(U_SMALL)
            sp.wait_ge(x_taken, 16)
            sp.dma_start(xT_dram, resid[:]).then_inc(xT_stored, 16)
            for u in range(U_IQ, U_MLP):
                load_unit(u)
                for q in range(4 * (u - 2), 4 * (u - 1)):
                    slot(q)
                after_unit(u - 2)
            with sp.Fori(0, STEPS) as c:
                for m in range(PER_C):
                    u = U_MLP + m
                    sp.wait_ge(lo_done, 4 * (u - 1) + 4 * PER_C * c)
                    if m < 4:
                        a, hf = divmod(m, 2)
                        src = w1_v[:, 8 * hf:8 * hf + 8, bass.ds(1024 * c + 512 * a, 512)]
                    else:
                        src = w2_v[:, bass.ds(8 * c, 8), 512 * (m - 4):512 * (m - 3)]
                    sp.dma_start(raw[:, u % 2, :].rearrange("p (k n) -> p k n", k=8),
                                 src).then_inc(raw_landed[u % 2], 16)

        @block.scalar
        def _(act):
            def split_hi(u, j, trip=0):
                need(act, chunk_used, 4 * (u - 1) + j + 1 + 4 * PER_C * trip)
                if j == 0:
                    act.wait_ge(raw_landed[u % 2], 16 * (u // 2 + 1) + 16 * (PER_C // 2) * trip)
                act.activation(split_chunk(w_hi, u, j), raw_chunk(u, j), ACT.Copy).then_inc(hi_done, 1)

            def scale_shift(cc, s):
                n = 4 * cc + s
                act.wait_ge(first_landed[1 + 2 * (n % 2)], 16 * (n // 2 + 1))
                for i in range(2):
                    tile = first[1 + 2 * (n % 2)][:, 512 * i:512 * i + 512]
                    act.activation(tile, tile, ACT.Copy, scale=csilu[:, 0, 4 * s + i:4 * s + i + 1]).then_inc(
                        first_scaled, 1)

            def h_high(kt):
                act.wait_ge(t_ready, kt + 1)
                act.activation(h[:, kt, HI, :], tmp1[:, kt % 2, :], ACT.Identity,
                               bias=mod[:, kt:kt + 1]).then_inc(h_hi, 1)

            def softmax_exp(hd):
                act.wait_ge(logits_ready, hd + 1)
                for i in range(NB):
                    at_ = MASK_AT[i]
                    act.activation(prob[:, at_:at_ + span(i)], prob[:, at_:at_ + span(i)], ACT.Exp,
                                   bias=mx[:, 4 + i:5 + i], accum_out=sums[:, i:i + 1]).then_inc(exp_done, 1)

            def take_pT(hd):
                for kb in TURN_ORDER:
                    (bank, col), width = TURN_AT[kb], L - P * kb
                    act.wait_ge(p_turned, 3 * hd + bank + 1)
                    act.activation(pT[:, PT_AT[kb]:PT_AT[kb] + width], pa[:, bank, col:col + width],
                                   ACT.Copy).then_inc(pT_ready, 1)

            def take_iq(tile, place, bank, q):
                act.wait_ge(chunk_used, q + 1)
                if place == 0:
                    act.wait_ge(xT_stored, 16)
                    act.wait_ge(h_ready, KT)
                act.activation(iqT[:, tile, :], bank, ACT.Copy).then_inc(iq_ready, 1)

            def take_group(g, group, done):
                for tb in range(NB):
                    if tb < 3:
                        act.wait_ge(proj_done, 3 * (1 + group + 5 * g) + tb + 1)
                    else:
                        act.wait_ge(chunk_used, Q_LOOP + PER_GQ * g + 8 * group + 8)
                    if tb == 0 and group == 0:
                        need(act, nat_stored, 32 * g)
                        act.wait_ge(ik_turned, 1)
                    if tb == 0 and group == 1:
                        act.wait_ge(q_turned, 4 * g + 4)
                    if tb == 0 and group == 4:
                        act.wait_ge(p_turned, 12 * g + 12)
                    act.activation(nat[:, tb, :], pj[:, tb, :], ACT.Copy).then_inc(done, 1)

            def before_split(q):
                if Q_LOOP <= q < Q_WO:
                    g, r = divmod(q - Q_LOOP, PER_GQ)
                    if r in (7, 15):
                        take_group(g, r // 8, proj_free)
                    if r == 39:
                        take_group(g, 4, v_taken)

            def scale_ada(n, k):
                piece = 8 * n + k
                act.wait_ge(ada_landed[piece % 2], 16 * (piece // 2 + 1))
                tile = ada[:, piece % 2, 512:1024]
                act.activation(tile, tile, ACT.Copy,
                               scale=csilu[:, 0, 2 * k + 1:2 * k + 2]).then_inc(ada_scaled, 1)

            def gate_exp(k):
                act.wait_ge(ret_landed[k % 3], 64 * (k // 3 + 1))
                need(act, z_ready, k - 1)
                act.activation(gate_e[k % 2][:], ret[:, k % 3, 0].rearrange("p b d -> p (b d)"), ACT.Exp,
                               scale=-1.0).then_inc(rg_exp, 1)

            def index_relu(n):
                i, hh = ITEMS[n]
                act.wait_ge(idx_done, n + 1)
                need(act, idx_added, n - 1)
                act.activation(stage[:, n % 2, 0:span(i)], pa[:, n % 4, 0:span(i)], ACT.Relu).then_inc(idx_taken, 1)

            def slot(q):
                if q < Q_TOPK:
                    for n, k in ada_pieces_at(q):
                        scale_ada(n, k)
                if q == Q_SMALL - 1:
                    for t in range(IQ_EARLY):
                        take_iq(t, t, pa[:, t, :], q)
                if q == Q_IQ - 1:
                    take_iq(IQ_ORDER[3], 3, pa[:, 3, :], q)
                if Q_IQ + 4 <= q < Q_LOOP:
                    j = q - Q_IQ - 4
                    take_iq(IQ_ORDER[4 + j], 4 + j, pj[:, j, :], q)
                for n in items_at(q):
                    index_relu(n)
                if Q_LOOP <= q < Q_WO:
                    g, r = divmod(q - Q_LOOP, PER_GQ)
                    if r in LOGITS_AT:
                        softmax_exp(4 * g + LOGITS_AT.index(r))
                    if r in TURNS_AT:
                        take_pT(4 * g + TURNS_AT.index(r))
                if q >= Q_TOPK:
                    for n, k in ada_pieces_at(q):
                        scale_ada(n, k)
                if q == Q_WO - 1:
                    act.wait_ge(chunk_used, Q_WO)
                    act.wait_ge(y_ready, HEADS)
                    for t in range(HEADS):
                        act.activation(h[:, 8 + t, HI, :], y_raw[:, t, :], ACT.Copy).then_inc(yd_hi, 1)
                    gate_exp(0)
                if Q_WO < q < Q_WO + 14 and q % 2:
                    gate_exp((q - Q_WO + 1) // 2)
                if Q_WO <= q < Q_WO + 16 and q % 2 == 0:
                    for b in range(2):
                        act.wait_ge(qk_turned, q - Q_WO + b + 1)
                        act.activation(qkT[:, b, :], pa[:, b, :], ACT.Copy).then_inc(qkT_ready, 1)
                if Q_WO + 3 <= q < Q_WO + 16 and q % 2:
                    retention_hi((q - Q_WO - 3) // 2)
                if q == Q_WO + 15:
                    retention_hi(7)

            def retention_hi(k):
                act.wait_ge(z_turned, k + 1)
                act.activation(h[:, k, HI, :], pa[:, 0, :], ACT.Copy,
                               scale=vec[:, V_RB + k:V_RB + k + 1]).then_inc(yr_hi, 1)

            act.dma_start(rows[0:96, 0, :], b_ada).then_inc(rows_landed, 16)
            act.dma_start(rows[0:V_ROWS, 1, :], vecs).then_inc(rows_landed, 16)
            act.wait_ge(rows_taken, 2)
            act.activation(csilu[:, 1, :], vec[:, V_C:V_C + KT], ACT.Exp, scale=-1.0).then_inc(silu_exp, 1)
            for tb in range(NB):
                act.wait_ge(x_landed[tb % 2], 16 * (tb // 2 + 1))
                need(act, x_squared, tb)
                act.activation(x_junk[:], x_nat[:, tb % 2, :], ACT.Square,
                               accum_out=ms[:, tb:tb + 1]).then_inc(x_squared, 1)
                for q in range(4):
                    act.wait_ge(x_turned, 4 * tb + q + 1)
                    act.activation(resid[:, 4 * q:4 * q + 4, P * tb:P * tb + P],
                                   pj[:, q, :].rearrange("p (k t) -> p k t", k=4), ACT.Copy).then_inc(x_taken, 1)
            act.wait_ge(silu_ready, 1)
            for cc in range(4):
                for s in range(4):
                    scale_shift(cc, s)
                    if cc > 0:
                        split_hi(cc, s)
                if cc == 0:
                    for j in range(4):
                        split_hi(0, j)
                for m in range(4):
                    h_high(4 * cc + m)
            for q in range(Q_SMALL, Q_MLP):
                before_split(q - 4)
                split_hi(q // 4, q % 4)
                slot(q - 4)
            for j in range(4):
                split_hi(U_MLP, j)
            for kt in range(KT):
                act.wait_ge(t2_ready, kt + 1)
                act.activation(h[:, kt, HI, :], relu[:, kt % 2, :], ACT.Identity,
                               bias=mod[:, 48 + kt:49 + kt]).then_inc(h2_hi, 1)

            def relu_tile(n, c):
                a, j = divmod(n, 4)
                act.wait_ge(chunk_used, 4 * (U_MLP + 2 * a + 1) + j + 1 + 32 * c)
                if isinstance(c, int) and c == 0 and n < 2:
                    act.wait_ge(h2_ready, KT)
                else:
                    act.wait_ge(sq_ready, 8 * c + n - 1)
                act.activation(relu[:, n % 2, :], (pa if a else pj)[:, j, :], ACT.Relu).then_inc(relu_done, 1)

            def mid_high(n, c):
                act.wait_ge(sq_ready, 8 * c + n + 1)
                act.activation(mid[:, n, HI, :], sq[:, n % 2, :], ACT.Copy).then_inc(mid_hi, 1)

            def output(t):
                act.wait_ge(out_turned, t + 1)
                need(act, out_stored[t % 2], 16 * (t // 2))
                act.activation(out_nat[:, t % 2, :], (pa if t // 4 % 2 else pj)[:, t % 4, :],
                               ACT.Copy).then_inc(out_ready, 1)
                act.wait_ge(out_ready, t + 1)
                act.dma_start(out[:, P * t:P * t + P].rearrange("(b p) d -> p b d", p=P),
                              out_nat[:, t % 2, :].rearrange("p (b d) -> p b d", b=NB)).then_inc(out_stored[t % 2], 16)

            def mlp_step(c, from_chunk, last=False):
                for qn in range(from_chunk, 32):
                    split_hi(U_MLP + qn // 4, qn % 4, c)
                    if 8 <= qn < 12 or 16 <= qn < 20:
                        n = qn - 8 if qn < 12 else qn - 12
                        relu_tile(n, c)
                        if n > 0:
                            mid_high(n - 1, c)
                        if n == 7:
                            mid_high(n, c)
                    if last and qn > 20:
                        output(qn - 21)
                if last:
                    for t in range(11, KT):
                        output(t)

            mlp_step(0, 4)
            with act.Fori(1, STEPS - 1) as c:
                mlp_step(c, 0)
            mlp_step(STEPS - 1, 0, last=True)
            for s in range(2):
                act.wait_ge(out_stored[s], 16 * KT // 2)

        @block.gpsimd
        def _(pool):
            def split_lo(u, j, trip=0):
                pool.wait_ge(hi_done, 4 * u + j + 1 + 4 * PER_C * trip)
                pool.tensor_tensor(split_chunk(w_lo, u, j), raw_chunk(u, j), split_chunk(w_hi, u, j).bitcast(F32),
                                   ALU.subtract).then_inc(lo_done, 1)

            powers, pool_steps = [0], [0]

            def root(dst, src, width):
                powers[0] += 1
                pool.wait_ge(ms_ready, powers[0])
                pool.tensor_tensor(dst, src, half[:, 0:1].to_broadcast([P, width]), ALU.pow).then_inc(rstd_ready, 1)

            def ada_piece(n, k):
                piece = 8 * n + k
                pool.wait_ge(ada_scaled, piece + 1)
                src = ada[:, piece % 2, 512:1024]
                if k == 0:
                    need(pool, mod_summed, 4 + n)
                    pool.tensor_copy(acc[:, 1, :], src).then_inc(ada_used[1], 1)
                else:
                    pool.wait_ge(ada_used[1], piece)
                    pool.tensor_tensor(acc[:, 1, :], acc[:, 1, :], src, ALU.add).then_inc(ada_used[1], 1)

            def slot(q):
                for n, k in ada_pieces_at(q):
                    ada_piece(n, k)
                if q == Q_SMALL:
                    root(ms[:, 0:8], ms[:, 0:8], 8)
                if q == Q_IQ:
                    root(ms[:, 0:NB], ms[:, 0:NB], NB)
                if Q_LOOP <= q < Q_WO and (q - Q_LOOP) % PER_GQ == 8:
                    root(ms[:], ms[:], 16)
                if Q_WO + 2 <= q < Q_WO + 16 and q % 2 == 0:
                    root(ms[:, 0:NB], ms[:, 0:NB], NB)
                if q == Q_WO + 15:
                    root(ms[:, 0:NB], ms[:, 0:NB], NB)

            def add_shift(cc, s):
                n = 4 * cc + s
                if s == 0:
                    need(pool, mod_summed, cc)
                tiles = first[1 + 2 * (n % 2)]
                pool.wait_ge(first_scaled, 2 * n + 2)
                if s == 0:
                    pool.tensor_tensor(acc[:, 1, :], tiles[:, 0:512], tiles[:, 512:1024],
                                       ALU.add).then_inc(shift_used[1], 1)
                else:
                    pool.wait_ge(shift_used[1], n)
                    pool.tensor_tensor(acc[:, 1, :], acc[:, 1, :], tiles[:, 0:512], ALU.add).then_inc(pool_step, 1)
                    pool_steps[0] += 1
                    pool.wait_ge(pool_step, pool_steps[0])
                    pool.tensor_tensor(acc[:, 1, :], acc[:, 1, :], tiles[:, 512:1024],
                                       ALU.add).then_inc(shift_used[1], 1)

            pool.wait_ge(half_set, 1)
            for cc in range(4):
                for s in range(4):
                    add_shift(cc, s)
                    if cc > 0:
                        split_lo(cc, s)
                if cc == 0:
                    root(ms[:, 0:NB], ms[:, 0:NB], NB)
                    for j in range(4):
                        split_lo(0, j)
            for q in range(Q_SMALL, Q_MLP):
                split_lo(q // 4, q % 4)
                slot(q - 4)
            for j in range(4):
                split_lo(U_MLP, j)
            root(ms[:, 0:NB], ms[:, 0:NB], NB)
            for j in range(4, 32):
                split_lo(U_MLP + j // 4, j % 4)
            with pool.Fori(1, STEPS) as c:
                for j in range(32):
                    split_lo(U_MLP + j // 4, j % 4, c)

        @block.vector
        def _(dve):
            own = Steps(dve, dve_step)
            dve.memset(half[:], -0.5).then_inc(half_set, 1)
            dve.wait_ge(rows_turned, 1)
            dve.tensor_copy(bias_cols[:], pa[:, 0, 0:96]).then_inc(rows_taken, 1)
            dve.wait_ge(rows_turned, 2)
            dve.tensor_copy(vec[:, 0:V_ROWS], pa[:, 1, 0:V_ROWS]).then_inc(rows_taken, 1)
            dve.wait_ge(silu_exp, 1)
            own.link(dve.tensor_scalar(csilu[:, 1, :], csilu[:, 1, :], 1.0, None, ALU.add))
            own.link(dve.reciprocal(csilu[:, 1, :], csilu[:, 1, :]))
            dve.tensor_tensor(csilu[:, 0, :], csilu[:, 1, :], vec[:, V_C:V_C + KT], ALU.mult).then_inc(silu_ready, 1)
            dve.wait_ge(silu_ready, 1)

            def take_mod(n):
                col = 2 * KT + 4 * n
                dve.wait_ge(mod_summed, 4 + n + 1)
                dve.tensor_tensor(mod[:, col:col + 4], pa[:, 3, 0:4], bias_cols[:, col:col + 4],
                                  ALU.add).then_inc(mod_taken, 1)

            def take_first_mods(cc):
                dve.wait_ge(mod_summed, cc + 1)
                for sec in range(2):
                    col = KT * (1 - sec) + 4 * cc
                    dve.tensor_tensor(mod[:, col:col + 4], pa[:, 3, 4 * sec:4 * sec + 4], bias_cols[:, col:col + 4],
                                      ALU.add).then_inc(mod_taken, 1)

            def scale_piece(cc, s):
                n = 4 * cc + s
                src = first[2 * (n % 2)]
                dve.wait_ge(first_landed[2 * (n % 2)], 16 * (n // 2 + 1))
                for i in range(4):
                    dst, c_col = acc[:, 0, :], csilu[:, 0, 4 * s + i:4 * s + i + 1]
                    if s == 0 and i == 0:
                        last = dve.tensor_scalar(dst, src[:, 0:512], c_col, None, ALU.mult)
                    else:
                        if i == 0:
                            dve.wait_ge(scale_used, n)
                        else:
                            own.wait()
                        last = dve.scalar_tensor_tensor(dst, src[:, 512 * i:512 * i + 512], c_col, dst, ALU.mult,
                                                        ALU.add)
                    if i < 3:
                        own.step(last)
                    else:
                        last.then_inc(scale_used, 1)

            def shift_piece(cc, s):
                n = 4 * cc + s
                tiles = first[1 + 2 * (n % 2)]
                dve.wait_ge(first_landed[1 + 2 * (n % 2)], 16 * (n // 2 + 1))
                c_col = csilu[:, 0, 4 * s + 2:4 * s + 3]
                if s == 0:
                    own.link(dve.tensor_scalar(shift_acc[:], tiles[:, 1024:1536], c_col, None, ALU.mult))
                else:
                    dve.wait_ge(shift_used[0], n)
                    own.link(dve.scalar_tensor_tensor(shift_acc[:], tiles[:, 1024:1536], c_col, shift_acc[:],
                                                      ALU.mult, ALU.add))
                dve.scalar_tensor_tensor(shift_acc[:], tiles[:, 1536:2048], csilu[:, 0, 4 * s + 3:4 * s + 4],
                                         shift_acc[:], ALU.mult, ALU.add).then_inc(shift_used[0], 1)

            def spread(stat, diag, ready_count):
                dve.wait_ge(rstd_ready, ready_count)
                for tb in range(NB):
                    dve.tensor_scalar(diag[:, tb, :], ident, stat[:, tb:tb + 1], None, ALU.mult).then_inc(diag_ready, 1)

            def fold(kt0, which, scale_col, norm_row, count):
                own.link(dve.scalar_tensor_tensor(gain[:, which, kt0:kt0 + count],
                                                  mod[:, scale_col + kt0:scale_col + kt0 + count], 1.0,
                                                  vec[:, norm_row + kt0:norm_row + kt0 + count], ALU.add, ALU.mult))

            def modulate(kt, which, src, rstd, tmp, shift_col, ready, hi_sem, done, go):
                if go == 0:
                    need(dve, done, kt - 1)
                    dve.scalar_tensor_tensor(tmp[:, kt % 2, :], src[:, kt, :], gain[:, which, kt:kt + 1], rstd,
                                             ALU.mult, ALU.mult).then_inc(ready, 1)
                else:
                    dve.wait_ge(hi_sem, kt + 1)
                    dve.scalar_tensor_tensor(h[:, kt, LO, :], tmp[:, kt % 2, :], mod[:, shift_col + kt:shift_col + kt + 1],
                                             h[:, kt, HI, :].bitcast(F32), ALU.add, ALU.subtract).then_inc(done, 1)

            for cc in range(4):
                for s in range(4):
                    scale_piece(cc, s)
                    shift_piece(cc, s)
                if cc == 0:
                    dve.wait_ge(x_squared, NB)
                    dve.tensor_scalar(ms[:, 0:NB], ms[:, 0:NB], 1.0 / D, EPS, ALU.mult, ALU.add).then_inc(ms_ready, 1)
                take_first_mods(cc)
                dve.wait_ge(mod_taken, 2 * cc + 2)
                fold(4 * cc, 0, KT, V_N1, 4)
                if cc == 0:
                    spread(ms, diag1, 1)
                    dve.wait_ge(rstd_spread, 1)
                    own.link(dve.tensor_copy(rstd1[:], pa[:, 2, :]))
                    dve.wait_ge(x_taken, 16)
                for m in range(5):
                    kt = 4 * cc + m
                    if m < 4:
                        modulate(kt, 0, resid, rstd1[:], tmp1, 0, t_ready, h_hi, h_ready, 0)
                    if m > 0:
                        modulate(kt - 1, 0, resid, rstd1[:], tmp1, 0, t_ready, h_hi, h_ready, 1)

            def bank_ready(u_last, ni, b):
                if b < 3:
                    dve.wait_ge(proj_done, 3 * ni + b + 1)
                else:
                    dve.wait_ge(chunk_used, 4 * u_last + 4)

            def mean_square(src, n, width):
                places = L // width
                for i in range(n):
                    if i % places == 0:
                        own.wait()
                    at_ = width * (i % places)
                    own.step(dve.tensor_tensor_reduce(junk[:, at_:at_ + width], src(i), src(i), 1.0, 0.0, ALU.mult, ALU.add,
                                                      ms[:, i:i + 1]))
                own.wait()
                dve.tensor_scalar(ms[:, 0:n], ms[:, 0:n], 1.0 / width, EPS, ALU.mult, ALU.add).then_inc(ms_ready, 1)

            def take_small():
                for tb in range(NB):
                    dve.wait_ge(chunk_used, 4 * U_SMALL + 4)
                    own.step(dve.tensor_copy(ik_nat[:, tb, :], pj[:, tb, 0:IDX_DIM]))
                    dve.tensor_scalar(w_idx[:, tb, :], pj[:, tb, IDX_DIM:SMALL], (IDX_HEADS * IDX_DIM) ** -0.5, None,
                                      ALU.mult).then_inc(proj_free, 1)
                own.wait()
                dve.wait_ge(k_ready, 8)
                mean_square(lambda tb: ik_nat[:, tb, :], NB, IDX_DIM)

            def scale_small():
                dve.wait_ge(rstd_ready, 3)
                for tb in range(NB):
                    for twice in range(2):
                        dve.tensor_scalar(ik2[:, tb, twice, :], ik_nat[:, tb, :], ms[:, tb:tb + 1], None,
                                          ALU.mult).then_inc(ik_ready, 1)

            def take_kv():
                dve.wait_ge(xT_stored, 16)
                for tb in range(NB):
                    bank_ready(U_SMALL - 1, 0, tb)
                    own.step(dve.tensor_copy(k_nat[:, tb, :], pj[:, tb, 0:KV * P]))
                    dve.tensor_copy(v_nat[:, tb, :], pj[:, tb, KV * P:]).then_inc(proj_free, 1)
                own.wait()
                mean_square(lambda i: k_nat[:, i // 2, P * (i % 2):P * (i % 2) + P], 8, P)

            def scale_k():
                dve.wait_ge(rstd_ready, 2)
                for i in range(8):
                    k_i = k_nat[:, i // 2, P * (i % 2):P * (i % 2) + P]
                    dve.tensor_scalar(k_i, k_i, ms[:, i:i + 1], None, ALU.mult).then_inc(k_ready, 1)

            def take_kT():
                for g in range(KV):
                    dve.wait_ge(k_turned, g + 1)
                    dve.tensor_scalar(kT[:, g, :], pa[:, 1 + g, :], vec[:, V_KG:V_KG + 1], None,
                                      ALU.mult).then_inc(kT_ready, 1)

            def take_ikT():
                dve.wait_ge(ik_turned, 1)
                dve.tensor_scalar(ikT[:], pa[:, 0, :], vec[:, V_IG:V_IG + 1], None, ALU.mult).then_inc(ikT_ready, 1)

            def index_item(n):
                i, hh = ITEMS[n]
                dst = score[:, SCORE_AT[i]:SCORE_AT[i] + span(i)]
                src, w_col = stage[:, n % 2, 0:span(i)], w_idx[:, i, hh:hh + 1]
                dve.wait_ge(idx_taken, n + 1)
                if hh == 0:
                    dve.tensor_scalar(dst, src, w_col, None, ALU.mult).then_inc(idx_added, 1)
                else:
                    dve.wait_ge(idx_added, n)
                    dve.scalar_tensor_tensor(dst, src, w_col, dst, ALU.mult, ALU.add).then_inc(idx_added, 1)

            def topk_round(n):
                i, k = 1 + n // (TOPK // 8), n % (TOPK // 8)
                s_i = score[:, SCORE_AT[i]:SCORE_AT[i] + span(i)]
                if k == 0:
                    dve.wait_ge(idx_added, 24 + 8 * i)
                    own.link(dve.tensor_tensor(s_i[:, span(i) - P:], s_i[:, span(i) - P:], neg, ALU.add))
                own.link(dve.max(m8[:], s_i))
                own.link(dve.match_replace(s_i, m8[:], s_i, TAKEN))
                if k == TOPK // 8 - 1:
                    own.link(dve.tensor_scalar(masks[:, MASK_AT[i]:MASK_AT[i] + span(i)], s_i, 0.5 * (TAKEN + DROP),
                                               DROP, ALU.is_gt, ALU.mult))

            def square_q(g):
                dve.wait_ge(proj_free, 8 + 16 * g + 4)
                mean_square(lambda i: nat[:, i // 4, P * (i % 4):P * (i % 4) + P], 16, P)

            def scale_q(g, blocks):
                dve.wait_ge(rstd_ready, 4 + g)
                for tb in blocks:
                    n3 = nat[:, tb, :].rearrange("p (h d) -> p h d", h=4)
                    dve.tensor_tensor(n3, n3, ms[:, 4 * tb:4 * tb + 4].unsqueeze(2).to_broadcast([P, 4, P]),
                                      ALU.mult).then_inc(q_ready, 1)

            def take_qT(g):
                for j in range(PER_KV):
                    dve.wait_ge(q_turned, 4 * g + j + 1)
                    dve.tensor_scalar(qT[:, j, :], pa[:, j, :], vec[:, V_QG:V_QG + 1], float(P) ** -0.5, ALU.mult,
                                      ALU.mult).then_inc(qT_ready, 1)

            def take_rotated(g, gr):
                dec = C_QDEC if gr == GR_RQ else C_KDEC
                for tb in range(NB):
                    use = 8 * g + 4 * (gr - GR_RQ) + tb
                    x3 = pj[:, tb, :].rearrange("p (h d two) -> p h d two", h=4, two=2)
                    s3 = stage[:, use % 2, :].rearrange("p (h d two) -> p h d two", h=4, two=2)
                    cos = con[:, C_COS + 64 * tb:C_COS + 64 * tb + 64].unsqueeze(1).to_broadcast([P, 4, 64])
                    sin = con[:, C_SIN + 64 * tb:C_SIN + 64 * tb + 64].unsqueeze(1).to_broadcast([P, 4, 64])
                    r0 = rot[:, 0, :].rearrange("p (h d) -> p h d", h=4)
                    r1 = rot[:, 1, :].rearrange("p (h d) -> p h d", h=4)
                    bank_ready(U_LOOP + PER_G * g + 2 * gr + 1, 1 + gr + 5 * g, tb)
                    need(dve, ret_stored[use % 2], 16 * (use // 2))
                    own.step(dve.tensor_tensor(s3[:, :, :, 0], x3[:, :, :, 0], cos, ALU.mult))
                    own.step(dve.tensor_tensor(s3[:, :, :, 1], x3[:, :, :, 0], sin, ALU.mult))
                    own.step(dve.tensor_tensor(r0, x3[:, :, :, 1], sin, ALU.mult))
                    dve.tensor_tensor(r1, x3[:, :, :, 1], cos, ALU.mult).then_inc(proj_free, 1)
                    own.wait()
                    own.step(dve.tensor_tensor(s3[:, :, :, 0], s3[:, :, :, 0], r0, ALU.subtract))
                    dve.wait_ge(proj_free, 8 + 16 * g + 4 * gr + tb + 1)
                    own.link(dve.tensor_tensor(s3[:, :, :, 1], s3[:, :, :, 1], r1, ALU.add))
                    sh = stage[:, use % 2, :].rearrange("p (h d) -> p h d", h=4)
                    d_ = con[:, dec + 8 * tb + 4 * g:dec + 8 * tb + 4 * g + 4].unsqueeze(2).to_broadcast([P, 4, P])
                    dve.tensor_tensor(sh, sh, d_, ALU.mult).then_inc(stage_ready, 1)

            def masked_logits(hd):
                for i in (0, 2, 1, 3):
                    bank, col = LOGIT_AT[i]
                    dve.wait_ge(logits_done, 3 * hd + bank + 1)
                    own.step(dve.tensor_tensor_reduce(
                        prob[:, MASK_AT[i]:MASK_AT[i] + span(i)], pa[:, bank, col:col + span(i)],
                        masks[:, MASK_AT[i]:MASK_AT[i] + span(i)], 1.0, -3.0e38, ALU.add, ALU.max, mx[:, i:i + 1]))
                own.wait()
                dve.tensor_scalar(mx[:, 4:8], mx[:, 0:4], -1.0, None, ALU.mult).then_inc(logits_ready, 1)

            def normalise(hd):
                dve.wait_ge(exp_done, 4 * hd + 4)
                own.link(dve.reciprocal(sums[:, 4:8], sums[:, 0:4]))
                for i in range(NB):
                    p_i = prob[:, MASK_AT[i]:MASK_AT[i] + span(i)]
                    dve.tensor_scalar(p_i, p_i, sums[:, 4 + i:5 + i], None, ALU.mult).then_inc(p_ready, 1)

            def take_y(hd):
                dve.wait_ge(pv_done, hd + 1)
                dve.tensor_scalar(y_raw[:, hd, :], pa[:, 3, :], vec[:, V_DB + hd:V_DB + hd + 1], None,
                                  ALU.mult).then_inc(y_ready, 1)

            def later_piece(n, k):
                piece = 8 * n + k
                dve.wait_ge(ada_landed[piece % 2], 16 * (piece // 2 + 1))
                src, c_col = ada[:, piece % 2, 0:512], csilu[:, 0, 2 * k:2 * k + 1]
                if k == 0:
                    dve.tensor_scalar(acc[:, 0, :], src, c_col, None, ALU.mult).then_inc(ada_used[0], 1)
                else:
                    dve.wait_ge(ada_used[0], piece)
                    dve.scalar_tensor_tensor(acc[:, 0, :], src, c_col, acc[:, 0, :], ALU.mult,
                                             ALU.add).then_inc(ada_used[0], 1)

            def pieces_first(q):
                return q < Q_TOPK or (q - Q_LOOP) % PER_GQ in (7, 9, 10, 11)

            rounds_done = 0
            for q in range(Q_WO):
                for n in ada_sum_at(q - 1):
                    take_mod(n)
                if q == Q_SMALL - 1:
                    take_kv()
                if q == Q_SMALL + 1:
                    scale_k()
                if q == Q_SMALL + 2:
                    take_kT()
                if q == Q_IQ - 1:
                    take_small()
                if q == Q_IQ + 1:
                    scale_small()
                if q == Q_IQ + 2:
                    take_ikT()
                if pieces_first(q):
                    for n, k in ada_pieces_at(q):
                        later_piece(n, k)
                for n in items_at(q):
                    index_item(n)
                if q >= Q_LOOP:
                    g, r = divmod(q - Q_LOOP, PER_GQ)
                    if r == 7:
                        square_q(g)
                    if r in (9, 10):
                        scale_q(g, (0, 1) if r == 9 else (2, 3))
                    if r == Q_TURN_AT:
                        take_qT(g)
                    if r == 18:
                        own.step(dve.tensor_copy(v_cur[:], v_nat[:, :, P * g:P * g + P]))
                        if g == 0:
                            own.step(dve.tensor_copy(masks[:, 0:P], neg))
                        own.wait()
                    if r in (23, 31):
                        take_rotated(g, GR_RQ if r == 23 else GR_RK)
                    if r in OUTS_AT:
                        take_y(4 * g + OUTS_AT.index(r))
                    if r in LOGITS_AT:
                        masked_logits(4 * g + LOGITS_AT.index(r))
                    if r - 1 in LOGITS_AT:
                        normalise(4 * g + LOGITS_AT.index(r - 1))
                if Q_TOPK <= q < Q_TOPK + len(ROUNDS):
                    for _ in range(ROUNDS[q - Q_TOPK]):
                        topk_round(rounds_done)
                        rounds_done += 1
                if not pieces_first(q):
                    for n, k in ada_pieces_at(q):
                        later_piece(n, k)
            dve.wait_ge(mod_taken, 8 + ADA_ACCS)
            fold(0, 1, 4 * KT, V_N2, KT)

            for t in range(HEADS):
                dve.wait_ge(yd_hi, t + 1)
                dve.tensor_tensor(h[:, 8 + t, LO, :], y_raw[:, t, :], h[:, 8 + t, HI, :].bitcast(F32),
                                  ALU.subtract).then_inc(yd_ready, 1)

            def add_out(v, last):
                t = v % KT
                dve.wait_ge(chunk_used, 4 * U_WO + v + 1)
                if v == 0:
                    dve.wait_ge(resid_landed, 16)
                if last:
                    dve.wait_ge(added, v - KT + 1)
                dve.scalar_tensor_tensor(resid[:, t, :], pj[:, t % 4, :], mod[:, 2 * KT + t:2 * KT + t + 1],
                                         resid[:, t, :], ALU.mult, ALU.add).then_inc(added, 1)
                if last:
                    dve.wait_ge(added, v + 1)
                    if t == 0:
                        own.link(dve.tensor_tensor(ss[:], resid[:, t, :], resid[:, t, :], ALU.mult))
                    else:
                        own.link(dve.tensor_tensor(sq[:, 0, :], resid[:, t, :], resid[:, t, :], ALU.mult))
                        if t < KT - 1:
                            own.link(dve.tensor_tensor(ss[:], ss[:], sq[:, 0, :], ALU.add))
                        else:
                            dve.tensor_tensor(ss[:], ss[:], sq[:, 0, :], ALU.add).then_inc(ss_ready, 1)

            def ret_state(k):
                dve.wait_ge(state_done, k + 1)
                dve.tensor_copy(state[:].rearrange("p a b -> p (a b)"), pa[:, 2, 0:3 * P]).then_inc(state_ready, 1)

            def ret_inner(k):
                dve.wait_ge(inner_done, k + 1)
                dve.tensor_tensor(innerT[:].rearrange("p (n c) -> p n c", n=NB),
                                  pa[:, 3, :].rearrange("p (n c) -> p n c", n=NB),
                                  causal.unsqueeze(1).to_broadcast([P, NB, P]), ALU.mult).then_inc(inner_ready, 1)

            def ret_norm(k):
                dve.wait_ge(o_done, k + 1)
                for n in range(NB):
                    own.step(dve.bn_stats(bn6[:, n, :], pa[:, 3, P * n:P * n + P]))
                own.wait()
                for n in range(NB):
                    own.step(dve.bn_aggr(bn2[:, n, :], bn6[:, n, :]))
                own.wait()
                dve.tensor_scalar(ms[:, 0:NB], bn2[:, :, 1], EPS, None, ALU.add).then_inc(ms_ready, 1)
                dve.wait_ge(rstd_ready, 6 + k)
                for n in range(NB):
                    own.step(dve.tensor_scalar(z[:, n, :], pa[:, 3, P * n:P * n + P], bn2[:, n, 0:1], ms[:, n:n + 1],
                                               ALU.subtract, ALU.mult))
                own.wait()
                dve.tensor_tensor(z[:], z[:], gate_e[k % 2][:].rearrange("p (b d) -> p b d", b=NB),
                                  ALU.mult).then_inc(z_ready, 1)

            def silu_gate(k):
                e = gate_e[k % 2][:]
                dve.wait_ge(rg_exp, k + 1)
                own.link(dve.tensor_scalar(e, e, 1.0, None, ALU.add))
                own.link(dve.reciprocal(e, e))
                own.link(dve.tensor_tensor(e, e, ret[:, k % 3, 0].rearrange("p b d -> p (b d)"), ALU.mult))

            def ret_low(k):
                dve.wait_ge(yr_hi, k + 1)
                dve.scalar_tensor_tensor(h[:, k, LO, :], pa[:, 0, :], vec[:, V_RB + k:V_RB + k + 1],
                                         h[:, k, HI, :].bitcast(F32), ALU.mult, ALU.subtract).then_inc(yr_ready, 1)

            silu_gate(0)
            for r in range(16):
                add_out(r, False)
                k, odd = divmod(r, 2)
                if not odd:
                    if k > 0:
                        ret_norm(k - 1)
                    ret_state(k)
                else:
                    ret_inner(k)
                    if k > 0:
                        ret_low(k - 1)
                    if k < HEADS - 1:
                        silu_gate(k + 1)
            ret_norm(7)
            ret_low(7)
            for r in range(16, 32):
                add_out(r, True)

            dve.wait_ge(ss_summed, 1)
            dve.tensor_scalar(ms[:, 0:NB], pa[:, 2, 0:NB], 1.0 / D, EPS, ALU.mult, ALU.add).then_inc(ms_ready, 1)
            spread(ms, diag2, 14)
            dve.wait_ge(rstd_spread, 2)
            for kt in range(KT + 1):
                if kt < KT:
                    modulate(kt, 1, resid, pa[:, 2, :], relu, 3 * KT, t2_ready, h2_hi, h2_ready, 0)
                if kt > 0:
                    modulate(kt - 1, 1, resid, pa[:, 2, :], relu, 3 * KT, t2_ready, h2_hi, h2_ready, 1)

            def mlp_step(c, last):
                for n in range(9):
                    if n < 8:
                        dve.wait_ge(relu_done, 8 * c + n + 1)
                        if n > 1:
                            dve.wait_ge(mid_ready, 8 * c + n - 1)
                        dve.tensor_tensor(sq[:, n % 2, :], relu[:, n % 2, :], relu[:, n % 2, :],
                                          ALU.mult).then_inc(sq_ready, 1)
                    if n > 0:
                        dve.wait_ge(mid_hi, 8 * c + n)
                        dve.tensor_tensor(mid[:, n - 1, LO, :], sq[:, (n - 1) % 2, :],
                                          mid[:, n - 1, HI, :].bitcast(F32), ALU.subtract).then_inc(mid_ready, 1)
                dve.wait_ge(mid_ready, 8 * c + 8)
                dve.wait_ge(added, 32 + 16 * c)
                for t in range(KT):
                    v, j = divmod(t, 4)
                    dve.wait_ge(chunk_used, 4 * (U_MLP + 4 + v) + j + 1 + 32 * c)
                    dve.scalar_tensor_tensor(resid[:, t, :], (pa if v % 2 else pj)[:, j, :],
                                             mod[:, 5 * KT + t:5 * KT + t + 1], resid[:, t, :], ALU.mult,
                                             ALU.add).then_inc(added, 1)

            with dve.Fori(0, STEPS) as c:
                mlp_step(c, False)

        @block.tensor
        def _(pe):
            def product(dst, lhs, rhs, start, stop):
                for n, (a, b) in enumerate(PASSES):
                    last = pe.matmul(dst, lhs[a], rhs[b], start=start and n == 0, stop=stop and n == 2)
                return last

            def turn(dst, src):
                return pe.transpose(dst, src, ident)

            def tokens_chunk(u, j, k0, is_first, is_last, freed, count):
                pe.wait_ge(lo_done, 4 * u + j + 1)
                for tb in range(NB):
                    if is_first and j == 0 and freed is not None:
                        pe.wait_ge(freed, count + tb + 1)
                    for kk in range(2):
                        kt = k0 + 2 * j + kk
                        cols = slice(512 * kk, 512 * kk + 512)
                        last = product(pj[:, tb, :], [h[:, kt, s, P * tb:P * tb + P] for s in (HI, LO)],
                                       [w_hi[:, j, cols], w_lo[:, j, cols]],
                                       is_first and j == 0 and kk == 0, is_last and j == 3 and kk == 1)
                    if is_last and j == 3 and tb < 3:
                        last.then_inc(proj_done, 1)
                last.then_inc(chunk_used, 1)

            def features_chunk(q, src, k0, bank, start, stop, ready=None, count=0, trip=0):
                j = q % 4
                pe.wait_ge(lo_done, q + 1 + 32 * trip)
                for kk in range(8):
                    if ready is not None:
                        pe.wait_ge(ready, count + kk + 1)
                    last = product(bank, [w[:, j, P * kk:P * kk + P] for w in (w_hi, w_lo)],
                                   [src[:, k0 + kk, s, :] for s in (HI, LO)], start and kk == 0, stop and kk == 7)
                last.then_inc(chunk_used, 1)

            pe.wait_ge(const_landed, 16)
            pe.wait_ge(rows_landed, 32)
            pe.transpose(pa[:, 0, 0:96], rows[0:96, 0, :], con[0:96, C_ID:C_ID + 96]).then_inc(rows_turned, 1)
            pe.transpose(pa[:, 1, 0:V_ROWS], rows[0:V_ROWS, 1, :],
                         con[0:V_ROWS, C_ID:C_ID + V_ROWS]).then_inc(rows_turned, 1)
            for tb in range(NB):
                pe.wait_ge(x_landed[tb % 2], 16 * (tb // 2 + 1))
                for q in range(4):
                    need(pe, x_taken, 4 * tb + q - 3)
                    for m in range(4):
                        last = turn(pj[:, q, P * m:P * m + P], x_nat[:, tb % 2, P * (4 * q + m):P * (4 * q + m + 1)])
                    last.then_inc(x_turned, 1)
            def spread(diag, count):
                pe.wait_ge(diag_ready, count)
                for tb in range(NB):
                    last = pe.matmul(pa[:, 2, P * tb:P * tb + P], ones, diag[:, tb, :], start=True, stop=True)
                last.then_inc(rstd_spread, 1)

            def sum_mod():
                for m in range(4):
                    for e in range(2):
                        last = pe.matmul(pa[:, 3, m:m + 1], acc[:, e, P * m:P * m + P], ones[:, 0:1],
                                         start=e == 0, stop=e == 1)
                last.then_inc(mod_summed, 1)

            def sum_first(cc):
                need(pe, mod_taken, 2 * cc)
                for sec, sums_ in enumerate((((acc[:, 0], scale_used),),
                                             ((shift_acc[:], shift_used[0]), (acc[:, 1], shift_used[1])))):
                    for _, used in sums_:
                        pe.wait_ge(used, 4 * cc + 4)
                    for m in range(4):
                        for e, (part, _) in enumerate(sums_):
                            last = pe.matmul(pa[:, 3, 4 * sec + m:4 * sec + m + 1], part[:, P * m:P * m + P],
                                             ones[:, 0:1], start=e == 0, stop=e == len(sums_) - 1)
                last.then_inc(mod_summed, 1)

            def early_chunk(kt):
                j = kt % 4
                pe.wait_ge(h_ready, kt + 1)
                pe.wait_ge(lo_done, kt + 1)
                for tb in range(NB):
                    last = product(pj[:, tb, :], [h[:, kt, s, P * tb:P * tb + P] for s in (HI, LO)],
                                   [w_hi[:, j, 0:512], w_lo[:, j, 0:512]], kt == 0, kt == KT - 1)
                    if kt == KT - 1 and tb < 3:
                        last.then_inc(proj_done, 1)
                for t in range(IQ_EARLY):
                    cols = slice(512 + P * t, 512 + P * t + P)
                    last = product(pa[:, t, :], [w_hi[:, j, cols], w_lo[:, j, cols]],
                                   [h[:, kt, s, :] for s in (HI, LO)], kt == 0, kt == KT - 1)
                last.then_inc(chunk_used, 1)

            for cc in range(5):
                if cc > 0:
                    for s in range(4):
                        early_chunk(4 * (cc - 1) + s)
                if cc < 4:
                    sum_first(cc)
                if cc == 0:
                    spread(diag1, NB)
                    pe.wait_ge(x_taken, 16)
            for j in range(4):
                pe.wait_ge(lo_done, Q_SMALL + j + 1)
                if j == 0:
                    pe.wait_ge(mod_taken, 8)
                for kk in range(4):
                    cols = slice(LATE * kk, LATE * kk + P)
                    product(pa[:, 3, :], [w_hi[:, j, cols], w_lo[:, j, cols]],
                            [h[:, 4 * j + kk, s, :] for s in (HI, LO)], j == 0 and kk == 0, j == 3 and kk == 3)
                for tb in range(NB):
                    if j == 0:
                        pe.wait_ge(proj_free, tb + 1)
                    for kk in range(4):
                        cols = slice(LATE * kk + P, LATE * kk + LATE)
                        last = product(pj[:, tb, 0:SMALL],
                                       [h[:, 4 * j + kk, s, P * tb:P * tb + P] for s in (HI, LO)],
                                       [w_hi[:, j, cols], w_lo[:, j, cols]],
                                       j == 0 and kk == 0, j == 3 and kk == 3)
                last.then_inc(chunk_used, 1)
                if j == 2:
                    pe.wait_ge(k_ready, 8)
                    pe.wait_ge(iq_ready, IQ_EARLY)
                    for g in range(KV):
                        for tb in range(NB):
                            last = turn(pa[:, 1 + g, P * tb:P * tb + P], k_nat[:, tb, P * g:P * g + P])
                        last.then_inc(k_turned, 1)

            done = {"items": 0, "mods": 8, "heads": 0, "turns": 0}

            def bank3_free():
                pe.wait_ge(iq_ready, 4)
                need(pe, idx_taken, done["items"])
                pe.wait_ge(mod_taken, done["mods"])
                need(pe, y_ready, done["heads"])
                need(pe, qT_ready, done["turns"])

            def later_mod(n):
                for used in ada_used:
                    pe.wait_ge(used, 8 * n + 8)
                bank3_free()
                sum_mod()
                done["mods"] += 1

            def index_item(n):
                i, hh = ITEMS[n]
                rows = slice(IDX_DIM * (hh % 2), IDX_DIM * (hh % 2) + IDX_DIM)
                if n == 0:
                    pe.wait_ge(ikT_ready, 1)
                    pe.wait_ge(kT_ready, KV)
                if n % 4 == 3:
                    pe.wait_ge(mod_taken, done["mods"])
                need(pe, idx_taken, n - 3)
                pe.wait_ge(iq_ready, 4 if n < 24 else 8)
                pe.matmul(pa[:, n % 4, 0:span(i)], iqT[rows, hh // 2, P * i:P * i + P], ikT[rows, 0:span(i)],
                          start=True, stop=True).then_inc(idx_done, 1)
                done["items"] += 1

            for q in range(Q_IQ, Q_LOOP):
                hf, j = divmod(q - Q_IQ, 4)
                if hf == 0:
                    pe.wait_ge(proj_free, 4 + j + 1)
                features_chunk(q, h, 8 * hf, pj[:, j, :], hf == 0, hf == 1)
                if q == Q_IQ + 2:
                    pe.wait_ge(ik_ready, 8)
                    for tb in range(NB):
                        last = turn(pa[:, 0, P * tb:P * tb + P], ik2[:, tb].rearrange("p a b -> p (a b)"))
                    last.then_inc(ik_turned, 1)
                for n in items_at(q):
                    index_item(n)
                for n in ada_sum_at(q):
                    later_mod(n)

            def q_transposes(g):
                pe.wait_ge(q_ready, 4 * g + 4)
                bank3_free()
                for j in range(PER_KV):
                    for tb in range(NB):
                        last = turn(pa[:, j, P * tb:P * tb + P], nat[:, tb, P * j:P * j + P])
                    last.then_inc(q_turned, 1)
                done["turns"] += 4

            def head_logits(hd):
                g, j = divmod(hd, PER_KV)
                pe.wait_ge(qT_ready, 4 * g + 4)
                need(pe, pT_ready, 4 * hd)
                for i in (0, 2, 1, 3):
                    bank, col = LOGIT_AT[i]
                    last = pe.matmul(pa[:, bank, col:col + span(i)], qT[:, j, P * i:P * i + P], kT[:, g, 0:span(i)],
                                     start=True, stop=True)
                    if i != 0:
                        last.then_inc(logits_done, 1)

            def p_transposes(hd):
                pe.wait_ge(p_ready, 4 * hd + 4)
                need(pe, logits_ready, hd + 1)
                for kb in TURN_ORDER:
                    bank, col = TURN_AT[kb]
                    for i in range(kb, NB):
                        at_ = MASK_AT[i] + P * kb
                        last = turn(pa[:, bank, col + P * (i - kb):col + P * (i - kb + 1)], prob[:, at_:at_ + P])
                    if kb != 1:
                        last.then_inc(p_turned, 1)

            def head_out(hd):
                bank3_free()
                for kb in range(NB):
                    pe.wait_ge(pT_ready, 4 * hd + (1, 2, 4, 4)[kb])
                    width = L - P * kb
                    last = pe.matmul(pa[:, 3, P * kb:], v_cur[:, kb, :], pT[:, PT_AT[kb]:PT_AT[kb] + width],
                                     start=kb == 0, stop=kb == NB - 1, skip_group_check=True)
                last.then_inc(pv_done, 1)
                done["heads"] += 1

            for q in range(Q_LOOP, Q_WO):
                g, r = divmod(q - Q_LOOP, PER_GQ)
                group, hf = r // 8, r % 8 // 4
                if group == 0:
                    freed, count = (v_taken, 4 * g - 4) if g else (iq_ready, 4)
                else:
                    freed, count = proj_free, 8 + 16 * g + 4 * (group - 1)
                tokens_chunk(q // 4, q % 4, 8 * hf, hf == 0, hf == 1, freed, count)
                for n in items_at(q):
                    index_item(n)
                if r == Q_TURN_AT:
                    q_transposes(g)
                if r in TURNS_AT:
                    p_transposes(4 * g + TURNS_AT.index(r))
                if r in OUTS_AT:
                    head_out(4 * g + OUTS_AT.index(r))
                if r in LOGITS_AT:
                    head_logits(4 * g + LOGITS_AT.index(r))
                for n in ada_sum_at(q):
                    later_mod(n)

            def ret_turn(k):
                pe.wait_ge(ret_landed[k % 3], 64 * (k // 3 + 1))
                bank3_free()
                need(pe, yr_ready, k - 1)
                need(pe, state_ready, k)
                for b, kind in enumerate((1, 2)):
                    for n in range(NB):
                        last = turn(pa[:, b, P * n:P * n + P], ret[:, k % 3, kind, n, :])
                    last.then_inc(qk_turned, 1)
                for n in range(1, NB):
                    for e in range(n):
                        last = pe.matmul(pa[:, 2, P * (n - 1):P * n], ret[:, k % 3, 2, e, :], ret[:, k % 3, 3, e, :],
                                         start=e == 0, stop=e == n - 1)
                last.then_inc(state_done, 1)

            def ret_inner(k):
                pe.wait_ge(qkT_ready, 2 * k + 2)
                need(pe, z_ready, k)
                for n in range(NB):
                    last = pe.matmul(pa[:, 3, P * n:P * n + P], qkT[:, 1, P * n:P * n + P], qkT[:, 0, P * n:P * n + P],
                                     start=True, stop=True)
                last.then_inc(inner_done, 1)

            def ret_out(k):
                pe.wait_ge(inner_ready, k + 1)
                pe.wait_ge(state_ready, k + 1)
                for n in range(NB):
                    last = pe.matmul(pa[:, 3, P * n:P * n + P], innerT[:, P * n:P * n + P], ret[:, k % 3, 3, n, :],
                                     start=True, stop=n == 0)
                    if n > 0:
                        last = pe.matmul(pa[:, 3, P * n:P * n + P], qkT[:, 0, P * n:P * n + P], state[:, n - 1, :],
                                         start=False, stop=True)
                last.then_inc(o_done, 1)

            def ret_back(k):
                pe.wait_ge(z_ready, k + 1)
                pe.wait_ge(qkT_ready, 2 * min(k + 2, HEADS))
                for n in range(NB):
                    last = turn(pa[:, 0, P * n:P * n + P], z[:, n, :])
                last.then_inc(z_turned, 1)

            for r in range(32):
                half_, t = divmod(r, KT)
                if r >= 4:
                    pe.wait_ge(added, r - 3)
                if r < 4:
                    pe.wait_ge(v_taken, 4 + r + 1)
                features_chunk(4 * U_WO + r, h, 8 * (1 - half_), pj[:, t % 4, :], True, True,
                               (yd_ready if half_ == 0 else yr_ready) if t == 0 else None)
                if r < 16:
                    k, odd = divmod(r, 2)
                    if not odd:
                        if k > 0:
                            ret_out(k - 1)
                        need(pe, yr_ready, k - 1)
                        ret_turn(k)
                    else:
                        ret_inner(k)
                        if k > 0:
                            ret_back(k - 1)
                if r == 15:
                    ret_out(7)
                    ret_back(7)

            pe.wait_ge(ss_ready, 1)
            for tb in range(NB):
                last = pe.matmul(pa[:, 2, tb:tb + 1], ss[:, P * tb:P * tb + P], ones[:, 0:1], start=True, stop=True)
            last.then_inc(ss_summed, 1)
            spread(diag2, 2 * NB)

            def output(t):
                pe.wait_ge(added, 32 + KT * (STEPS - 1) + t + 1)
                for tb in range(NB):
                    last = turn((pa if t // 4 % 2 else pj)[:, t % 4, P * tb:P * tb + P], resid[:, t, P * tb:P * tb + P])
                last.then_inc(out_turned, 1)

            def mlp_step(c, final=False):
                for m in range(4):
                    a, hf = divmod(m, 2)
                    banks = pa if a else pj
                    for j in range(4):
                        if hf == 0:
                            pe.wait_ge(added, (24 if a == 0 else 28) + j + 1 + 16 * c)
                        features_chunk(4 * (U_MLP + m) + j, h, 8 * hf, banks[:, j, :], hf == 0, hf == 1,
                                       h2_ready if a == 0 and j == 0 else None, 8 * hf, c)
                for v in range(4):
                    banks = pa if v % 2 else pj
                    for j in range(4):
                        if v < 2:
                            pe.wait_ge(relu_done, 4 * v + j + 1 + 8 * c)
                        elif final:
                            pe.wait_ge(out_ready, 4 * (v - 2) + j + 1)
                        else:
                            pe.wait_ge(added, 32 + 4 * (v - 2) + j + 1 + 16 * c)
                        q = 4 * (U_MLP + 4 + v) + j
                        pe.wait_ge(lo_done, q + 1 + 32 * c)
                        for kk in range(8):
                            if v == 0 and j == 0:
                                pe.wait_ge(mid_ready, kk + 1 + 8 * c)
                            last = product(banks[:, j, :], [w[:, j, P * kk:P * kk + P] for w in (w_hi, w_lo)],
                                           [mid[:, kk, s, :] for s in (HI, LO)], kk == 0, kk == 7)
                        last.then_inc(chunk_used, 1)
                        if final and 4 * v + j > 0:
                            output(4 * v + j - 1)
                if final:
                    output(KT - 1)

            with pe.Fori(0, STEPS - 1) as c:
                mlp_step(c)
            mlp_step(STEPS - 1, final=True)


def _constants():
    c = np.zeros((P, C_END), np.float32)
    i = np.arange(P)
    c[:, C_ID:C_ID + P] = np.eye(P)
    c[:, C_CAUSAL:C_CAUSAL + P] = i[None, :] >= i[:, None]
    c[:, C_NEG:C_NEG + P] = np.where(i[None, :] <= i[:, None], 0.0, DROP)
    c[:, C_ONES:C_ONES + P] = 1.0
    angle = (1.0 / (np.float32(10000.0) ** np.linspace(0.0, 1.0, P // 2, dtype=np.float32))).astype(np.float32)
    for b in range(NB):
        theta = ((P * b + i).astype(np.float32)[:, None] * angle[None, :]).astype(np.float64)
        c[:, C_COS + 64 * b:C_COS + 64 * b + 64] = np.cos(theta)
        c[:, C_SIN + 64 * b:C_SIN + 64 * b + 64] = np.sin(theta)
        for hd in range(HEADS):
            log_gamma = math.log(1.0 - 2.0 ** (-5.0 - hd))
            c[:, C_QDEC + 8 * b + hd] = np.exp(log_gamma * (P * b + i))
            c[:, C_KDEC + 8 * b + hd] = np.exp(-log_gamma * (P * b + i)) * P ** -0.5
    return c


def kernel(x, c, w_ada, b_ada, norm1_g, norm2_g, w_in, ret_beta, q_norm_g, k_norm_g, idx_k_norm_g, dsa_beta,
           w_out, w_mlp1, w_mlp2):
    import concourse.bacc as _bacc
    from concourse.bass_utils import run_bass_kernel_spmd as _run

    flat = lambda a: np.ascontiguousarray(a).reshape(-1)
    arrays = {
        "x_in": np.ascontiguousarray(x).reshape(L, D),
        "vecs": np.concatenate([flat(a) for a in (c, norm1_g, norm2_g, ret_beta, dsa_beta, q_norm_g, k_norm_g,
                                                  idx_k_norm_g, idx_k_norm_g)]).reshape(V_ROWS, P),
        "b_ada_in": np.ascontiguousarray(b_ada).reshape(6 * KT, P),
        "consts": _constants(),
        "w_ada_in": np.ascontiguousarray(w_ada).reshape(D, 6 * D),
        "w_in_in": np.ascontiguousarray(w_in).reshape(D, -1),
        "w_out_in": np.ascontiguousarray(w_out).reshape(D, D),
        "w_mlp1_in": np.ascontiguousarray(w_mlp1).reshape(D, FF),
        "w_mlp2_in": np.ascontiguousarray(w_mlp2).reshape(FF, D),
    }
    nc = _bacc.Bacc("TRN2", target_bir_lowering=False, num_devices=1)
    args = [nc.dram_tensor(n, a.shape, mybir.dt.from_np(a.dtype), kind="ExternalInput").ap()
            for n, a in arrays.items()]
    out = nc.dram_tensor("out", (L, D), F32, kind="ExternalOutput").ap()
    build(nc, *args, out)
    r = _run(nc, [arrays], core_ids=[0])
    return r.results[0]["out"].reshape(1, L, D)
```
